# Optimizing a Trainium2 kernel written in Bass

```python
import math
import jax, jax.numpy as jnp
from jax import lax
import numpy as np

D_MODEL = 1024
BATCH = 1
SEQ = 512
DEPTH = 1

CHUNK = 64
QBLOCK = 128
ROPE_THETA = 10000.0
EPS = 1e-6
N_ATTN_HEADS = 8
HEAD_DIM = D_MODEL // 16
D_ATTN = N_ATTN_HEADS * HEAD_DIM
N_IDX_HEADS = 8
IDX_DIM = 64
TOPK_MAX = 256
D_RNN = D_MODEL // 2
N_RNN_BLOCKS = 8
RNN_BLOCK = D_RNN // N_RNN_BLOCKS
CONV_WIDTH = 4
RG_C = 8.0
D_MIX = D_ATTN + D_RNN
IN_SPLITS = [D_ATTN, D_ATTN, D_ATTN, N_IDX_HEADS * IDX_DIM, IDX_DIM, N_IDX_HEADS, D_RNN, D_RNN]
D_IN = sum(IN_SPLITS)
IN_OFFSETS = [int(o) for o in np.cumsum(IN_SPLITS)[:-1]]
N_GROUPS = 4
EXP_PER_GROUP = 8
TOP_E = 2
D_EXPERT = D_MODEL // 4
N_MOD = 6

kernel_name = "hybrid_dsa_rglru_hmoe_block"

def rms_norm(x, g):
    xf = x.astype(jnp.float32)
    y = xf * lax.rsqrt(jnp.mean(xf * xf, axis=-1, keepdims=True) + EPS)
    return (y * g.astype(jnp.float32)).astype(x.dtype)

def rope_tables(seq_len, dim):
    pos = jnp.arange(seq_len, dtype=jnp.float32)
    inv = ROPE_THETA ** (-jnp.arange(0, dim, 2, dtype=jnp.float32) / dim)
    ang = pos[:, None] * inv[None, :]
    return jnp.cos(ang), jnp.sin(ang)

def apply_rope(x, cos, sin):
    xf = x.astype(jnp.float32)
    x1, x2 = jnp.split(xf, 2, axis=-1)
    c, s = cos[None, :, None, :], sin[None, :, None, :]
    return jnp.concatenate([x1 * c - x2 * s, x2 * c + x1 * s], axis=-1).astype(x.dtype)

def sparse_indexed_attention(q, k, v, q_idx, k_idx, w_idx):
    B, S, H, Dh = q.shape
    n_sel = min(TOPK_MAX, S // 4)
    key_pos = jnp.arange(S)
    qi_f = q_idx.astype(jnp.float32)
    ki_f = k_idx.astype(jnp.float32)
    wi_f = w_idx.astype(jnp.float32) * (N_IDX_HEADS ** -0.5)
    gather = jax.vmap(lambda t, i: t[i])

    def one_block(start):
        sl = lambda a: lax.dynamic_slice_in_dim(a, start, QBLOCK, axis=1)
        q_b, qi_b, wi_b = sl(q), sl(qi_f), sl(wi_f)
        q_pos = start + jnp.arange(QBLOCK)
        limit = (q_pos // CHUNK + 1) * CHUNK
        dots = jnp.einsum('bqhd,bsd->bqhs', qi_b, ki_f) * (IDX_DIM ** -0.5)
        score = jnp.einsum('bqh,bqhs->bqs', wi_b, jax.nn.relu(dots))
        score = jnp.where(key_pos[None, None, :] < limit[None, :, None], score, -jnp.inf)
        _, idx = lax.top_k(score, n_sel)
        valid = idx < limit[None, :, None]
        k_sel = gather(k, idx)
        v_sel = gather(v, idx)
        logits = jnp.einsum('bqhd,bqkhd->bhqk', q_b, k_sel).astype(jnp.float32) * (Dh ** -0.5)
        logits = jnp.where(valid[:, None], logits, -jnp.inf)
        p = jax.nn.softmax(logits, axis=-1).astype(v.dtype)
        return jnp.einsum('bhqk,bqkhd->bqhd', p, v_sel)

    starts = jnp.arange(S // QBLOCK) * QBLOCK
    out = lax.map(one_block, starts)
    return out.transpose(1, 0, 2, 3, 4).reshape(B, S, H * Dh)

def rglru_branch(xr, conv_w, conv_b, w_a, b_a, w_x, b_x, lam):
    B, S, R = xr.shape
    conv = lax.conv_general_dilated(
        xr, conv_w[:, None, :].astype(xr.dtype), window_strides=(1,),
        padding=[(CONV_WIDTH - 1, 0)], dimension_numbers=('NWC', 'WIO', 'NWC'),
        feature_group_count=R) + conv_b.astype(xr.dtype)
    xf = conv.astype(jnp.float32)
    xb = xf.reshape(B, S, N_RNN_BLOCKS, RNN_BLOCK)
    r = jax.nn.sigmoid(jnp.einsum('bsnc,ncd->bsnd', xb, w_a.astype(jnp.float32)).reshape(B, S, R) + b_a.astype(jnp.float32))
    i = jax.nn.sigmoid(jnp.einsum('bsnc,ncd->bsnd', xb, w_x.astype(jnp.float32)).reshape(B, S, R) + b_x.astype(jnp.float32))
    log_a = -RG_C * r * jax.nn.softplus(-lam.astype(jnp.float32))
    a = jnp.exp(log_a)
    b = jnp.sqrt(-jnp.expm1(2.0 * log_a)) * (i * xf)

    def combine(left, right):
        a_l, b_l = left
        a_r, b_r = right
        return a_l * a_r, a_r * b_l + b_r

    _, h = lax.associative_scan(combine, (a, b), axis=1)
    return h.astype(xr.dtype)

def hierarchical_moe(h, w_rg, b_rg, w_re, b_re, w_gate, w_up, w_down):
    B, S, D = h.shape
    hf = h.reshape(B * S, D)
    h32 = hf.astype(jnp.float32)
    p_groups = jax.nn.softmax(h32 @ w_rg.astype(jnp.float32) + b_rg.astype(jnp.float32), axis=-1)
    g_idx = jnp.argmax(p_groups, axis=-1)
    p_g = jnp.max(p_groups, axis=-1)
    e_logits = (h32 @ w_re.astype(jnp.float32) + b_re.astype(jnp.float32)).reshape(-1, N_GROUPS, EXP_PER_GROUP)
    e_chosen = jnp.take_along_axis(e_logits, g_idx[:, None, None], axis=1)[:, 0]
    e_val, e_idx = lax.top_k(jax.nn.softmax(e_chosen, axis=-1), TOP_E)
    e_val = e_val / jnp.sum(e_val, axis=-1, keepdims=True)
    e_w = jnp.sum(jax.nn.one_hot(e_idx, EXP_PER_GROUP, dtype=jnp.float32) * e_val[..., None], axis=1)
    comb = (jax.nn.one_hot(g_idx, N_GROUPS, dtype=jnp.float32)[:, :, None]
            * (p_g[:, None] * e_w)[:, None, :]).astype(h.dtype)
    out = jnp.zeros_like(hf)
    for g in range(N_GROUPS):
        gate = jnp.einsum('td,edf->tef', hf, w_gate[g])
        up = jnp.einsum('td,edf->tef', hf, w_up[g])
        act = jax.nn.silu(gate) * up * comb[:, g, :, None]
        out = out + jnp.einsum('tef,efd->td', act, w_down[g])
    return out.reshape(B, S, D)

def setup_inputs(seed: int = 0) -> dict:
    key = jax.random.key(seed)
    ks = jax.random.split(key, 24)
    f32 = jnp.float32
    nrm = lambda k, shape, fan_in, s=1.0: jax.random.normal(k, shape, f32) * (s * fan_in ** -0.5)
    small = lambda k, shape: 0.01 * jax.random.normal(k, shape, f32)
    gain = lambda k: 1.0 + 0.05 * jax.random.normal(k, (DEPTH, D_MODEL), f32)
    u = jax.random.uniform(ks[15], (DEPTH, D_RNN), f32, 0.9, 0.999)
    a0 = u ** (1.0 / RG_C)
    return {
        "x": jax.random.normal(ks[0], (BATCH, SEQ, D_MODEL), f32),
        "c": jax.random.normal(ks[1], (BATCH, D_MODEL), f32),
        "w_ada": nrm(ks[2], (DEPTH, D_MODEL, N_MOD * D_MODEL), D_MODEL, 0.5),
        "b_ada": small(ks[3], (DEPTH, N_MOD * D_MODEL)),
        "g_pre_mix": gain(ks[4]),
        "g_post_mix": gain(ks[5]),
        "g_pre_ffn": gain(ks[6]),
        "g_post_ffn": gain(ks[7]),
        "w_in": nrm(ks[8], (DEPTH, D_MODEL, D_IN), D_MODEL),
        "conv_w": nrm(ks[9], (DEPTH, CONV_WIDTH, D_RNN), CONV_WIDTH),
        "conv_b": small(ks[10], (DEPTH, D_RNN)),
        "w_rg_a": nrm(ks[11], (DEPTH, N_RNN_BLOCKS, RNN_BLOCK, RNN_BLOCK), RNN_BLOCK),
        "b_rg_a": small(ks[12], (DEPTH, D_RNN)),
        "w_rg_x": nrm(ks[13], (DEPTH, N_RNN_BLOCKS, RNN_BLOCK, RNN_BLOCK), RNN_BLOCK),
        "b_rg_x": small(ks[14], (DEPTH, D_RNN)),
        "lru_lambda": jnp.log(a0) - jnp.log1p(-a0),
        "w_out": nrm(ks[16], (DEPTH, D_MIX, D_MODEL), D_MIX),
        "w_router_group": nrm(ks[17], (DEPTH, D_MODEL, N_GROUPS), D_MODEL),
        "b_router_group": small(ks[18], (DEPTH, N_GROUPS)),
        "w_router_expert": nrm(ks[19], (DEPTH, D_MODEL, N_GROUPS * EXP_PER_GROUP), D_MODEL),
        "b_router_expert": small(ks[20], (DEPTH, N_GROUPS * EXP_PER_GROUP)),
        "w_gate": nrm(ks[21], (DEPTH, N_GROUPS, EXP_PER_GROUP, D_MODEL, D_EXPERT), D_MODEL),
        "w_up": nrm(ks[22], (DEPTH, N_GROUPS, EXP_PER_GROUP, D_MODEL, D_EXPERT), D_MODEL),
        "w_down": nrm(ks[23], (DEPTH, N_GROUPS, EXP_PER_GROUP, D_EXPERT, D_MODEL), D_EXPERT),
    }

def reference(x, c, w_ada, b_ada, g_pre_mix, g_post_mix, g_pre_ffn, g_post_ffn, w_in,
              conv_w, conv_b, w_rg_a, b_rg_a, w_rg_x, b_rg_x, lru_lambda, w_out,
              w_router_group, b_router_group, w_router_expert, b_router_expert,
              w_gate, w_up, w_down):
    B, S, D = x.shape
    cos, sin = rope_tables(S, HEAD_DIM)
    cos_i, sin_i = rope_tables(S, IDX_DIM)
    for l in range(DEPTH):
        mod = jax.nn.silu(c) @ w_ada[l] + b_ada[l]
        shift1, scale1, gate1, shift2, scale2, gate2 = [m[:, None, :] for m in jnp.split(mod, N_MOD, axis=-1)]

        h = rms_norm(x, g_pre_mix[l]) * (1 + scale1) + shift1
        proj = h @ w_in[l]
        q, k, v, qi, ki, wi, xr, xg = jnp.split(proj, IN_OFFSETS, axis=-1)
        q = apply_rope(q.reshape(B, S, N_ATTN_HEADS, HEAD_DIM), cos, sin)
        k = apply_rope(k.reshape(B, S, N_ATTN_HEADS, HEAD_DIM), cos, sin)
        v = v.reshape(B, S, N_ATTN_HEADS, HEAD_DIM)
        qi = apply_rope(qi.reshape(B, S, N_IDX_HEADS, IDX_DIM), cos_i, sin_i)
        ki = apply_rope(ki.reshape(B, S, 1, IDX_DIM), cos_i, sin_i)[:, :, 0]
        y_attn = sparse_indexed_attention(q, k, v, qi, ki, wi)
        y_rnn = rglru_branch(xr, conv_w[l], conv_b[l], w_rg_a[l], b_rg_a[l],
                             w_rg_x[l], b_rg_x[l], lru_lambda[l]) * jax.nn.gelu(xg)
        mix = jnp.concatenate([y_attn, y_rnn], axis=-1) @ w_out[l]
        x = x + gate1 * rms_norm(mix, g_post_mix[l])

        h2 = rms_norm(x, g_pre_ffn[l]) * (1 + scale2) + shift2
        y = hierarchical_moe(h2, w_router_group[l], b_router_group[l], w_router_expert[l],
                             b_router_expert[l], w_gate[l], w_up[l], w_down[l])
        x = x + gate2 * rms_norm(y, g_post_ffn[l])
    return x


_drawn_inputs = setup_inputs


def setup_inputs(seed=0):
    import zlib

    import numpy as np

    out = dict(_drawn_inputs(seed))
    spreads = {}
    factors = {'g_post_ffn': 4.133, 'b_rg_a': 8.0, 'b_rg_x': 6.227, 'b_router_group': 3.182}
    for name, (base, spread) in spreads.items():
        noise = np.random.default_rng([zlib.crc32(name.encode()), seed]).standard_normal(out[name].shape)
        drawn = base * np.exp(spread * noise) if base else spread * noise
        out[name] = __import__('jax').numpy.asarray(drawn.astype(out[name].dtype))
    for name, factor in factors.items():
        out[name] = (out[name] * factor).astype(out[name].dtype)
    return out
```

```python
from contextlib import ExitStack

import concourse.bass as bass
from concourse import mybir

P = 128
F32 = mybir.dt.float32
BF16 = mybir.dt.bfloat16
I32 = mybir.dt.int32
U32 = mybir.dt.uint32
ALU = mybir.AluOpType
ACT = mybir.ActivationFunctionType
AX = mybir.AxisListType

EPS = 1e-6
CHUNK = 64
TOPK_MAX = 256
ROPE_THETA = 10000.0
NOT_ADMISSIBLE = -3.0e38
TAKEN = -3.4e38
BETWEEN = -3.2e38
MASKED = -1.0e30
GELU_CUBIC = 0.044715
GELU_SCALE = 0.7978845608028654
SLOTS = 6
RING = 4
CAP = 64


def hybrid_block(nc, a):
    _, S, D = a["x"].shape
    NT = S // P
    KD = D // P
    H, HD = 8, D // 16
    DA = H * HD
    IH, ID = 8, 64
    R = D // 2
    RC = R // P
    NTAPS = a["conv_w"].shape[1]
    NG, NE_G = a["w_gate"].shape[1:3]
    NE = NG * NE_G
    FE = a["w_gate"].shape[4]
    FC = FE // P
    NSEL = min(TOPK_MAX, S // 4)
    ROUNDS = NSEL // 8
    NL = NG + NE
    KI = IH * ID + 3 * DA
    assert NT == 4 and KD == 8 and NSEL == P and RC == 4 and HD == ID == 64 and FC == 2

    w_in = a["w_in"][0].rearrange("(k p) n -> p k n", p=P)
    w_ada = a["w_ada"][0].rearrange("(p k) n -> p k n", k=KD)
    w_out = a["w_out"][0].rearrange("(k p) n -> p k n", p=P)
    w_gate = a["w_gate"][0].rearrange("g e (p k) f -> (g e) p k f", k=KD)
    w_up = a["w_up"][0].rearrange("g e (p k) f -> (g e) p k f", k=KD)
    w_down = a["w_down"][0].rearrange("g e (p k) n -> (g e) p k n", k=FC)
    x_rows = a["x"][0].rearrange("(t p) d -> t p d", p=P)
    out_rows = a["out"][0].rearrange("(t p) d -> t p d", p=P)

    h2_dram = nc.dram_tensor("h2_dram", [S, D], F32).ap()
    table_dram = nc.dram_tensor("table_dram", [S * NE, 1], I32).ap()
    y_dram = nc.dram_tensor("y_dram", [4 * S, D // 2], F32).ap()
    table_rows = table_dram.rearrange("(s e) one -> s (e one)", e=NE)

    with ExitStack() as ctx:
        def sb(name, shape, dt=F32):
            return ctx.enter_context(nc.sbuf_tensor(name, shape, dt))

        def sem(name):
            return ctx.enter_context(nc.semaphore(name))

        region_x = sb("region_x", [P, 4096])
        region_y = sb("region_y", [P, 4096])
        region_w = sb("region_w", [P, 4096 * SLOTS])
        region_h = sb("region_h", [P, 8192])
        region_qk = sb("region_qk", [P, 4096])
        region_v = sb("region_v", [P, 2048])
        region_m = sb("region_m", [P, 1280])
        region_t = sb("region_t", [P, 4096])
        ident = sb("ident", [P, P])
        c_rep = sb("c_rep", [P, KD, 32])
        before = sb("before", [P, P], BF16)
        ones_b = sb("ones_b", [P, P], BF16)
        small = sb("small", [P, 192])

        ada = region_x[:, 0:1536].rearrange("p (s n) -> p s n", s=3)
        gain = region_x[:, 1536:3072].rearrange("p (s n) -> p s n", s=3)
        kiT = region_x[:, 3072:3584]
        rope_cos = region_x[:, 3584:3712].rearrange("p (t f) -> p t f", t=NT)
        rope_sin = region_x[:, 3712:3968].rearrange("p (t s f) -> p t s f", t=NT, s=2)
        ones_f = region_x[:, 3968:4096]
        x2 = region_x[:, :].rearrange("p (t d) -> p t d", t=NT)
        x_in_sb = region_y[:, :].rearrange("p (t d) -> p t d", t=NT)
        roped = region_y[:, 0:1024].rearrange("p (b n) -> p b n", b=2)
        rope_tmp = region_y[:, 1024:1536]
        w_gates = region_y[:, 1536:2048].rearrange("p (g c n) -> p g c n", g=2, c=RC)
        mixT = region_y[:, :].rearrange("p (k s) -> p k s", k=KD)
        y_out = region_y[:, 0:2048].rearrange("p (b n) -> p b n", b=RING)
        xgT = region_y[:, 2048:3072].rearrange("p (b k s) -> p b k s", b=2, k=KD)
        hid = region_y[0:CAP, 3072:3584].rearrange("p (b n) -> p b n", b=2)
        silu_g = region_y[0:CAP, 3584:4096].rearrange("p (b n) -> p b n", b=2)
        slot = region_w[:, :].rearrange("p (s n) -> p s n", s=SLOTS)
        expert_w = region_w[:, :].rearrange("p (b m n) -> p b m n", b=RING, m=3)
        hT = region_h[:, 0:4096].rearrange("p (k s) -> p k s", k=KD)
        qiT = region_h[:, 4096:6144].rearrange("p (k s) -> p k s", k=4)
        xr = region_h[:, 6144:8192].rearrange("p (c s) -> p c s", c=RC)
        wo_sb = region_h[:, :].rearrange("p (k n) -> p k n", k=KD)
        x_gath = region_h[0:CAP, 0:4096].rearrange("p (b n) -> p b n", b=RING)
        y_back = region_h[:, :].rearrange("p (k t n) -> p k t n", k=2, t=NT)
        qT = region_qk[:, 0:2048].rearrange("p (k s) -> p k s", k=4)
        kT = region_qk[:, 2048:4096].rearrange("p (k s) -> p k s", k=4)
        mod_rows = region_qk[:, :].rearrange("p (m n) -> p m n", m=4)
        GATE1, SHIFT2, SCALE2, GATE2 = range(4)
        v_sb = region_v[:, :].rearrange("p (t n) -> p t n", t=NT)
        h2T = region_v[:, :].rearrange("p (b k s) -> p b k s", b=2, k=KD)
        hidT = region_v[:, 0:256].rearrange("p (b k s) -> p b k s", b=2, k=FC)
        score_at = [0, 128, 384, 768]
        score = [region_m[:, score_at[t]:score_at[t] + P * (t + 1)] for t in range(NT)]
        m_at = [0]

        def in_m(n, dt=F32):
            m_at[0] += n
            v = region_m[:, m_at[0] - n:m_at[0]]
            return v if dt == F32 else v.bitcast(dt)

        w_router = in_m(KD * NL).rearrange("p (k n) -> p k n", k=KD)
        b_router = in_m(NL)
        logit = in_m(NT * NL).rearrange("p (t n) -> p t n", t=NT)
        group8 = in_m(8)
        in_group = in_m(NT * NG).rearrange("p (t n) -> p t n", t=NT)
        choice = [in_m(NT * NE).rearrange("p (t n) -> p t n", t=NT) for _ in range(2)]
        chosen = in_m(NT * NE // 2, BF16).rearrange("p (t n) -> p t n", t=NT)
        iota_e = in_m(NE)
        route_tmp = in_m(NE)
        pos_sb = in_m(NE)
        table_sb = in_m(NE, I32)
        gather_at = in_m(NE, I32)
        scatter_at = in_m(NE, I32)
        top_e = in_m(NT * 8).rearrange("p (t n) -> p t n", t=NT)
        top_i = in_m(NT * 8, U32).rearrange("p (t n) -> p t n", t=NT)
        gtop_i = in_m(8, U32)
        junk = region_t[:, 1024:2048]
        w_kiwi = region_t[:, 0:576].rearrange("p (k n) -> p k n", k=KD)
        ki_rows = region_t[:, 576:832].rearrange("p (b n) -> p b n", b=2)
        ki_tmp = region_t[:, 832:896]
        a_rec = region_t[:, 0:2048].rearrange("p (c s) -> p c s", c=RC)
        conv = region_t[:, 2048:3072].rearrange("p (b s) -> p b s", b=2)
        tanh_r = region_t[:, 3072:3584]
        tanh_i = region_t[:, 3584:4096]
        relu_b = region_t[:, 3072:4096].rearrange("p (b s) -> p b s", b=2)
        gel = region_t[:, 3072:4096].rearrange("p (b s) -> p b s", b=2)
        prob = region_t[:, 0:3072].rearrange("p (b h s) -> p b h s", b=3, h=2)
        probT = region_t[:, 3072:4096].rearrange("p (h s) -> p h s", h=2)
        h2 = region_t[:, :].rearrange("p (t d) -> p t d", t=NT)

        n_small = [0]

        def col(n, dt=F32):
            n_small[0] += n
            v = small[:, n_small[0] - n:n_small[0]]
            return v if dt == F32 else v.bitcast(dt)

        c_col = col(KD)
        ssq = col(NT)
        rstd = col(NT)
        mod1 = col(2 * KD)
        par = col(32)
        sp4 = col(RC)
        sp4n = col(RC)
        spt = col(2 * RC)
        w_idx = col(NT * IH).rearrange("p (t n) -> p t n", t=NT)
        top8 = col(3 * 8).rearrange("p (t n) -> p t n", t=3)
        rmax = col(4)
        nmax = col(4)
        rsum = col(4)
        pssq = col(2)
        gmax = col(1)
        cw = col(2 * NT).rearrange("p (k t) -> p k t", k=2)
        token_v = col(2 * NT, I32)
        slot_i = col(2 * NT, I32)
        slot_f = col(1)
        gidx = col(RING, I32)
        sidx = col(RING, I32)
        gi_f = col(1)
        ei_f = col(2)
        half = col(1)
        most_tokens = col(2, I32)
        assert n_small[0] <= 192 and m_at[0] <= 1280, (n_small, m_at)
        par_rows = region_t[0:32, 3968:4096]

        ps = [ctx.enter_context(nc.psum_tensor(f"ps{i}", [P, 512], F32)) for i in range(8)]

        x_loaded = [sem(f"x_loaded{t}") for t in range(NT)]
        params_loaded = sem("params_loaded")
        rope_loaded = sem("rope_loaded")
        kiwi_loaded = sem("kiwi_loaded")
        gates_loaded = sem("gates_loaded")
        slot_loaded = [sem(f"slot_loaded{s}") for s in range(SLOTS)]
        ada_used = sem("ada_used")
        wo_loaded = sem("wo_loaded")
        router_loaded = sem("router_loaded")
        x_again = sem("x_again")
        setup = sem("setup")
        chain = sem("chain")
        achain = sem("achain")
        pchain = sem("pchain")
        silu_c = sem("silu_c")
        c_ready = sem("c_ready")
        sq_done = sem("sq_done")
        var_ready = sem("var_ready")
        root_ready = sem("root_ready")
        xn_ready = sem("xn_ready")
        par_T = sem("par_T")
        par_sb = sem("par_sb")
        sp_exp = sem("sp_exp")
        xT_done = sem("xT_done")
        xT_even = sem("xT_even")
        xT_odd = sem("xT_odd")
        ada_ready = sem("ada_ready")
        mod1_T = sem("mod1_T")
        h_ready = sem("h_ready")
        proj_done = sem("proj_done")
        rope_ready = sem("rope_ready")
        ropeT_done = sem("ropeT_done")
        ropeT_out = sem("ropeT_out")
        ki_done = sem("ki_done")
        ki_ready = sem("ki_ready")
        kiT_done = sem("kiT_done")
        kiT_out = sem("kiT_out")
        v_out = sem("v_out")
        dots_done = sem("dots_done")
        relu_done = sem("relu_done")
        score_acc = sem("score_acc")
        xr_done = sem("xr_done")
        xr_out = sem("xr_out")
        conv_ready = sem("conv_ready")
        gate_mm = sem("gate_mm")
        gate_act = sem("gate_act")
        rec_done = sem("rec_done")
        rec_root = sem("rec_root")
        rec_b = sem("rec_b")
        xg_done = sem("xg_done")
        xg_sq = sem("xg_sq")
        xg_cubic = sem("xg_cubic")
        xg_tanh = sem("xg_tanh")
        xg_mult = sem("xg_mult")
        mask_ready = sem("mask_ready")
        qk_done = sem("qk_done")
        nmax_ready = sem("nmax_ready")
        exp_done = sem("exp_done")
        prob_ready = sem("prob_ready")
        probT_done = sem("probT_done")
        probT_even = sem("probT_even")
        probT_odd = sem("probT_odd")
        pv_done = sem("pv_done")
        attn_out = sem("attn_out")
        rows_mm = sem("rows_mm")
        rows_out = sem("rows_out")
        mix_done = sem("mix_done")
        mix_sq = sem("mix_sq")
        mix_var = sem("mix_var")
        mix_root = sem("mix_root")
        x2_ready = sem("x2_ready")
        x2_sq = sem("x2_sq")
        x2_var = sem("x2_var")
        x2_root = sem("x2_root")
        h2_ready = sem("h2_ready")
        h2_stored = sem("h2_stored")
        h2T_done = sem("h2T_done")
        h2T_out = sem("h2T_out")
        logit_mm = sem("logit_mm")
        logit_ready = sem("logit_ready")
        route_exp = sem("route_exp")
        chosen_ready = sem("chosen_ready")
        pos_mm = sem("pos_mm")
        slots_ready = sem("slots_ready")
        table_clear = sem("table_clear")
        table_set = sem("table_set")
        table_loaded = sem("table_loaded")
        gath_idx = sem("gath_idx")
        gidx_ready = sem("gidx_ready")
        sidx_ready = sem("sidx_ready")
        gathered = [sem(f"gathered{j}") for j in range(RING)]
        expert_loaded = [sem(f"expert_loaded{j}") for j in range(RING)]
        xgT_done = sem("xgT_done")
        xgT_out = sem("xgT_out")
        gu_done = sem("gu_done")
        silu_done = sem("silu_done")
        hid_ready = sem("hid_ready")
        hidT_done = sem("hidT_done")
        hidT_out = sem("hidT_out")
        down_done = sem("down_done")
        y_ready = sem("y_ready")
        scattered = [sem(f"scattered{j}") for j in range(RING)]
        all_scattered = sem("all_scattered")
        y_loaded = [sem(f"y_loaded{t}") for t in range(NT)]
        fin_scaled = sem("fin_scaled")
        fin_sum = sem("fin_sum")
        fin_sq = sem("fin_sq")
        fin_var = sem("fin_var")
        fin_root = sem("fin_root")
        fin_out = sem("fin_out")
        stored = sem("stored")
        count_ready = sem("count_ready")
        passed = sem("passed")
        more_turn = sem("more_turn")
        more_loaded = sem("more_loaded")
        more_table = sem("more_table")
        more_idx = sem("more_idx")
        more_gathered = sem("more_gathered")
        more_xT = sem("more_xT")
        more_xT_out = sem("more_xT_out")
        more_gu = sem("more_gu")
        more_silu = sem("more_silu")
        more_hid = sem("more_hid")
        more_hidT = sem("more_hidT")
        more_hidT_out = sem("more_hidT_out")
        more_down = sem("more_down")
        more_y = sem("more_y")
        more_scattered = sem("more_scattered")

        ADA0, QI, Q, K, V, XR, XG, ADA1, ADA2 = 0, 4, 5, 6, 7, 8, 9, 10, 14
        streamed = []
        for s in (0,):
            streamed += [("ada", s, j) for j in range(4)]
        streamed += [("in", c0, 0) for c0 in (3 * DA, 0, DA, 2 * DA, KI + ID + IH, KI + ID + IH + R)]
        streamed += [("ada", s, j) for s in (1, 2) for j in range(4)]

        def slot_of(n):
            return slot[:, n % SLOTS, :]

        def wait_slot(eng, n):
            eng.wait_ge(slot_loaded[n % SLOTS], 16 * (n // SLOTS + 1))

        def wait_used(eng, n):
            if n < QI:
                eng.wait_ge(ada_used, n + 1)
            elif n < XR:
                eng.wait_ge(proj_done, NT * (n - QI + 1))
            elif n < ADA1:
                eng.wait_ge(xr_done if n == XR else xg_done, RC)
            else:
                eng.wait_ge(ada_used, n - ADA1 + 5)

        UNITS = [(w, t) for w in (QI, Q, K, V) for t in range(NT)]
        NROPE = 3 * NT
        PAIRS = [(t, hp) for t in range(NT) for hp in range(H // 2)]

        def load_expert(eng, e, j):
            for m, (w, k) in enumerate(((w_gate, KD), (w_up, KD), (w_down, FC))):
                src = w[bass.ds(e, 1)].rearrange("e p k n -> p (e k) n")
                eng.dma_start(expert_w[:, j, m, :].rearrange("p (k n) -> p k n", k=k), src).then_inc(expert_loaded[j], 16)

        def attn_copy(act, t):
            act.wait_ge(pv_done, 4 * (t + 1))
            act.activation(mixT[:, 0:4, t * P:(t + 1) * P], ps[6 + t % 2][:].rearrange("p (k s) -> p k s", k=4),
                           ACT.Copy).then_inc(attn_out, 1)

        def apart(eng):
            eng.sem_inc(passed, 1)

        def more_rounds(eng, body):
            eng.wait_ge(count_ready, 1)
            most = eng.value_load(most_tokens[0:1, 0:1], min_val=0, max_val=S)
            with eng.If(most > CAP):
                with eng.Fori(1, S // CAP) as r:
                    with eng.Fori(0, NE) as e:
                        body(r, e, r * NE + e - (NE - 1))

        block = ctx.enter_context(nc.Block())

        @block.sync
        def _(sp):
            for t in range(NT):
                sp.dma_start(x_in_sb[:, t, :], x_rows[t]).then_inc(x_loaded[t], 16)
            for n, (kind, c0, j) in enumerate(streamed):
                if n >= SLOTS:
                    wait_used(sp, n - SLOTS)
                if kind == "ada":
                    dst = slot_of(n).rearrange("p (k n) -> p k n", k=2)
                    src = w_ada[:, 2 * j:2 * j + 2, 2048 * c0:2048 * (c0 + 1)]
                else:
                    dst = slot_of(n).rearrange("p (k n) -> p k n", k=KD)
                    src = w_in[:, :, c0:c0 + 512]
                sp.dma_start(dst, src).then_inc(slot_loaded[n % SLOTS], 16)
                if n == QI:
                    sp.dma_start(w_kiwi, w_in[:, :, KI:KI + ID + IH]).then_inc(kiwi_loaded, 16)
                    sp.wait_ge(xT_done, KD)
                    for g, name in enumerate(("w_rg_a", "w_rg_x")):
                        for half in range(2):
                            w = a[name][0].rearrange("(c b) i j -> b i c j", b=2)[half]
                            sp.dma_start(w_gates[64 * half:64 * half + 64, g], w).then_inc(gates_loaded, 16)
            wait_used(sp, XG)
            sp.wait_ge(dots_done, 8 * (NT - 1))
            sp.wait_ge(rec_b, 1)
            sp.dma_start(wo_sb, w_out).then_inc(wo_loaded, 16)
            wait_used(sp, len(streamed) - 1)
            for j in range(RING):
                load_expert(sp, j, j)
            sp.wait_ge(rows_out, 8)
            for t in range(NT):
                sp.dma_start(x2[:, t, :], x_rows[t]).then_inc(x_again, 16)
            sp.wait_ge(qk_done, len(PAIRS))
            sp.wait_ge(nmax_ready, len(PAIRS))
            sp.dma_start(w_router[:, :, 0:NG], a["w_router_group"][0].rearrange("(k p) n -> p k n", p=P)).then_inc(router_loaded, 16)
            sp.dma_start(w_router[:, :, NG:NL], a["w_router_expert"][0].rearrange("(k p) n -> p k n", p=P)).then_inc(router_loaded, 16)
            sp.dma_start(b_router[:, 0:NG], a["b_router_group"][0].partition_broadcast(P)).then_inc(router_loaded, 16)
            sp.dma_start(b_router[:, NG:NL], a["b_router_expert"][0].partition_broadcast(P)).then_inc(router_loaded, 16)
            for t in range(NT):
                sp.wait_ge(h2_ready, t + 1)
                sp.dma_start(h2_dram[t * P:(t + 1) * P, :], h2[:, t, :]).then_inc(h2_stored, 16)
            sp.wait_ge(table_set, 16 * 2 * NT)
            for half in range(2):
                sp.dma_start(table_sb[CAP * half:CAP * half + CAP, :], table_rows[0:CAP, :]).then_inc(table_loaded, 16)
            with sp.Fori(0, NE // RING - 1) as i:
                for j in range(RING):
                    sp.wait_ge(down_done, i * RING + (j + 1))
                    load_expert(sp, i * RING + (j + RING), j)
            def more(r, e, m):
                sp.wait_ge(more_turn, m)
                for k, (w, kc) in enumerate(((w_gate, KD), (w_up, KD), (w_down, FC))):
                    src = w[bass.ds(e, 1)].rearrange("e p k n -> p (e k) n")
                    sp.dma_start(expert_w[:, 0, k, :].rearrange("p (k n) -> p k n", k=kc), src).then_inc(more_loaded, 16)
                for n in range(2):
                    sp.dma_start(table_sb[CAP * n:CAP * n + CAP, :], table_rows[bass.ds(r * CAP, CAP), :]).then_inc(more_loaded, 16)

            more_rounds(sp, more)
            sp.wait_ge(all_scattered, 1)
            for t in range(NT):
                for k in range(2):
                    src = y_dram[2 * (k * S + t * P):2 * (k * S + t * P + P), :].rearrange("(p two) n -> p (two n)", two=2)
                    sp.dma_start(y_back[:, k, t, :], src).then_inc(y_loaded[t], 16)
            for t in range(NT):
                sp.wait_ge(fin_out, t + 1)
                sp.dma_start(out_rows[t], y_back[:, 0, t, :]).then_inc(stored, 16)
            sp.wait_ge(stored, 16 * NT)

        @block.gpsimd
        def _(pool):
            pool.memset(ident[:], 0.0).then_inc(pchain, 1)
            pool.memset(before[:], 0.0).then_inc(pchain, 1)
            pool.wait_ge(pchain, 2)
            pool.affine_select(out=ident[:], in_=ident[:], compare_op=ALU.not_equal, fill=1.0, base=0,
                               pattern=[[-1, P]], channel_multiplier=1).then_inc(setup, 1)
            pool.affine_select(out=before[:], in_=before[:], compare_op=ALU.is_ge, fill=1.0, base=0,
                               pattern=[[-1, P]], channel_multiplier=1).then_inc(setup, 1)
            pool.memset(ones_b[:], 1.0).then_inc(setup, 1)
            pool.iota(token_v[:, :], pattern=[[S, 2], [P, NT]], base=0, channel_multiplier=1).then_inc(setup, 1)
            clear = region_v[:, 0:P].bitcast(I32)
            pool.iota(clear, pattern=[[0, P]], base=2 * S, channel_multiplier=0).then_inc(pchain, 1)
            pool.wait_ge(pchain, 3)
            pool.dma_start(table_dram.rearrange("(p n) one -> p (n one)", p=P), clear).then_inc(table_clear, 16)
            pool.wait_ge(nmax_ready, len(PAIRS))
            pool.iota(iota_e, pattern=[[1, NE]], base=0, channel_multiplier=0,
                      allow_small_or_imprecise_dtypes=True).then_inc(setup, 1)
            pool.wait_ge(table_clear, 16)
            pool.wait_ge(slots_ready, 1)
            for n in range(2 * NT):
                pool.indirect_dma_start(out=table_dram, out_offset=bass.IndirectOffsetOnAxis(ap=slot_i[:, n:n + 1], axis=0),
                                        in_=token_v[:, n:n + 1], in_offset=None).then_inc(table_set, 16)
            pool.wait_ge(h2_stored, 16 * NT)
            pool.wait_ge(gath_idx, 1)

            def gather(e, j):
                pool.tensor_copy(gidx[0:CAP, j:j + 1], gather_at[0:CAP, bass.ds(e, 1)]).then_inc(gidx_ready, 1)
                pool.wait_ge(gidx_ready, e + 1)
                apart(pool)
                pool.indirect_dma_start(out=x_gath[:, j, :], out_offset=None, in_=h2_dram,
                                        in_offset=bass.IndirectOffsetOnAxis(ap=gidx[0:CAP, j:j + 1], axis=0)).then_inc(gathered[j], 16)

            def scatter(e, j, turn):
                if not (isinstance(turn, int) and turn == 0):
                    pool.wait_ge(scattered[j], turn * 16)
                pool.tensor_copy(sidx[:, j:j + 1], scatter_at[:, bass.ds(e, 1)]).then_inc(sidx_ready, 1)
                pool.wait_ge(sidx_ready, e + 1)
                pool.wait_ge(y_ready, e + 1)
                apart(pool)
                pool.indirect_dma_start(out=y_dram, out_offset=bass.IndirectOffsetOnAxis(ap=sidx[:, j:j + 1], axis=0),
                                        in_=y_out[:, j, :], in_offset=None, bounds_check=4 * S - 1,
                                        oob_is_err=False).then_inc(scattered[j], 16)

            def pool_turn(i):
                for j in range(RING):
                    pool.wait_ge(xgT_done, i * RING + (j + 1))
                    apart(pool)
                    gather(i * RING + (j + RING), j)
                    scatter(i * RING + j, j, i)

            for j in range(RING):
                gather(j, j)
            pool_turn(0)
            with pool.Fori(1, NE // RING - 1) as i:
                pool_turn(i)
            for j in range(RING):
                scatter(NE - RING + j, j, NE // RING - 1)
            for j in range(RING):
                pool.wait_ge(scattered[j], NE // RING * 16)

            def more(r, e, m):
                pool.wait_ge(more_table, m * 2)
                pool.tensor_copy(gidx[0:CAP, 0:1], gather_at[0:CAP, bass.ds(e, 1)]).then_inc(more_idx, 1)
                pool.tensor_copy(sidx[:, 0:1], scatter_at[:, bass.ds(e, 1)]).then_inc(more_idx, 1)
                pool.wait_ge(more_idx, m * 2)
                apart(pool)
                pool.indirect_dma_start(out=x_gath[:, 0, :], out_offset=None, in_=h2_dram,
                                        in_offset=bass.IndirectOffsetOnAxis(ap=gidx[0:CAP, 0:1], axis=0)).then_inc(more_gathered, 16)
                pool.wait_ge(more_y, m)
                apart(pool)
                pool.indirect_dma_start(out=y_dram, out_offset=bass.IndirectOffsetOnAxis(ap=sidx[:, 0:1], axis=0),
                                        in_=y_out[:, 0, :], in_offset=None, bounds_check=4 * S - 1,
                                        oob_is_err=False).then_inc(more_scattered, 16)
                pool.wait_ge(more_scattered, m * 16)
                pool.sem_inc(more_turn, 1)

            pool.sem_inc(more_turn, 1)
            more_rounds(pool, more)
            pool.engine_nop().then_inc(all_scattered, 1)

        @block.tensor
        def _(pe):
            pe.wait_ge(setup, 1)
            for t in range(NT):
                pe.wait_ge(xn_ready, t + 1)
            for k in range(KD):
                for t in range(NT):
                    last = pe.transpose(ps[k][:, t * P:(t + 1) * P], x_in_sb[:, t, k * P:(k + 1) * P], ident[:])
                last.then_inc(xT_done, 1)

            def ada_pass(s, n0, bank):
                for j in range(4):
                    wait_slot(pe, n0 + j)
                    w = slot_of(n0 + j).rearrange("p (k n) -> p k n", k=2)
                    for kk in range(2):
                        k = 2 * j + kk
                        for r in range(4):
                            last = pe.matmul(ps[bank][32 * r:32 * r + 32, :], c_rep[:, k, :],
                                             w[:, kk, 512 * r:512 * (r + 1)], start=(k == 0), stop=(k == KD - 1))
                    last.then_inc(ada_used, 1)

            pe.wait_ge(c_ready, 1)
            pe.wait_ge(xT_even, 1)
            pe.wait_ge(xT_odd, 1)
            pe.wait_ge(params_loaded, 16 * 14)
            pe.transpose(ps[1][:, 0:32], par_rows, ident[0:32, 0:32]).then_inc(par_T, 1)
            ada_pass(0, ADA0, 0)
            pe.wait_ge(ada_ready, 1)
            pe.wait_ge(par_sb, 1)
            for j in range(4):
                last = pe.transpose(ps[1][:, j * P:(j + 1) * P], ada[:, 0, j * P:(j + 1) * P], ident[:])
            last.then_inc(mod1_T, 1)

            def rope_T(u):
                pe.wait_ge(rope_ready, u + 1)
                if u >= 2:
                    pe.wait_ge(ropeT_out, u - 1)
                else:
                    pe.wait_ge(xT_even, KD // 2)
                    pe.wait_ge(xT_odd, KD // 2)
                for j in range(4):
                    last = pe.transpose(ps[2 + u % 2][:, j * P:(j + 1) * P], roped[:, u % 2, j * P:(j + 1) * P], ident[:])
                last.then_inc(ropeT_done, 1)

            def ki_T(t):
                pe.wait_ge(ki_ready, t + 1)
                pe.transpose(ps[5][:, t * P:(t + 1) * P], ki_rows[:, t % 2, :], ident[:]).then_inc(kiT_done, 1)

            def index_dots(t):
                for h in range(IH):
                    n = (t - 1) * IH + h
                    if n >= 2:
                        pe.wait_ge(relu_done, n - 1)
                    hp = 64 * (h % 2)
                    pe.matmul(ps[6 + h % 2][:, 0:P * (t + 1)], qiT[hp:hp + 64, h // 2, t * P:(t + 1) * P],
                              kiT[hp:hp + 64, 0:P * (t + 1)], start=True, stop=True).then_inc(dots_done, 1)

            for u, (w, t) in enumerate(UNITS):
                wait_slot(pe, w)
                if u < 2:
                    pe.wait_ge(mod1_T, 1)
                elif u - 2 < NROPE:
                    pe.wait_ge(rope_ready, u - 1)
                else:
                    pe.wait_ge(v_out, u - 1 - NROPE)
                wt = slot_of(w).rearrange("p (k n) -> p k n", k=KD)
                for k in range(KD):
                    if u == 0:
                        pe.wait_ge(h_ready, k + 1)
                    last = pe.matmul(ps[u % 2][:], hT[:, k, t * P:(t + 1) * P], wt[:, k, :], start=(k == 0), stop=(k == KD - 1))
                last.then_inc(proj_done, 1)
                if w == QI:
                    pe.wait_ge(kiwi_loaded, 16)
                    pe.wait_ge(xT_even, KD // 2)
                    if t >= 2:
                        pe.wait_ge(ki_ready, t - 1)
                    for k in range(KD):
                        last = pe.matmul(ps[4 + 2 * (t % 2)][:, 0:ID + IH], hT[:, k, t * P:(t + 1) * P], w_kiwi[:, k, :],
                                         start=(k == 0), stop=(k == KD - 1))
                    last.then_inc(ki_done, 1)
                if 1 <= u <= NROPE:
                    rope_T(u - 1)
                if 1 <= u <= NT:
                    ki_T(u - 1)
                if u in (5, 6, 7):
                    if u == 5:
                        pe.wait_ge(ropeT_out, NT)
                        pe.wait_ge(kiT_out, 1)
                    index_dots(u - 4)

            def proj_T(n, c, bank, done):
                wt = slot_of(n).rearrange("p (k n) -> p k n", k=KD)
                for k in range(KD):
                    last = pe.matmul(ps[bank][:], wt[:, k, c * P:(c + 1) * P], hT[:, k, :], start=(k == 0), stop=(k == KD - 1))
                last.then_inc(done, 1)

            def gates(c):
                pe.wait_ge(conv_ready, c + 1)
                if c >= 1:
                    pe.wait_ge(gate_act, c)
                for g in range(2):
                    for half in range(2):
                        r = slice(64 * half, 64 * half + 64)
                        last = pe.matmul(ps[4 + g][r, :], w_gates[r, g, c, :], conv[r, c % 2, :], start=True, stop=True)
                last.then_inc(gate_mm, 1)

            wait_slot(pe, XR)
            pe.wait_ge(v_out, NT)
            pe.wait_ge(gates_loaded, 64)
            for c in range(RC):
                if c >= 2:
                    pe.wait_ge(xr_out, c - 1)
                proj_T(XR, c, c % 2, xr_done)
                if c >= 1:
                    gates(c - 1)
            wait_slot(pe, XG)
            pe.wait_ge(ropeT_out, NROPE)
            pe.wait_ge(relu_done, IH * (NT - 1))
            for c in range(RC):
                proj_T(XG, c, (2, 3, 6, 7)[c], xg_done)
                if c == 0:
                    gates(RC - 1)
            pe.wait_ge(xr_out, RC)
            ada_pass(1, ADA1, 0)
            ada_pass(2, ADA2, 1)

            def scores_mm(i):
                t, hp = PAIRS[i]
                if i == 0:
                    pe.wait_ge(ada_ready, 3)
                    pe.wait_ge(xg_mult, RC)
                if i >= 2:
                    pe.wait_ge(nmax_ready, i - 1)
                for hh in range(2):
                    r = slice(64 * hh, 64 * hh + 64)
                    last = pe.matmul(ps[2 * (i % 2) + hh][:, 0:P * (t + 1)], qT[r, hp, t * P:(t + 1) * P],
                                     kT[r, hp, 0:P * (t + 1)], start=True, stop=True)
                last.then_inc(qk_done, 1)

            def prob_T(i):
                t, hp = PAIRS[i]
                pe.wait_ge(prob_ready, i + 1)
                if i >= 1:
                    pe.wait_ge(probT_even, i)
                    pe.wait_ge(probT_odd, i)
                for hh in range(2):
                    for kc in range(t + 1):
                        last = pe.transpose(ps[4 + hh][:, kc * P:(kc + 1) * P], prob[:, i % 3, hh, kc * P:(kc + 1) * P], ident[:])
                last.then_inc(probT_done, 1)

            def values_mm(i):
                t, hp = PAIRS[i]
                pe.wait_ge(probT_even, i + 1)
                pe.wait_ge(probT_odd, i + 1)
                if hp == 0 and t >= 2:
                    pe.wait_ge(attn_out, t - 1)
                for kc in range(t + 1):
                    for hh in range(2):
                        h = 2 * hp + hh
                        last = pe.matmul(ps[6 + t % 2][64 * hh:64 * hh + 64, hp * P:(hp + 1) * P], v_sb[:, kc, h * HD:(h + 1) * HD],
                                         probT[:, hh, kc * P:(kc + 1) * P], start=(kc == 0), stop=(kc == t))
                last.then_inc(pv_done, 1)

            for i in range(len(PAIRS) + 3):
                if i < len(PAIRS):
                    scores_mm(i)
                if 2 <= i < len(PAIRS) + 2:
                    prob_T(i - 2)
                if i >= 3:
                    values_mm(i - 3)

            pe.wait_ge(nmax_ready, len(PAIRS))
            for s in range(2):
                for r in range(4):
                    if s == 1:
                        pe.wait_ge(rows_out, r + 1)
                    pe.matmul(ps[r][:], ones_f[32 * r:32 * r + 1, :], ada[32 * r:32 * r + 1, 1 + s, :],
                              start=True, stop=True).then_inc(rows_mm, 1)

            def router(t):
                pe.wait_ge(h2_ready, t + 1)
                if t >= 1:
                    pe.wait_ge(h2T_out, t)
                for k in range(KD):
                    last = pe.transpose(ps[4 + k // 4][:, (k % 4) * P:(k % 4 + 1) * P], h2[:, t, k * P:(k + 1) * P], ident[:])
                last.then_inc(h2T_done, 1)
                pe.wait_ge(h2T_out, t + 1)
                if t == 0:
                    pe.wait_ge(router_loaded, 64)
                    pe.wait_ge(attn_out, NT)
                if t >= 2:
                    pe.wait_ge(chosen_ready, t - 1)
                for k in range(KD):
                    last = pe.matmul(ps[6 + t % 2][:, 0:NL], h2T[:, t % 2, k, :], w_router[:, k, :],
                                     start=(k == 0), stop=(k == KD - 1))
                last.then_inc(logit_mm, 1)

            pe.wait_ge(wo_loaded, 16)
            pe.wait_ge(attn_out, NT)
            pe.wait_ge(rows_out, 8)
            for t in range(NT):
                if t >= 2:
                    pe.wait_ge(x2_ready, t - 1)
                for n in range(2):
                    for k in range(KD):
                        last = pe.matmul(ps[2 * (t % 2) + n][:], mixT[:, k, t * P:(t + 1) * P], wo_sb[:, k, 512 * n:512 * (n + 1)],
                                         start=(k == 0), stop=(k == KD - 1))
                last.then_inc(mix_done, 1)
                if t >= 1:
                    router(t - 1)
            router(NT - 1)
            pe.wait_ge(chosen_ready, NT)
            for t in range(NT):
                for s in range(t + 1):
                    last = pe.matmul(ps[7][:, t * NE:(t + 1) * NE], before[:] if s == t else ones_b[:], chosen[:, s, :],
                                     start=(s == 0), stop=(s == t))
            for s in range(NT):
                last = pe.matmul(ps[7][:, NT * NE:(NT + 1) * NE], ones_b[:], chosen[:, s, :], start=(s == 0), stop=(s == NT - 1))
            last.then_inc(pos_mm, 1)

            def rows_T(e, j, turn):
                pe.wait_ge(gathered[j], turn * 16 + 16)
                if not (isinstance(e, int) and e < 2):
                    pe.wait_ge(xgT_out, e - 1)
                apart(pe)
                for k in range(KD):
                    last = pe.transpose(ps[j % 2][:, k * CAP:(k + 1) * CAP], x_gath[:, j, k:D:KD], ident[0:CAP, 0:CAP])
                last.then_inc(xgT_done, 1)

            def gate_up(e, j, turn):
                pe.wait_ge(expert_loaded[j], turn * 48 + 48)
                pe.wait_ge(xgT_out, e + 1)
                if not (isinstance(e, int) and e < 2):
                    pe.wait_ge(hid_ready, e - 1)
                for k in range(KD):
                    for m in range(2):
                        last = pe.matmul(ps[2 + j % 2][CAP * m:CAP * m + CAP, 0:FE], xgT[:, j % 2, k, :],
                                         expert_w[:, j, m, k * FE:(k + 1) * FE], start=(k == 0), stop=(k == KD - 1))
                last.then_inc(gu_done, 1)

            def hidden_T(e, j):
                pe.wait_ge(hid_ready, e + 1)
                apart(pe)
                for k in range(FC):
                    last = pe.transpose(ps[4 + j % 2][:, k * CAP:(k + 1) * CAP], hid[:, j % 2, k:FE:FC], ident[0:CAP, 0:CAP])
                last.then_inc(hidT_done, 1)

            def down(e, j):
                pe.wait_ge(hidT_out, e + 1)
                if not (isinstance(e, int) and e < 2):
                    pe.wait_ge(y_ready, e - 1)
                for k in range(FC):
                    for n in range(2):
                        last = pe.matmul(ps[6 + j % 2][CAP * n:CAP * n + CAP, :], hidT[:, j % 2, k, :],
                                         expert_w[:, j, 2, k * D + 512 * n:k * D + 512 * (n + 1)],
                                         start=(k == 0), stop=(k == FC - 1))
                last.then_inc(down_done, 1)

            def turn_of(i, n):
                return i + n // RING

            def step(i, n):
                e, j = i * RING + n, n % RING
                gate_up(e, j, turn_of(i, n))
                hidden_T(i * RING + (n - 1), (n - 1) % RING)
                rows_T(i * RING + (n + 1), (n + 1) % RING, turn_of(i, n + 1))
                down(i * RING + (n - 1), (n - 1) % RING)

            pe.wait_ge(slots_ready, 1)
            rows_T(0, 0, 0)
            gate_up(0, 0, 0)
            rows_T(1, 1, 0)
            step(0, 1)
            step(0, 2)
            with pe.Fori(0, NE // RING - 1) as i:
                for n in range(3, 3 + RING):
                    step(i, n)
            gate_up(NE - 1, RING - 1, NE // RING - 1)
            hidden_T(NE - 2, RING - 2)
            down(NE - 2, RING - 2)
            hidden_T(NE - 1, RING - 1)
            down(NE - 1, RING - 1)

            def more(r, e, m):
                pe.wait_ge(more_loaded, m * 80)
                pe.wait_ge(more_gathered, m * 16)
                apart(pe)
                for k in range(KD):
                    last = pe.transpose(ps[0][:, k * CAP:(k + 1) * CAP], x_gath[:, 0, k:D:KD], ident[0:CAP, 0:CAP])
                last.then_inc(more_xT, 1)
                pe.wait_ge(more_xT_out, m)
                for k in range(KD):
                    for g in range(2):
                        last = pe.matmul(ps[2][CAP * g:CAP * g + CAP, 0:FE], xgT[:, 0, k, :],
                                         expert_w[:, 0, g, k * FE:(k + 1) * FE], start=(k == 0), stop=(k == KD - 1))
                last.then_inc(more_gu, 1)
                pe.wait_ge(more_hid, m)
                apart(pe)
                for k in range(FC):
                    last = pe.transpose(ps[4][:, k * CAP:(k + 1) * CAP], hid[:, 0, k:FE:FC], ident[0:CAP, 0:CAP])
                last.then_inc(more_hidT, 1)
                pe.wait_ge(more_hidT_out, m)
                for k in range(FC):
                    for n in range(2):
                        last = pe.matmul(ps[6][CAP * n:CAP * n + CAP, :], hidT[:, 0, k, :],
                                         expert_w[:, 0, 2, k * D + 512 * n:k * D + 512 * (n + 1)],
                                         start=(k == 0), stop=(k == FC - 1))
                last.then_inc(more_down, 1)

            more_rounds(pe, more)

        @block.scalar
        def _(act):
            n = [0]

            def link(ins):
                n[0] += 1
                ins.then_inc(achain, 1)
                act.wait_ge(achain, n[0])

            act.dma_start(c_col, a["c"][0].rearrange("(p k) -> p k", k=KD)).then_inc(params_loaded, 16)
            rows = (("conv_w", 0, 16), ("conv_b", 16, 4), ("b_rg_a", 20, 4), ("b_rg_x", 24, 4), ("lru_lambda", 28, 4))
            for name, r0, nr in rows:
                src = a[name][0]
                src = src.rearrange("w (c p) -> (w c) p", p=P) if name == "conv_w" else src.rearrange("(c p) -> c p", p=P)
                act.dma_start(par_rows[r0:r0 + nr, :], src).then_inc(params_loaded, 16)
            b_quad = a["b_ada"][0].rearrange("(q n) -> q n", n=512)
            for s in range(3):
                for r in range(4):
                    act.dma_start(ada[32 * r:32 * r + 32, s, :], b_quad[4 * s + r].partition_broadcast(32)).then_inc(rope_loaded, 16)
            for name, s, half in (("g_pre_mix", 0, 1), ("g_post_mix", 1, 0), ("g_pre_ffn", 2, 0), ("g_post_ffn", 2, 1)):
                g = a[name][0].rearrange("(q n) -> q n", n=512)
                for q in range(2):
                    r = 2 * half + q
                    act.dma_start(gain[32 * r:32 * r + 32, s, :], g[q].partition_broadcast(32)).then_inc(params_loaded, 16)
            act.dma_start(rope_cos, a["rope_cos"].rearrange("(t p) f -> p t f", p=P)).then_inc(rope_loaded, 16)
            act.dma_start(rope_sin, a["rope_sin"].rearrange("(t p) s f -> p t s f", p=P)).then_inc(rope_loaded, 16)
            for t in range(NT):
                act.wait_ge(x_loaded[t], 16)
                if t >= 1:
                    act.wait_ge(sq_done, t)
                act.activation(junk, x_in_sb[:, t, :], ACT.Square, accum_out=ssq[:, t:t + 1]).then_inc(sq_done, 1)
            act.wait_ge(var_ready, 1)
            act.activation(rstd, rstd, ACT.Sqrt).then_inc(root_ready, 1)
            act.wait_ge(params_loaded, 16 * 14)
            act.activation(c_col, c_col, ACT.Silu).then_inc(silu_c, 1)
            for k in range(0, KD, 2):
                act.wait_ge(xT_done, k + 1)
                act.activation(hT[:, k, :], ps[k][:], ACT.Copy).then_inc(xT_even, 1)
            act.wait_ge(par_sb, 2)
            act.activation(spt[:, 0:RC], spt[:, 0:RC], ACT.Exp, scale=-1.0).then_inc(sp_exp, 1)

            def unit_out(u):
                dst = {QI: qiT, Q: qT, K: kT}[UNITS[u][0]]
                t = UNITS[u][1]
                act.wait_ge(ropeT_done, u + 1)
                act.activation(dst[:, :, t * P:(t + 1) * P], ps[2 + u % 2][:].rearrange("p (k s) -> p k s", k=4),
                               ACT.Copy).then_inc(ropeT_out, 1)

            def relus(t):
                for h in range(IH):
                    m = (t - 1) * IH + h
                    act.wait_ge(dots_done, m + 1)
                    if m >= 2:
                        act.wait_ge(score_acc, m - 1)
                    act.activation(relu_b[:, m % 2, 0:P * (t + 1)], ps[6 + h % 2][:, 0:P * (t + 1)], ACT.Relu).then_inc(relu_done, 1)

            for u, (w, t) in enumerate(UNITS):
                if w == V:
                    act.wait_ge(proj_done, u + 1)
                    act.wait_ge(table_clear, 16)
                    act.activation(v_sb[:, t, :], ps[u % 2][:], ACT.Copy).then_inc(v_out, 1)
                    if u == NROPE:
                        unit_out(u - 1)
                if 1 <= u < NROPE:
                    unit_out(u - 1)
                if u == NT:
                    act.wait_ge(kiT_done, NT)
                    act.activation(kiT, ps[5][:], ACT.Copy).then_inc(kiT_out, 1)
                if u in (5, 6, 7):
                    relus(u - 4)

            def gate_acts(c):
                act.wait_ge(gate_mm, c + 1)
                if c >= 1:
                    act.wait_ge(rec_done, c)
                act.activation(tanh_r, ps[4][:], ACT.Tanh, bias=par[:, 20 + c:21 + c], scale=0.5).then_inc(achain, 1)
                act.activation(tanh_i, ps[5][:], ACT.Tanh, bias=par[:, 24 + c:25 + c], scale=0.5).then_inc(achain, 1)
                n[0] += 2
                act.wait_ge(achain, n[0])
                link(act.activation(a_rec[:, c, :], tanh_r, ACT.Exp, bias=sp4n[:, c:c + 1], scale=sp4n[:, c:c + 1]))
                act.activation(tanh_r, tanh_r, ACT.Tanh, bias=sp4[:, c:c + 1], scale=sp4[:, c:c + 1]).then_inc(gate_act, 1)

            act.wait_ge(par_sb, 3)
            for c in range(RC):
                act.wait_ge(xr_done, c + 1)
                act.activation(xr[:, c, :], ps[c % 2][:], ACT.Copy).then_inc(xr_out, 1)
                if c >= 1:
                    gate_acts(c - 1)
            gate_acts(RC - 1)
            act.wait_ge(rec_done, RC)
            m_all = xr.rearrange("p c s -> p (c s)")
            act.activation(m_all, m_all, ACT.Sqrt, scale=0.25).then_inc(rec_root, 1)

            def gelu_sq(c):
                act.wait_ge(xg_done, c + 1)
                if c >= 2:
                    act.wait_ge(xg_mult, c - 1)
                act.activation(gel[:, c % 2, :], ps[(2, 3, 6, 7)[c]][:], ACT.Square).then_inc(xg_sq, 1)

            gelu_sq(0)
            for c in range(RC):
                if c + 1 < RC:
                    gelu_sq(c + 1)
                act.wait_ge(xg_cubic, c + 1)
                act.activation(gel[:, c % 2, :], gel[:, c % 2, :], ACT.Tanh, scale=GELU_SCALE).then_inc(xg_tanh, 1)

            def exps(i):
                t, hp = PAIRS[i]
                act.wait_ge(nmax_ready, i + 1)
                if i >= 2:
                    act.wait_ge(prob_ready, i - 1)
                for hh in range(2):
                    p = prob[:, i % 3, hh, 0:P * (t + 1)]
                    q = 2 * (i % 2) + hh
                    act.activation(p, p, ACT.Exp, bias=nmax[:, q:q + 1], scale=HD ** -0.5, accum_out=rsum[:, q:q + 1]).then_inc(exp_done, 1)

            def probT_copy(i):
                t, hp = PAIRS[i]
                act.wait_ge(probT_done, i + 1)
                if i >= 1:
                    act.wait_ge(pv_done, i)
                act.activation(probT[:, 0, 0:P * (t + 1)], ps[4][:, 0:P * (t + 1)], ACT.Copy).then_inc(probT_even, 1)

            for i in range(len(PAIRS) + 2):
                if i < len(PAIRS):
                    exps(i)
                if i >= 2:
                    probT_copy(i - 2)
                if i >= 3 and (i - 3) % 4 == 3:
                    attn_copy(act, (i - 3) // 4)
            attn_copy(act, NT - 1)
            for m in range(8):
                act.wait_ge(rows_mm, m + 1)
                act.activation(mod_rows[:, m // 2, 512 * (m % 2):512 * (m % 2 + 1)], ps[m % 4][:], ACT.Copy).then_inc(rows_out, 1)

            def mix_norm(t):
                act.wait_ge(mix_done, t + 1)
                for m in range(2):
                    if t >= 1 and m == 0:
                        act.wait_ge(mix_var, t)
                    act.activation(h2[:, t, 512 * m:512 * (m + 1)], ps[2 * (t % 2) + m][:], ACT.Square,
                                   accum_out=pssq[:, m:m + 1]).then_inc(mix_sq, 1)
                act.wait_ge(mix_var, t + 1)
                act.activation(rstd[:, t:t + 1], ssq[:, t:t + 1], ACT.Sqrt).then_inc(mix_root, 1)

            def x2_norm(t):
                act.wait_ge(x2_ready, t + 1)
                act.activation(h2[:, t, :], x2[:, t, :], ACT.Square, accum_out=ssq[:, t:t + 1]).then_inc(x2_sq, 1)
                act.wait_ge(x2_var, t + 1)
                act.activation(rstd[:, t:t + 1], ssq[:, t:t + 1], ACT.Sqrt).then_inc(x2_root, 1)

            def h2T_copy(t):
                act.wait_ge(h2T_done, t + 1)
                for m in range(2):
                    last = act.activation(h2T[:, t % 2, 4 * m:4 * m + 4, :].rearrange("p k s -> p (k s)"), ps[4 + m][:], ACT.Copy)
                last.then_inc(h2T_out, 1)

            for t in range(NT):
                mix_norm(t)
                x2_norm(t)
                h2T_copy(t)
            for t in range(NT):
                act.wait_ge(logit_ready, t + 1)
                act.activation(logit[:, t, 0:NG], logit[:, t, 0:NG], ACT.Exp, accum_out=ssq[:, t:t + 1]).then_inc(route_exp, 1)
                act.activation(cw[:, 1, t:t + 1], cw[:, 1, t:t + 1], ACT.Exp).then_inc(route_exp, 1)

            def xgT_copy(e, j):
                act.wait_ge(xgT_done, e + 1)
                if not (isinstance(e, int) and e < 2):
                    act.wait_ge(gu_done, e - 1)
                act.activation(xgT[:, j % 2].rearrange("p k s -> p (k s)"), ps[j % 2][:], ACT.Copy).then_inc(xgT_out, 1)

            def silu(e, j):
                act.wait_ge(gu_done, e + 1)
                if not (isinstance(e, int) and e < 2):
                    act.wait_ge(hid_ready, e - 1)
                act.activation(silu_g[:, j % 2, :], ps[2 + j % 2][0:CAP, 0:FE], ACT.Silu).then_inc(silu_done, 1)

            xgT_copy(0, 0)
            xgT_copy(1, 1)
            silu(0, 0)
            silu(1, 1)
            with act.Fori(0, NE // RING - 1) as i:
                for m in range(2, 2 + RING):
                    xgT_copy(i * RING + m, m % RING)
                    silu(i * RING + m, m % RING)
            for m in range(NE - 2, NE):
                xgT_copy(m, m % RING)
                silu(m, m % RING)

            def more(r, e, m):
                act.wait_ge(more_xT, m)
                act.activation(xgT[:, 0].rearrange("p k s -> p (k s)"), ps[0][:], ACT.Copy).then_inc(more_xT_out, 1)
                act.wait_ge(more_gu, m)
                act.activation(silu_g[:, 0, :], ps[2][0:CAP, 0:FE], ACT.Silu).then_inc(more_silu, 1)

            more_rounds(act, more)

            def scale_first(t):
                act.wait_ge(y_loaded[t], 32)
                act.activation(y_back[:, 0, t, :], y_back[:, 0, t, :], ACT.Copy, scale=cw[:, 0, t:t + 1]).then_inc(fin_scaled, 1)

            scale_first(0)
            for t in range(NT):
                if t + 1 < NT:
                    scale_first(t + 1)
                act.wait_ge(fin_sum, t + 1)
                act.activation(h2[:, t, :], y_back[:, 0, t, :], ACT.Square, accum_out=ssq[:, t:t + 1]).then_inc(fin_sq, 1)
                act.wait_ge(fin_var, t + 1)
                act.activation(rstd[:, t:t + 1], ssq[:, t:t + 1], ACT.Sqrt).then_inc(fin_root, 1)

        @block.vector
        def _(dve):
            n = [0]

            def link(ins):
                n[0] += 1
                ins.then_inc(chain, 1)
                dve.wait_ge(chain, n[0])

            def tick(ins):
                n[0] += 1
                ins.then_inc(chain, 1)

            def settle():
                dve.wait_ge(chain, n[0])

            tick(dve.memset(gain[0:64, 0, :], 1.0))
            tick(dve.memset(gain[64:P, 1, :], 1.0))
            tick(dve.memset(ones_f, 1.0))
            tick(dve.memset(half[0:CAP, :], 0.0))
            tick(dve.memset(half[CAP:P, :], 1.0))
            tick(dve.memset(score[0], 0.0))
            settle()
            tick(dve.memset(score[0][0:CHUNK, CHUNK:P], MASKED))
            dve.wait_ge(sq_done, NT)
            dve.tensor_scalar(rstd, ssq, 1.0 / D, EPS, ALU.mult, ALU.add).then_inc(var_ready, 1)
            dve.wait_ge(root_ready, 1)
            link(dve.reciprocal(rstd, rstd))
            for t in range(NT):
                dve.tensor_scalar(x_in_sb[:, t, :], x_in_sb[:, t, :], rstd[:, t:t + 1], None, ALU.mult).then_inc(xn_ready, 1)
            dve.wait_ge(silu_c, 1)
            dve.tensor_copy(c_rep[:], c_col.unsqueeze(2).broadcast_to([P, KD, 32])).then_inc(c_ready, 1)
            for k in range(1, KD, 2):
                dve.wait_ge(xT_done, k + 1)
                dve.tensor_copy(hT[:, k, :], ps[k][:]).then_inc(xT_odd, 1)
            dve.wait_ge(par_T, 1)
            dve.tensor_copy(par, ps[1][:, 0:32]).then_inc(par_sb, 1)
            dve.wait_ge(par_sb, 1)
            lam = par[:, 28:32]
            z, q = spt[:, 0:RC], spt[:, RC:2 * RC]
            tick(dve.tensor_scalar(par[:, 20:28], par[:, 20:28], 0.5, None, ALU.mult))
            link(dve.tensor_scalar(q, lam, -1.0, None, ALU.mult))
            dve.tensor_tensor(z, lam, q, ALU.max).then_inc(par_sb, 1)
            dve.wait_ge(sp_exp, 1)
            link(dve.tensor_scalar(q, z, 2.0, None, ALU.add))
            link(dve.reciprocal(q, q))
            link(dve.tensor_tensor(z, z, q, ALU.mult))
            link(dve.tensor_tensor(q, z, z, ALU.mult))
            TERMS = 8
            link(dve.tensor_scalar(sp4, q, 1.0 / (2 * TERMS + 1), 1.0 / (2 * TERMS - 1), ALU.mult, ALU.add))
            for m in range(TERMS - 1, 0, -1):
                link(dve.tensor_tensor(sp4, sp4, q, ALU.mult))
                link(dve.tensor_scalar(sp4, sp4, 1.0 / (2 * m - 1), None, ALU.add))
            link(dve.tensor_tensor(sp4, sp4, z, ALU.mult))
            link(dve.tensor_scalar(q, lam, -1.0, 0.0, ALU.mult, ALU.max))
            link(dve.scalar_tensor_tensor(sp4, sp4, 2.0, q, ALU.mult, ALU.add))
            link(dve.tensor_scalar(sp4, sp4, 4.0, None, ALU.mult))
            dve.tensor_scalar(sp4n, sp4, -1.0, None, ALU.mult).then_inc(par_sb, 1)

            dve.wait_ge(rope_loaded, 16 * 14)
            tick(dve.tensor_scalar(ada[64:P, 0, :], ada[64:P, 0, :], 1.0, None, ALU.add))
            tick(dve.tensor_scalar(ada[0:64, 2, :], ada[0:64, 2, :], 1.0, None, ALU.add))
            settle()

            def ada_rows(s, used, bank):
                dve.wait_ge(ada_used, used)
                link(dve.tensor_tensor(ada[:, s, :], ps[bank][:], ada[:, s, :], ALU.add))
                dve.tensor_tensor(ada[:, s, :], ada[:, s, :], gain[:, s, :], ALU.mult).then_inc(ada_ready, 1)

            ada_rows(0, 4, 0)
            dve.wait_ge(mod1_T, 1)
            link(dve.tensor_copy(mod1.rearrange("p (r j) -> p r j", j=4),
                                 ps[1][:].rearrange("p (j r q) -> p r j q", j=4, q=32)[:, :, :, 0]))
            for k in range(KD):
                if k == 0:
                    dve.wait_ge(xT_even, KD // 2)
                    dve.wait_ge(xT_odd, KD // 2)
                dve.tensor_scalar(hT[:, k, :], hT[:, k, :], mod1[:, KD + k:KD + k + 1], mod1[:, k:k + 1],
                                  ALU.mult, ALU.add).then_inc(h_ready, 1)

            def rope(u):
                t = UNITS[u][1]
                dve.wait_ge(proj_done, u + 1)
                if u >= 1:
                    dve.wait_ge(rope_ready, u)
                if u >= 2:
                    dve.wait_ge(ropeT_done, u - 1)
                x = ps[u % 2][:].rearrange("p (h s f) -> p h s f", s=2, f=32)
                o = roped[:, u % 2, :].rearrange("p (h s f) -> p h s f", s=2, f=32)
                o3 = roped[:, u % 2, :].rearrange("p (h f) -> p h f", f=32)
                x3 = ps[u % 2][:].rearrange("p (h f) -> p h f", f=32)
                tmp = rope_tmp.rearrange("p (h s f) -> p h s f", s=2, f=32)
                tick(dve.tensor_tensor(o3, x3, rope_cos[:, t, :].unsqueeze(1).broadcast_to([P, 16, 32]), ALU.mult))
                link(dve.tensor_tensor(tmp, x[:, :, ::-1, :], rope_sin[:, t].unsqueeze(1).broadcast_to([P, 8, 2, 32]), ALU.mult))
                dve.tensor_tensor(roped[:, u % 2, :], roped[:, u % 2, :], rope_tmp, ALU.add).then_inc(rope_ready, 1)

            def rope_ki(t):
                dve.wait_ge(ki_done, t + 1)
                if t >= 1:
                    dve.wait_ge(ki_ready, t)
                if t >= 2:
                    dve.wait_ge(kiT_done, t - 1)
                src = ps[4 + 2 * (t % 2)][:, 0:ID]
                row = ki_rows[:, t % 2, :].rearrange("p (a n) -> p a n", a=2)
                tick(dve.tensor_tensor(row[:, 0, :].rearrange("p (s f) -> p s f", s=2), src.rearrange("p (s f) -> p s f", s=2),
                                       rope_cos[:, t, :].unsqueeze(1).broadcast_to([P, 2, 32]), ALU.mult))
                tick(dve.tensor_tensor(ki_tmp.rearrange("p (s f) -> p s f", s=2), src.rearrange("p (s f) -> p s f", s=2)[:, ::-1, :],
                                       rope_sin[:, t], ALU.mult))
                tick(dve.tensor_scalar(w_idx[:, t, :], ps[4 + 2 * (t % 2)][:, ID:ID + IH], IH ** -0.5 * ID ** -0.5, None, ALU.mult))
                settle()
                link(dve.tensor_tensor(row[:, 0, :], row[:, 0, :], ki_tmp, ALU.add))
                dve.tensor_copy(row[:, 1, :], row[:, 0, :]).then_inc(ki_ready, 1)

            def index_sum(t):
                for h in range(IH):
                    m = (t - 1) * IH + h
                    dve.wait_ge(relu_done, m + 1)
                    r = relu_b[:, m % 2, 0:P * (t + 1)]
                    if h == 0:
                        dve.tensor_scalar(score[t], r, w_idx[:, t, 0:1], None, ALU.mult).then_inc(score_acc, 1)
                    else:
                        dve.wait_ge(score_acc, m)
                        dve.scalar_tensor_tensor(score[t], r, w_idx[:, t, h:h + 1], score[t], ALU.mult, ALU.add).then_inc(score_acc, 1)
                dve.wait_ge(score_acc, t * IH)
                tick(dve.memset(score[t][0:CHUNK, P * t + CHUNK:P * (t + 1)], NOT_ADMISSIBLE))

            def topk_round():
                settle()
                for t in range(1, NT):
                    tick(dve.max(top8[:, t - 1, :], score[t]))
                for t in range(1, NT):
                    dve.wait_ge(chain, n[0] - (NT - 1 - t) - (t - 1))
                    tick(dve.match_replace(score[t], top8[:, t - 1, :], score[t], TAKEN))

            for u in range(NROPE):
                rope(u)
                if u < NT:
                    rope_ki(u)
                if u in (5, 6, 7):
                    index_sum(u - 4)
                if u >= 8:
                    topk_round()
                    topk_round()
            for _ in range(ROUNDS - 8):
                topk_round()
            settle()
            for t in range(1, NT):
                dve.tensor_scalar(score[t], score[t], BETWEEN, MASKED, ALU.is_gt, ALU.mult).then_inc(mask_ready, 1)

            def convolve(c):
                dve.wait_ge(xr_out, c + 1)
                if c >= 2:
                    dve.wait_ge(gate_mm, c - 1)
                o = conv[:, c % 2, :]
                tap = lambda j: par[:, RC * j + c:RC * j + c + 1]
                link(dve.tensor_scalar(o, xr[:, c, :], tap(NTAPS - 1), par[:, 16 + c:17 + c], ALU.mult, ALU.add))
                for back in range(1, NTAPS):
                    ins = dve.scalar_tensor_tensor(o[:, back:], xr[:, c, 0:S - back], tap(NTAPS - 1 - back), o[:, back:], ALU.mult, ALU.add)
                    if back < NTAPS - 1:
                        link(ins)
                    else:
                        ins.then_inc(conv_ready, 1)

            def recur_in(c):
                dve.wait_ge(conv_ready, c + 1)
                dve.wait_ge(gate_act, c + 1)
                tick(dve.scalar_tensor_tensor(mixT[:, 4 + c, :], tanh_i, 1.0, conv[:, c % 2, :], ALU.add, ALU.mult))
                link(dve.tensor_tensor(xr[:, c, :], a_rec[:, c, :], a_rec[:, c, :], ALU.mult))
                dve.scalar_tensor_tensor(xr[:, c, :], xr[:, c, :], 1.0, tanh_r, ALU.add, ALU.mult).then_inc(rec_done, 1)

            for c in range(RC):
                convolve(c)
                if c >= 1:
                    recur_in(c - 1)
            recur_in(RC - 1)
            dve.wait_ge(rec_root, 1)
            settle()
            rnn = mixT[:, 4:8, :]
            dve.tensor_tensor(rnn, rnn, xr, ALU.mult).then_inc(rec_b, 1)
            dve.wait_ge(rec_b, 1)
            for c in range(RC):
                tick(dve.tensor_tensor_scan(rnn[:, c, :], a_rec[:, c, :], rnn[:, c, :], 0.0, ALU.mult, ALU.add))

            def gelu_cubic(c):
                g = gel[:, c % 2, :]
                dve.wait_ge(xg_sq, c + 1)
                link(dve.tensor_scalar(g, g, GELU_CUBIC, 1.0, ALU.mult, ALU.add))
                dve.tensor_tensor(g, g, ps[(2, 3, 6, 7)[c]][:], ALU.mult).then_inc(xg_cubic, 1)

            gelu_cubic(0)
            for c in range(RC):
                if c + 1 < RC:
                    gelu_cubic(c + 1)
                g = gel[:, c % 2, :]
                dve.wait_ge(xg_tanh, c + 1)
                link(dve.scalar_tensor_tensor(g, g, 1.0, ps[(2, 3, 6, 7)[c]][:], ALU.add, ALU.mult))
                dve.scalar_tensor_tensor(rnn[:, c, :], g, 0.5, rnn[:, c, :], ALU.mult, ALU.mult).then_inc(xg_mult, 1)

            ada_rows(1, 8, 0)
            ada_rows(2, 12, 1)

            def masked_max(i):
                t, hp = PAIRS[i]
                dve.wait_ge(qk_done, i + 1)
                if i >= 3:
                    dve.wait_ge(probT_done, i - 2)
                if i >= 2:
                    dve.wait_ge(exp_done, 2 * (i - 1))
                if i == 0:
                    dve.wait_ge(xg_mult, RC)
                for hh in range(2):
                    q = 2 * (i % 2) + hh
                    tick(dve.tensor_tensor_reduce(prob[:, i % 3, hh, 0:P * (t + 1)], ps[2 * (i % 2) + hh][:, 0:P * (t + 1)], score[t],
                                                  1.0, TAKEN, ALU.add, ALU.max, rmax[:, q:q + 1]))
                settle()
                q = 2 * (i % 2)
                dve.tensor_scalar(nmax[:, q:q + 2], rmax[:, q:q + 2], -HD ** -0.5, None, ALU.mult).then_inc(nmax_ready, 1)

            def normalise(i):
                t, hp = PAIRS[i]
                q = 2 * (i % 2)
                dve.wait_ge(exp_done, 2 * i + 2)
                link(dve.reciprocal(rsum[:, q:q + 2], rsum[:, q:q + 2]))
                for hh in range(2):
                    p = prob[:, i % 3, hh, 0:P * (t + 1)]
                    last = dve.tensor_scalar(p, p, rsum[:, q + hh:q + hh + 1], None, ALU.mult)
                last.then_inc(prob_ready, 1)

            def probT_copy(i):
                t, hp = PAIRS[i]
                dve.wait_ge(probT_done, i + 1)
                if i >= 1:
                    dve.wait_ge(pv_done, i)
                dve.tensor_copy(probT[:, 1, 0:P * (t + 1)], ps[5][:, 0:P * (t + 1)]).then_inc(probT_odd, 1)

            dve.wait_ge(mask_ready, NT - 1)
            for i in range(len(PAIRS) + 2):
                if i < len(PAIRS):
                    masked_max(i)
                if 1 <= i <= len(PAIRS):
                    normalise(i - 1)
                if i >= 2:
                    probT_copy(i - 2)

            def post_mix(t):
                one = slice(t, t + 1)
                dve.wait_ge(mix_sq, 2 * t + 2)
                link(dve.tensor_tensor(ssq[:, one], pssq[:, 0:1], pssq[:, 1:2], ALU.add))
                dve.tensor_scalar(ssq[:, one], ssq[:, one], 1.0 / D, EPS, ALU.mult, ALU.add).then_inc(mix_var, 1)
                dve.wait_ge(mix_root, t + 1)
                link(dve.reciprocal(rstd[:, one], rstd[:, one]))
                for m in range(2):
                    w = slice(512 * m, 512 * (m + 1))
                    tick(dve.scalar_tensor_tensor(h2[:, t, w], ps[2 * (t % 2) + m][:], rstd[:, one], mod_rows[:, GATE1, w], ALU.mult, ALU.mult))
                settle()
                dve.wait_ge(x_again, 16 * NT)
                dve.tensor_tensor(x2[:, t, :], x2[:, t, :], h2[:, t, :], ALU.add).then_inc(x2_ready, 1)
                dve.wait_ge(x2_sq, t + 1)
                dve.tensor_scalar(ssq[:, one], ssq[:, one], 1.0 / D, EPS, ALU.mult, ALU.add).then_inc(x2_var, 1)
                dve.wait_ge(x2_root, t + 1)
                link(dve.reciprocal(rstd[:, one], rstd[:, one]))
                link(dve.scalar_tensor_tensor(h2[:, t, :], x2[:, t, :], rstd[:, one], mod_rows[:, SCALE2, :], ALU.mult, ALU.mult))
                dve.tensor_tensor(h2[:, t, :], h2[:, t, :], mod_rows[:, SHIFT2, :], ALU.add).then_inc(h2_ready, 1)

            def route(t):
                dve.wait_ge(logit_mm, t + 1)
                lg = logit[:, t, :]
                link(dve.tensor_tensor(lg, ps[6 + t % 2][:, 0:NL], b_router, ALU.add))
                link(dve.tensor_copy(group8[:, 0:NG], lg[:, 0:NG]))
                link(dve.max(top_e[:, t, :], group8))
                tick(dve.max_index(gtop_i, top_e[:, t, :], group8))
                tick(dve.tensor_scalar(lg[:, 0:NG], lg[:, 0:NG], top_e[:, t, 0:1], None, ALU.subtract))
                settle()
                link(dve.tensor_copy(gi_f, gtop_i[:, 0:1]))
                link(dve.tensor_scalar(in_group[:, t, :], iota_e[:, 0:NG], gi_f, None, ALU.is_equal))
                link(dve.tensor_scalar(in_group[:, t, :], in_group[:, t, :], -1.0, -MASKED, ALU.add, ALU.mult))
                link(dve.tensor_tensor(lg[:, NG:NL].rearrange("p (g e) -> p g e", g=NG), lg[:, NG:NL].rearrange("p (g e) -> p g e", g=NG),
                                       in_group[:, t, :].unsqueeze(2).broadcast_to([P, NG, NE_G]), ALU.add))
                link(dve.max(top_e[:, t, :], lg[:, NG:NL]))
                tick(dve.max_index(top_i[:, t, :], top_e[:, t, :], lg[:, NG:NL]))
                dve.tensor_tensor(cw[:, 1, t:t + 1], top_e[:, t, 1:2], top_e[:, t, 0:1], ALU.subtract).then_inc(logit_ready, 1)
                settle()
                link(dve.tensor_copy(ei_f, top_i[:, t, 0:2]))
                for k in range(2):
                    tick(dve.tensor_scalar(choice[k][:, t, :], iota_e, ei_f[:, k:k + 1], None, ALU.is_equal))
                settle()
                dve.tensor_tensor(chosen[:, t, :], choice[0][:, t, :], choice[1][:, t, :], ALU.add).then_inc(chosen_ready, 1)

            tick(dve.memset(group8, TAKEN))
            settle()
            dve.wait_ge(setup, 5)
            for t in range(NT):
                post_mix(t)
                if t >= 1:
                    if t == 1:
                        dve.wait_ge(router_loaded, 64)
                    route(t - 1)
            route(NT - 1)
            dve.wait_ge(pos_mm, 1)
            for k in range(2):
                for t in range(NT):
                    m = k * NT + t
                    link(dve.tensor_copy(pos_sb, ps[7][:, t * NE:(t + 1) * NE]))
                    link(dve.scalar_tensor_tensor(pos_sb, pos_sb, float(NE), iota_e, ALU.mult, ALU.add))
                    link(dve.tensor_tensor_reduce(route_tmp, pos_sb, choice[k][:, t, :], 1.0, 0.0, ALU.mult, ALU.add, slot_f))
                    link(dve.tensor_copy(slot_i[:, m:m + 1], slot_f))
            dve.engine_nop().then_inc(slots_ready, 1)
            link(dve.tensor_reduce(slot_f, ps[7][:, NT * NE:(NT + 1) * NE], AX.X, ALU.max))
            dve.tensor_copy(most_tokens[:, 0:1], slot_f).then_inc(count_ready, 1)
            dve.wait_ge(route_exp, 2 * NT)
            link(dve.tensor_scalar(cw[:, 0, :], cw[:, 1, :], 1.0, None, ALU.add))
            link(dve.tensor_tensor(cw[:, 0, :], cw[:, 0, :], ssq, ALU.mult))
            link(dve.reciprocal(cw[:, 0, :], cw[:, 0, :]))
            link(dve.tensor_tensor(cw[:, 1, :], cw[:, 1, :], cw[:, 0, :], ALU.mult))
            dve.wait_ge(table_loaded, 32)
            tick(dve.tensor_single_scalar(gather_at, table_sb, S - 1, ALU.bitwise_and))
            link(dve.tensor_scalar(scatter_at, table_sb, 2.0, half, ALU.mult, ALU.add))
            dve.engine_nop().then_inc(gath_idx, 1)

            def hidden(e, j):
                dve.wait_ge(silu_done, e + 1)
                if not (isinstance(e, int) and e < 2):
                    dve.wait_ge(hidT_done, e - 1)
                dve.tensor_tensor(hid[:, j % 2, :], silu_g[:, j % 2, :], ps[2 + j % 2][CAP:P, 0:FE], ALU.mult).then_inc(hid_ready, 1)

            def hiddenT_copy(e, j):
                dve.wait_ge(hidT_done, e + 1)
                if not (isinstance(e, int) and e < 2):
                    dve.wait_ge(down_done, e - 1)
                dve.tensor_copy(hidT[:, j % 2].rearrange("p k s -> p (k s)"), ps[4 + j % 2][:, 0:FC * CAP]).then_inc(hidT_out, 1)

            def y_copy(e, j, turn):
                dve.wait_ge(down_done, e + 1)
                if not (isinstance(turn, int) and turn == 0):
                    dve.wait_ge(scattered[j], turn * 16)
                dve.tensor_copy(y_out[:, j, :], ps[6 + j % 2][:]).then_inc(y_ready, 1)

            def dve_step(i, m):
                hiddenT_copy(i * RING + (m - 1), (m - 1) % RING)
                hidden(i * RING + m, m % RING)
                y_copy(i * RING + (m - 1), (m - 1) % RING, i + (m - 1) // RING)

            hidden(0, 0)
            for m in range(1, RING + 1):
                dve_step(0, m)
            with dve.Fori(1, NE // RING - 1) as i:
                for m in range(1, RING + 1):
                    dve_step(i, m)
            for m in range(1, RING):
                dve_step(NE // RING - 1, m)
            hiddenT_copy(NE - 1, RING - 1)
            y_copy(NE - 1, RING - 1, NE // RING - 1)

            def more(r, e, m):
                dve.wait_ge(more_loaded, m * 80)
                dve.tensor_single_scalar(gather_at, table_sb, S - 1, ALU.bitwise_and).then_inc(more_table, 1)
                dve.tensor_scalar(scatter_at, table_sb, 2.0, half, ALU.mult, ALU.add).then_inc(more_table, 1)
                dve.wait_ge(more_silu, m)
                dve.tensor_tensor(hid[:, 0, :], silu_g[:, 0, :], ps[2][CAP:P, 0:FE], ALU.mult).then_inc(more_hid, 1)
                dve.wait_ge(more_hidT, m)
                dve.tensor_copy(hidT[:, 0].rearrange("p k s -> p (k s)"), ps[4][:, 0:FC * CAP]).then_inc(more_hidT_out, 1)
                dve.wait_ge(more_down, m)
                dve.tensor_copy(y_out[:, 0, :], ps[6][:]).then_inc(more_y, 1)

            more_rounds(dve, more)

            def fin_add(t):
                y0, y1 = y_back[:, 0, t, :], y_back[:, 1, t, :]
                dve.wait_ge(fin_scaled, t + 1)
                dve.wait_ge(y_loaded[t], 32)
                dve.scalar_tensor_tensor(y0, y1, cw[:, 1, t:t + 1], y0, ALU.mult, ALU.add).then_inc(fin_sum, 1)

            def fin_norm(t):
                one = slice(t, t + 1)
                y0 = y_back[:, 0, t, :]
                dve.wait_ge(fin_sq, t + 1)
                dve.tensor_scalar(ssq[:, one], ssq[:, one], 1.0 / D, EPS, ALU.mult, ALU.add).then_inc(fin_var, 1)
                dve.wait_ge(fin_root, t + 1)
                link(dve.reciprocal(rstd[:, one], rstd[:, one]))
                link(dve.scalar_tensor_tensor(y0, y0, rstd[:, one], mod_rows[:, GATE2, :], ALU.mult, ALU.mult))
                dve.tensor_tensor(y0, y0, x2[:, t, :], ALU.add).then_inc(fin_out, 1)

            fin_add(0)
            for t in range(NT):
                if t + 1 < NT:
                    fin_add(t + 1)
                fin_norm(t)


_INS = ["x", "c", "w_ada", "b_ada", "g_pre_mix", "g_post_mix", "g_pre_ffn", "g_post_ffn", "w_in", "conv_w", "conv_b",
        "w_rg_a", "b_rg_a", "w_rg_x", "b_rg_x", "lru_lambda", "w_out", "w_router_group", "b_router_group",
        "w_router_expert", "b_router_expert", "w_gate", "w_up", "w_down"]


def kernel(**inputs):
    import numpy as _np
    import concourse.bacc as _bacc
    from concourse import mybir as _mybir
    from concourse.bass_utils import run_bass_kernel_spmd as _run

    nc = _bacc.Bacc("TRN2", target_bir_lowering=False, num_devices=1)
    arrays = {name: _np.ascontiguousarray(inputs[name]) for name in _INS}
    _, seq, d = arrays["x"].shape
    hd = d // 16
    inv = _np.float32(ROPE_THETA) ** (-_np.arange(0, hd, 2, dtype=_np.float32) / _np.float32(hd))
    ang = _np.arange(seq, dtype=_np.float32)[:, None] * inv.astype(_np.float32)[None, :]
    cos, sin = _np.cos(ang).astype(_np.float32), _np.sin(ang).astype(_np.float32)
    arrays["rope_cos"] = cos
    arrays["rope_sin"] = _np.ascontiguousarray(_np.stack([-sin, sin], axis=1))
    dram = {name: nc.dram_tensor(f"in_{name}_dram", v.shape, _mybir.dt.from_np(v.dtype), kind="ExternalInput").ap()
            for name, v in arrays.items()}
    dram["out"] = nc.dram_tensor("out_0_dram", (1, seq, d), _mybir.dt.float32, kind="ExternalOutput").ap()
    hybrid_block(nc, dram)
    r = _run(nc, [{f"in_{name}_dram": v for name, v in arrays.items()}], core_ids=[0])
    return r.results[0]["out_0_dram"]
```

```python
from contextlib import ExitStack

import concourse.bass as bass
from concourse import mybir

P = 128
F32 = mybir.dt.float32
F32R = mybir.dt.float32r
BF16 = mybir.dt.bfloat16
I32 = mybir.dt.int32
U32 = mybir.dt.uint32
ALU = mybir.AluOpType
ACT = mybir.ActivationFunctionType
AX = mybir.AxisListType

EPS = 1e-6
CHUNK = 64
TOPK_MAX = 256
ROPE_THETA = 10000.0
NOT_ADMISSIBLE = -3.0e38
TAKEN = -3.4e38
BETWEEN = -3.2e38
MASKED = -1.0e30
GELU_CUBIC = 0.044715
GELU_SCALE = 0.7978845608028654
SLOTS = 6
H_SLOT = 5
RING = 4
CAP = 64


def hybrid_block(nc, a):
    _, S, D = a["x"].shape
    NT = S // P
    KD = D // P
    H, HD = 8, D // 16
    DA = H * HD
    IH, ID = 8, 64
    R = D // 2
    RC = R // P
    NTAPS = a["conv_w"].shape[1]
    NG, NE_G = a["w_gate"].shape[1:3]
    NE = NG * NE_G
    FE = a["w_gate"].shape[4]
    FC = FE // P
    NSEL = min(TOPK_MAX, S // 4)
    ROUNDS = NSEL // 8
    NL = NG + NE
    KI = IH * ID + 3 * DA
    assert NT == 4 and KD == 8 and NSEL == P and RC == 4 and HD == ID == 64 and FC == 2

    w_in = a["w_in"][0].rearrange("(k p) n -> p k n", p=P)
    w_ada = a["w_ada"][0].rearrange("(p k) n -> p k n", k=KD)
    w_out = a["w_out"][0].rearrange("(k p) n -> p k n", p=P)
    w_gate = a["w_gate"][0].rearrange("g e (p k) f -> (g e) p k f", k=KD)
    w_up = a["w_up"][0].rearrange("g e (p k) f -> (g e) p k f", k=KD)
    w_down = a["w_down"][0].rearrange("g e (p k) n -> (g e) p k n", k=FC)
    x_rows = a["x"][0].rearrange("(t p) d -> t p d", p=P)
    out_rows = a["out"][0].rearrange("(t p) d -> t p d", p=P)

    h2_dram = nc.dram_tensor("h2_dram", [S, D], F32).ap()
    table_dram = nc.dram_tensor("table_dram", [S * NE, 1], I32).ap()
    y_dram = nc.dram_tensor("y_dram", [4 * S, D // 2], F32).ap()
    table_rows = table_dram.rearrange("(s e) one -> s (e one)", e=NE)

    with ExitStack() as ctx:
        def sb(name, shape, dt=F32):
            return ctx.enter_context(nc.sbuf_tensor(name, shape, dt))

        def sem(name):
            return ctx.enter_context(nc.semaphore(name))

        region_x = sb("region_x", [P, 4096])
        region_y = sb("region_y", [P, 4096])
        with nc.sbuf_tensor("split_w", [P, 4096 * SLOTS], F32R) as split_w:
            pass
        region_w = sb("region_w", [P, 4096 * SLOTS])
        with nc.sbuf_tensor("split_h", [P, 4096], F32R) as split_h:
            pass
        region_h = sb("region_h", [P, 8192])
        region_qk = sb("region_qk", [P, 4096])
        region_v = sb("region_v", [P, 2048])
        region_m = sb("region_m", [P, 1280])
        with nc.sbuf_tensor("split_t", [P, 4096], F32R) as split_t:
            pass
        region_t = sb("region_t", [P, 4096])
        ident = sb("ident", [P, P])
        region_c = sb("region_c", [P, KD * 32])
        before = sb("before", [P, P], BF16)
        ones_b = sb("ones_b", [P, P], BF16)
        small = sb("small", [P, 208])

        c_rep = region_c[:, :].rearrange("p (k n) -> p k n", k=KD)
        at_slot = region_c[:, :].rearrange("p (k n) -> p k n", k=2)
        ada = region_x[:, 0:1536].rearrange("p (s n) -> p s n", s=3)
        gain = region_x[:, 1536:3072].rearrange("p (s n) -> p s n", s=3)
        kiT = region_x[:, 3072:3584]
        rope_cos = region_x[:, 3584:3712].rearrange("p (t f) -> p t f", t=NT)
        rope_sin = region_x[:, 3712:3968].rearrange("p (t s f) -> p t s f", t=NT, s=2)
        ones_f = region_x[:, 3968:4096]
        x2 = region_x[:, :].rearrange("p (t d) -> p t d", t=NT)
        x_in_sb = region_y[:, :].rearrange("p (t d) -> p t d", t=NT)
        roped = region_y[:, 0:1024].rearrange("p (b n) -> p b n", b=2)
        rope_tmp = region_y[:, 1024:1536]
        w_gates = region_y[:, 1536:2048].rearrange("p (g c n) -> p g c n", g=2, c=RC)
        mixT = region_y[:, :].rearrange("p (k s) -> p k s", k=KD)
        y_out = region_y[:, 0:2048].rearrange("p (b n) -> p b n", b=RING)
        xgT = region_y[:, 2048:3072].rearrange("p (b k s) -> p b k s", b=2, k=KD)
        hid = region_y[0:CAP, 3072:3584].rearrange("p (b n) -> p b n", b=2)
        silu_g = region_y[0:CAP, 3584:4096].rearrange("p (b n) -> p b n", b=2)
        slot = region_w[:, :].rearrange("p (s n) -> p s n", s=SLOTS)
        split_slot = split_w[:, :].rearrange("p (s k n) -> p s k n", s=SLOTS, k=KD)
        expert_w = region_w[:, :].rearrange("p (b m n) -> p b m n", b=RING, m=3)
        hT = region_h[:, 0:4096].rearrange("p (k s) -> p k s", k=KD)
        h_lo = split_h[:, :].rearrange("p (k s) -> p k s", k=KD)
        h_hi = split_slot[:, H_SLOT, :, :]
        qiT = region_h[:, 4096:6144].rearrange("p (k s) -> p k s", k=4)
        xr = region_h[:, 6144:8192].rearrange("p (c s) -> p c s", c=RC)
        wo_sb = region_h[:, :].rearrange("p (k n) -> p k n", k=KD)
        x_gath = region_h[0:CAP, 0:4096].rearrange("p (b n) -> p b n", b=RING)
        y_back = region_h[:, :].rearrange("p (k t n) -> p k t n", k=2, t=NT)
        qT = region_qk[:, 0:2048].rearrange("p (k s) -> p k s", k=4)
        kT = region_qk[:, 2048:4096].rearrange("p (k s) -> p k s", k=4)
        mod_rows = region_qk[:, :].rearrange("p (m n) -> p m n", m=4)
        GATE1, SHIFT2, SCALE2, GATE2 = range(4)
        v_sb = region_v[:, :].rearrange("p (t n) -> p t n", t=NT)
        h2T = region_v[:, :].rearrange("p (b k s) -> p b k s", b=2, k=KD)
        hidT = region_v[:, 0:256].rearrange("p (b k s) -> p b k s", b=2, k=FC)
        score_at = [0, 128, 384, 768]
        score = [region_m[:, score_at[t]:score_at[t] + P * (t + 1)] for t in range(NT)]
        m_at = [0]

        def in_m(n, dt=F32):
            m_at[0] += n
            v = region_m[:, m_at[0] - n:m_at[0]]
            return v if dt == F32 else v.bitcast(dt)

        w_router = in_m(KD * NL).rearrange("p (k n) -> p k n", k=KD)
        b_router = in_m(NL)
        logit = in_m(NT * NL).rearrange("p (t n) -> p t n", t=NT)
        group8 = in_m(8)
        in_group = in_m(NT * NG).rearrange("p (t n) -> p t n", t=NT)
        choice = [in_m(NT * NE).rearrange("p (t n) -> p t n", t=NT) for _ in range(2)]
        chosen = in_m(NT * NE // 2, BF16).rearrange("p (t n) -> p t n", t=NT)
        iota_e = in_m(NE)
        route_tmp = in_m(NE)
        token_of = in_m(2 * NE).rearrange("p (k n) -> p k n", k=2)
        iota_slot = in_m(2 * CAP)
        table_sb = in_m(NE, I32)
        gather_at = in_m(NE, I32)
        scatter_at = in_m(NE, I32)
        top_e = in_m(NT * 8).rearrange("p (t n) -> p t n", t=NT)
        top_i = in_m(NT * 8, U32).rearrange("p (t n) -> p t n", t=NT)
        gtop_i = in_m(8, U32)
        junk = region_t[:, 1024:2048]
        w_kiwi = region_t[:, 0:576].rearrange("p (k n) -> p k n", k=KD)
        kiwi_lo = split_t[:, 0:576].rearrange("p (k n) -> p k n", k=KD)
        kiwi_hi = split_t[:, 1024:1600].rearrange("p (k n) -> p k n", k=KD)
        ki_rows = region_t[:, 576:832].rearrange("p (b n) -> p b n", b=2)
        ki_tmp = region_t[:, 832:896]
        a_rec = region_t[:, 0:2048].rearrange("p (c s) -> p c s", c=RC)
        conv = region_t[:, 2048:3072].rearrange("p (b s) -> p b s", b=2)
        tanh_r = region_t[:, 3072:3584]
        tanh_i = region_t[:, 3584:4096]
        relu_b = region_t[:, 3072:4096].rearrange("p (b s) -> p b s", b=2)
        gel = region_t[:, 3072:4096].rearrange("p (b s) -> p b s", b=2)
        prob = region_t[:, 0:3072].rearrange("p (b h s) -> p b h s", b=3, h=2)
        probT = region_t[:, 3072:4096].rearrange("p (h s) -> p h s", h=2)
        h2 = region_t[:, :].rearrange("p (t d) -> p t d", t=NT)

        n_small = [0]

        def col(n, dt=F32):
            n_small[0] += n
            v = small[:, n_small[0] - n:n_small[0]]
            return v if dt == F32 else v.bitcast(dt)

        c_col = col(KD)
        ssq = col(NT)
        rstd = col(NT)
        mod1 = col(2 * KD)
        par = col(32)
        sp4 = col(RC)
        sp4n = col(RC)
        spt = col(2 * RC)
        w_idx = col(NT * IH).rearrange("p (t n) -> p t n", t=NT)
        top8 = col(3 * 8).rearrange("p (t n) -> p t n", t=3)
        rmax = col(4)
        nmax = col(4)
        rsum = col(4)
        pssq = col(2)
        gmax = col(1)
        cw = col(2 * NT).rearrange("p (k t) -> p k t", k=2)
        token_v = col(2 * NT, I32)
        slot_i = col(2 * NT, I32)
        token_f = col(2 * NT)
        pos_f = col(2)
        count_f = col(1)
        gidx = col(RING, I32)
        sidx = col(RING, I32)
        gi_f = col(1)
        ei_f = col(2)
        half = col(1)
        most_tokens = col(2, I32)
        assert n_small[0] <= 208 and m_at[0] <= 1280, (n_small, m_at)
        par_rows = region_t[0:32, 3968:4096]

        ps = [ctx.enter_context(nc.psum_tensor(f"ps{i}", [P, 512], F32)) for i in range(8)]

        tile_loaded = [sem(f"tile_loaded{t}") for t in range(NT)]
        c_loaded = sem("c_loaded")
        first_loaded = sem("first_loaded")
        params_loaded = sem("params_loaded")
        ada_params_loaded = sem("ada_params_loaded")
        rope_loaded = sem("rope_loaded")
        kiwi_loaded = sem("kiwi_loaded")
        gates_loaded = sem("gates_loaded")
        slot_loaded = [sem(f"slot_loaded{s}") for s in range(H_SLOT)]
        ada_used = sem("ada_used")
        ada_loaded = [sem(f"ada_loaded{b}") for b in range(2)]
        hi_ready = sem("hi_ready")
        lo_ready = sem("lo_ready")
        lo_odd = sem("lo_odd")
        kiwi_hi_ready = sem("kiwi_hi_ready")
        kiwi_lo_ready = sem("kiwi_lo_ready")
        h_hi_ready = sem("h_hi_ready")
        h_lo_ready = sem("h_lo_ready")
        wo_loaded = sem("wo_loaded")
        router_loaded = sem("router_loaded")
        x_again = sem("x_again")
        setup = sem("setup")
        chain = sem("chain")
        achain = sem("achain")
        pchain = sem("pchain")
        silu_c = sem("silu_c")
        c_ready = sem("c_ready")
        sq_done = sem("sq_done")
        var_ready = sem("var_ready")
        root_ready = sem("root_ready")
        xn_ready = sem("xn_ready")
        par_T = sem("par_T")
        par_sb = sem("par_sb")
        sp_exp = sem("sp_exp")
        xT_done = sem("xT_done")
        xT_even = sem("xT_even")
        xT_odd = sem("xT_odd")
        ada_ready = sem("ada_ready")
        mod1_T = sem("mod1_T")
        h_ready = sem("h_ready")
        proj_done = sem("proj_done")
        rope_ready = sem("rope_ready")
        ropeT_done = sem("ropeT_done")
        ropeT_out = sem("ropeT_out")
        ki_done = sem("ki_done")
        ki_ready = sem("ki_ready")
        kiT_done = sem("kiT_done")
        kiT_out = sem("kiT_out")
        v_out = sem("v_out")
        dots_done = sem("dots_done")
        relu_done = sem("relu_done")
        score_acc = sem("score_acc")
        xr_done = sem("xr_done")
        xr_out = sem("xr_out")
        conv_ready = sem("conv_ready")
        gate_mm = sem("gate_mm")
        gate_act = sem("gate_act")
        rec_done = sem("rec_done")
        rec_root = sem("rec_root")
        rec_b = sem("rec_b")
        xg_done = sem("xg_done")
        xg_sq = sem("xg_sq")
        xg_cubic = sem("xg_cubic")
        xg_tanh = sem("xg_tanh")
        xg_mult = sem("xg_mult")
        mask_ready = sem("mask_ready")
        qk_done = sem("qk_done")
        nmax_ready = sem("nmax_ready")
        exp_done = sem("exp_done")
        prob_ready = sem("prob_ready")
        probT_done = sem("probT_done")
        probT_even = sem("probT_even")
        probT_odd = sem("probT_odd")
        pv_done = sem("pv_done")
        attn_out = sem("attn_out")
        rows_mm = sem("rows_mm")
        rows_out = sem("rows_out")
        mix_done = sem("mix_done")
        mix_sq = sem("mix_sq")
        mix_var = sem("mix_var")
        mix_root = sem("mix_root")
        x2_ready = sem("x2_ready")
        x2_sq = sem("x2_sq")
        x2_var = sem("x2_var")
        x2_root = sem("x2_root")
        h2_ready = sem("h2_ready")
        h2_stored = sem("h2_stored")
        h2T_done = sem("h2T_done")
        h2T_out = sem("h2T_out")
        logit_mm = sem("logit_mm")
        logit_ready = sem("logit_ready")
        route_exp = sem("route_exp")
        chosen_ready = sem("chosen_ready")
        pos_mm = sem("pos_mm")
        slots_ready = sem("slots_ready")
        table_clear = sem("table_clear")
        table_set = sem("table_set")
        table_mm = sem("table_mm")
        count_mm = sem("count_mm")
        gath_idx = sem("gath_idx")
        scat_idx = sem("scat_idx")
        gidx_ready = sem("gidx_ready")
        sidx_ready = sem("sidx_ready")
        gathered = [sem(f"gathered{j}") for j in range(RING)]
        expert_loaded = [sem(f"expert_loaded{j}") for j in range(RING)]
        xgT_done = sem("xgT_done")
        xgT_out = sem("xgT_out")
        gu_done = sem("gu_done")
        silu_done = sem("silu_done")
        hid_ready = sem("hid_ready")
        hidT_done = sem("hidT_done")
        hidT_out = sem("hidT_out")
        down_done = sem("down_done")
        y_ready = sem("y_ready")
        scattered = [sem(f"scattered{j}") for j in range(RING)]
        all_scattered = sem("all_scattered")
        fin_scaled = sem("fin_scaled")
        fin_sum = sem("fin_sum")
        fin_sq = sem("fin_sq")
        fin_var = sem("fin_var")
        fin_root = sem("fin_root")
        fin_out = sem("fin_out")
        stored = sem("stored")
        count_ready = sem("count_ready")
        passed = sem("passed")
        more_turn = sem("more_turn")
        more_loaded = sem("more_loaded")
        more_table = sem("more_table")
        more_idx = sem("more_idx")
        more_gathered = sem("more_gathered")
        more_xT = sem("more_xT")
        more_xT_out = sem("more_xT_out")
        more_gu = sem("more_gu")
        more_silu = sem("more_silu")
        more_hid = sem("more_hid")
        more_hidT = sem("more_hidT")
        more_hidT_out = sem("more_hidT_out")
        more_down = sem("more_down")
        more_y = sem("more_y")
        more_scattered = sem("more_scattered")

        QI, Q, K, V, XR, XG = range(6)
        W_COL = (3 * DA, 0, DA, 2 * DA, KI + ID + IH, KI + ID + IH + R)
        LO_SLOT = (4, 0, 1, 4, 1, 4)
        HI_SLOT = (2, 3, 2, 3, 2, 3)
        LO_USE = (1, 2, 2, 2, 3, 3)
        PIECES = (8, 2, 2, 2, 2, 2)
        ADA_SLOT = slot[:, 0, :].rearrange("p (b n) -> p b n", b=2)
        NADA = 2 * KD

        def piece(w, i):
            n = KD // PIECES[w]
            return slice(i * n, (i + 1) * n), sum(PIECES[:w]) + i + 1

        def halves(w):
            return split_slot[:, HI_SLOT[w]], split_slot[:, LO_SLOT[w]]

        def raw(w):
            return slot[:, LO_SLOT[w], :].rearrange("p (k n) -> p k n", k=KD)

        def split_hi(act, w, i):
            if i == 0:
                act.wait_ge(slot_loaded[LO_SLOT[w]], 16 * LO_USE[w])
                if w >= 2:
                    wait_used(act, w - 2)
                elif w == QI:
                    act.wait_ge(ada_used, 4)
                else:
                    act.wait_ge(ada_used, 4)
            k, _ = piece(w, i)
            act.activation(halves(w)[0][:, k, :], raw(w)[:, k, :], ACT.Copy).then_inc(hi_ready, 1)

        def split_lo(eng, w, i, done):
            k, n = piece(w, i)
            hi, lo = halves(w)
            eng.wait_ge(hi_ready, n)
            eng.tensor_tensor(lo[:, k, :], raw(w)[:, k, :], hi[:, k, :], ALU.subtract).then_inc(done, 1)

        def wait_lo(pe, w):
            if w == QI:
                pe.wait_ge(lo_odd, KD // 2)
            pe.wait_ge(lo_ready, KD // 2 + 2 * w)

        def wait_used(eng, w):
            if w < XR:
                eng.wait_ge(proj_done, NT * (w + 1))
            else:
                eng.wait_ge(xr_done if w == XR else xg_done, RC)

        UNITS = [(w, t) for w in (QI, Q, K, V) for t in range(NT)]
        NROPE = 3 * NT
        XG_BANK = (2, 3, 0, 1)
        PAIRS = [(t, hp) for t in range(NT) for hp in range(H // 2)]

        def load_expert(eng, e, j):
            for m, (w, k) in enumerate(((w_gate, KD), (w_up, KD), (w_down, FC))):
                src = w[bass.ds(e, 1)].rearrange("e p k n -> p (e k) n")
                eng.dma_start(expert_w[:, j, m, :].rearrange("p (k n) -> p k n", k=k), src).then_inc(expert_loaded[j], 16)

        def attn_copy(act, t):
            act.wait_ge(pv_done, 4 * (t + 1))
            act.activation(mixT[:, 0:4, t * P:(t + 1) * P], ps[6 + t % 2][:].rearrange("p (k s) -> p k s", k=4),
                           ACT.Copy).then_inc(attn_out, 1)

        def apart(eng):
            eng.sem_inc(passed, 1)

        def more_rounds(eng, body):
            eng.wait_ge(count_ready, 1)
            most = eng.value_load(most_tokens[0:1, 0:1], min_val=0, max_val=S)
            with eng.If(most > CAP):
                with eng.Fori(1, S // CAP) as r:
                    with eng.Fori(0, NE) as e:
                        body(r, e, r * NE + e - (NE - 1))

        block = ctx.enter_context(nc.Block())

        @block.sync
        def _(sp):
            for t in range(NT):
                sp.dma_start(x_in_sb[:, t, :], x_rows[t]).then_inc(tile_loaded[t], 16)

            b_quad = a["b_ada"][0].rearrange("(q n) -> q n", n=512)

            def load_bias(s, done):
                for r in range(4):
                    sp.dma_start(ada[32 * r:32 * r + 32, s, :], b_quad[4 * s + r].partition_broadcast(32)).then_inc(done, 16)

            def load_gain(name, s, half, done):
                g = a[name][0].rearrange("(q n) -> q n", n=512)
                for q in range(2):
                    r = 2 * half + q
                    sp.dma_start(gain[32 * r:32 * r + 32, s, :], g[q].partition_broadcast(32)).then_inc(done, 16)

            def load_weight(w):
                sp.dma_start(raw(w), w_in[:, :, W_COL[w]:W_COL[w] + 512]).then_inc(slot_loaded[LO_SLOT[w]], 16)

            def load_ada(q):
                if q >= 2:
                    sp.wait_ge(ada_used, 4 + q - 1)
                third = 1 + q // KD
                sp.dma_start(ADA_SLOT[:, q % 2, :], w_ada[:, q % KD, 2048 * third:2048 * (third + 1)]).then_inc(ada_loaded[q % 2], 16)

            for j in range(4):
                sp.dma_start(slot[:, j, :].rearrange("p (k n) -> p k n", k=2), w_ada[:, 2 * j:2 * j + 2, 0:2048]).then_inc(slot_loaded[j], 16)
            load_bias(0, first_loaded)
            load_gain("g_pre_mix", 0, 1, first_loaded)
            load_weight(QI)
            sp.dma_start(rope_cos, a["rope_cos"].rearrange("(t p) f -> p t f", p=P)).then_inc(rope_loaded, 16)
            sp.dma_start(rope_sin, a["rope_sin"].rearrange("(t p) s f -> p t s f", p=P)).then_inc(rope_loaded, 16)
            for name, r0, nr in (("conv_w", 0, 16), ("conv_b", 16, 4), ("b_rg_a", 20, 4), ("b_rg_x", 24, 4), ("lru_lambda", 28, 4)):
                src = a[name][0]
                src = src.rearrange("w (c p) -> (w c) p", p=P) if name == "conv_w" else src.rearrange("(c p) -> c p", p=P)
                sp.dma_start(par_rows[r0:r0 + nr, :], src).then_inc(params_loaded, 16)
            sp.dma_start(w_kiwi, w_in[:, :, KI:KI + ID + IH]).then_inc(kiwi_loaded, 16)
            sp.wait_ge(ada_used, 2)
            load_weight(Q)
            load_weight(K)
            sp.wait_ge(xT_done, KD)
            for g, name in enumerate(("w_rg_a", "w_rg_x")):
                for half in range(2):
                    w = a[name][0].rearrange("(c b) i j -> b i c j", b=2)[half]
                    sp.dma_start(w_gates[64 * half:64 * half + 64, g], w).then_inc(gates_loaded, 16)
            for s in (1, 2):
                load_bias(s, ada_params_loaded)
            for name, s, half in (("g_post_mix", 1, 0), ("g_pre_ffn", 2, 0), ("g_post_ffn", 2, 1)):
                load_gain(name, s, half, ada_params_loaded)
            wait_used(sp, QI)
            load_weight(V)
            wait_used(sp, Q)
            for q in range(NADA):
                if q == 5:
                    wait_used(sp, K)
                    load_weight(XR)
                if q == 9:
                    wait_used(sp, V)
                    load_weight(XG)
                load_ada(q)
            wait_used(sp, XG)
            sp.wait_ge(dots_done, 8 * (NT - 1))
            sp.wait_ge(rec_b, 1)
            sp.dma_start(wo_sb, w_out).then_inc(wo_loaded, 16)
            sp.wait_ge(ada_used, 4 + NADA)
            for j in range(RING):
                load_expert(sp, j, j)
            sp.wait_ge(rows_out, 8)
            for t in range(NT):
                sp.dma_start(x2[:, t, :], x_rows[t]).then_inc(x_again, 16)
            sp.wait_ge(qk_done, len(PAIRS))
            sp.wait_ge(nmax_ready, len(PAIRS))
            sp.dma_start(w_router[:, :, 0:NG], a["w_router_group"][0].rearrange("(k p) n -> p k n", p=P)).then_inc(router_loaded, 16)
            sp.dma_start(w_router[:, :, NG:NL], a["w_router_expert"][0].rearrange("(k p) n -> p k n", p=P)).then_inc(router_loaded, 16)
            sp.dma_start(b_router[:, 0:NG], a["b_router_group"][0].partition_broadcast(P)).then_inc(router_loaded, 16)
            sp.dma_start(b_router[:, NG:NL], a["b_router_expert"][0].partition_broadcast(P)).then_inc(router_loaded, 16)
            for t in range(NT):
                sp.wait_ge(h2_ready, t + 1)
                sp.dma_start(h2_dram[t * P:(t + 1) * P, :], h2[:, t, :]).then_inc(h2_stored, 16)
            with sp.Fori(0, NE // RING - 1) as i:
                for j in range(RING):
                    sp.wait_ge(down_done, i * RING + (j + 1))
                    load_expert(sp, i * RING + (j + RING), j)
            def more(r, e, m):
                sp.wait_ge(more_turn, m)
                for k, (w, kc) in enumerate(((w_gate, KD), (w_up, KD), (w_down, FC))):
                    src = w[bass.ds(e, 1)].rearrange("e p k n -> p (e k) n")
                    sp.dma_start(expert_w[:, 0, k, :].rearrange("p (k n) -> p k n", k=kc), src).then_inc(more_loaded, 16)
                for n in range(2):
                    sp.dma_start(table_sb[CAP * n:CAP * n + CAP, :], table_rows[bass.ds(r * CAP, CAP), :]).then_inc(more_loaded, 16)

            sp.wait_ge(table_set, 16 * 2 * NT)
            more_rounds(sp, more)
            sp.wait_ge(all_scattered, 1)
            for t in range(NT):
                for k in range(2):
                    src = y_dram[2 * (k * S + t * P):2 * (k * S + t * P + P), :].rearrange("(p two) n -> p (two n)", two=2)
                    sp.dma_start(y_back[:, k, t, :], src).then_inc(tile_loaded[t], 16)
            for t in range(NT):
                sp.wait_ge(fin_out, t + 1)
                sp.dma_start(out_rows[t], y_back[:, 0, t, :]).then_inc(stored, 16)
            sp.wait_ge(stored, 16 * NT)

        @block.gpsimd
        def _(pool):
            pool.memset(ident[:], 0.0).then_inc(pchain, 1)
            pool.memset(before[:], 0.0).then_inc(pchain, 1)
            pool.wait_ge(pchain, 2)
            pool.affine_select(out=ident[:], in_=ident[:], compare_op=ALU.not_equal, fill=1.0, base=0,
                               pattern=[[-1, P]], channel_multiplier=1).then_inc(setup, 1)
            pool.affine_select(out=before[:], in_=before[:], compare_op=ALU.is_ge, fill=1.0, base=0,
                               pattern=[[-1, P]], channel_multiplier=1).then_inc(setup, 1)
            pool.memset(ones_b[:], 1.0).then_inc(setup, 1)
            pool.iota(token_v[:, :], pattern=[[P, NT], [S, 2]], base=0, channel_multiplier=1).then_inc(setup, 1)
            pool.iota(token_f, pattern=[[S, 2], [P, NT]], base=-2 * S, channel_multiplier=1,
                      allow_small_or_imprecise_dtypes=True).then_inc(setup, 1)
            clear = region_v[:, 0:P].bitcast(I32)
            pool.iota(clear, pattern=[[0, P]], base=2 * S, channel_multiplier=0).then_inc(pchain, 1)
            pool.wait_ge(pchain, 3)
            pool.dma_start(table_dram.rearrange("(p n) one -> p (n one)", p=P), clear).then_inc(table_clear, 16)
            for w in range(6):
                for i in range(PIECES[w]):
                    if w == QI and i % 2 == 1:
                        continue
                    split_lo(pool, w, i, lo_ready)
                if w == QI:
                    pool.wait_ge(kiwi_hi_ready, 1)
                    pool.tensor_tensor(kiwi_lo, w_kiwi, kiwi_hi, ALU.subtract).then_inc(kiwi_lo_ready, 1)
            pool.wait_ge(nmax_ready, len(PAIRS))
            pool.iota(iota_e, pattern=[[1, NE]], base=0, channel_multiplier=0,
                      allow_small_or_imprecise_dtypes=True).then_inc(setup, 1)
            pool.iota(iota_slot, pattern=[[0, 2], [1, CAP]], base=0, channel_multiplier=0,
                      allow_small_or_imprecise_dtypes=True).then_inc(setup, 1)
            pool.wait_ge(h2_stored, 16 * NT)
            pool.wait_ge(gath_idx, 1)

            def gather(e, j):
                pool.tensor_copy(gidx[0:CAP, j:j + 1], gather_at[0:CAP, bass.ds(e, 1)]).then_inc(gidx_ready, 1)
                pool.wait_ge(gidx_ready, e + 1)
                apart(pool)
                pool.indirect_dma_start(out=x_gath[:, j, :], out_offset=None, in_=h2_dram,
                                        in_offset=bass.IndirectOffsetOnAxis(ap=gidx[0:CAP, j:j + 1], axis=0)).then_inc(gathered[j], 16)

            def scatter(e, j, turn):
                if not (isinstance(turn, int) and turn == 0):
                    pool.wait_ge(scattered[j], turn * 16)
                pool.tensor_copy(sidx[:, j:j + 1], scatter_at[:, bass.ds(e, 1)]).then_inc(sidx_ready, 1)
                pool.wait_ge(sidx_ready, e + 1)
                pool.wait_ge(y_ready, e + 1)
                apart(pool)
                pool.indirect_dma_start(out=y_dram, out_offset=bass.IndirectOffsetOnAxis(ap=sidx[:, j:j + 1], axis=0),
                                        in_=y_out[:, j, :], in_offset=None, bounds_check=4 * S - 1,
                                        oob_is_err=False).then_inc(scattered[j], 16)

            def pool_turn(i):
                for j in range(RING):
                    pool.wait_ge(xgT_done, i * RING + (j + 1))
                    apart(pool)
                    gather(i * RING + (j + RING), j)
                    scatter(i * RING + j, j, i)

            for j in range(RING):
                gather(j, j)
            pool.wait_ge(table_clear, 16)
            pool.wait_ge(slots_ready, NT)
            for n in range(2 * NT):
                pool.indirect_dma_start(out=table_dram, out_offset=bass.IndirectOffsetOnAxis(ap=slot_i[:, n:n + 1], axis=0),
                                        in_=token_v[:, n:n + 1], in_offset=None).then_inc(table_set, 16)
            pool.wait_ge(scat_idx, 1)
            pool_turn(0)
            with pool.Fori(1, NE // RING - 1) as i:
                pool_turn(i)
            for j in range(RING):
                scatter(NE - RING + j, j, NE // RING - 1)
            for j in range(RING):
                pool.wait_ge(scattered[j], NE // RING * 16)

            def more(r, e, m):
                pool.wait_ge(more_table, m * 2)
                pool.tensor_copy(gidx[0:CAP, 0:1], gather_at[0:CAP, bass.ds(e, 1)]).then_inc(more_idx, 1)
                pool.tensor_copy(sidx[:, 0:1], scatter_at[:, bass.ds(e, 1)]).then_inc(more_idx, 1)
                pool.wait_ge(more_idx, m * 2)
                apart(pool)
                pool.indirect_dma_start(out=x_gath[:, 0, :], out_offset=None, in_=h2_dram,
                                        in_offset=bass.IndirectOffsetOnAxis(ap=gidx[0:CAP, 0:1], axis=0)).then_inc(more_gathered, 16)
                pool.wait_ge(more_y, m)
                apart(pool)
                pool.indirect_dma_start(out=y_dram, out_offset=bass.IndirectOffsetOnAxis(ap=sidx[:, 0:1], axis=0),
                                        in_=y_out[:, 0, :], in_offset=None, bounds_check=4 * S - 1,
                                        oob_is_err=False).then_inc(more_scattered, 16)
                pool.wait_ge(more_scattered, m * 16)
                pool.sem_inc(more_turn, 1)

            pool.sem_inc(more_turn, 1)
            more_rounds(pool, more)
            pool.engine_nop().then_inc(all_scattered, 1)

        @block.tensor
        def _(pe):
            pe.wait_ge(setup, 1)
            for t in range(NT):
                pe.wait_ge(xn_ready, t + 1)
            for k in range(KD):
                for t in range(NT):
                    last = pe.transpose(ps[k][:, t * P:(t + 1) * P], x_in_sb[:, t, k * P:(k + 1) * P], ident[:])
                last.then_inc(xT_done, 1)

            def ada_chunk(k, w, bank):
                for r in range(4):
                    last = pe.matmul(ps[bank][32 * r:32 * r + 32, :], c_rep[:, k, :], w[:, 512 * r:512 * (r + 1)],
                                     start=(k == 0), stop=(k == KD - 1))
                return last

            def ada_later(q):
                pe.wait_ge(ada_loaded[q % 2], 16 * (q // 2 + 1))
                if q == 0:
                    pe.wait_ge(relu_done, IH * (NT - 1))
                ada_chunk(q % KD, ADA_SLOT[:, q % 2, :], 7 - q // KD).then_inc(ada_used, 1)

            pe.wait_ge(c_ready, 1)
            pe.wait_ge(xT_even, 1)
            pe.wait_ge(xT_odd, 1)
            for j in range(4):
                pe.wait_ge(slot_loaded[j], 16)
                for k in (2 * j, 2 * j + 1):
                    last = ada_chunk(k, slot[:, j, 2048 * (k % 2):2048 * (k % 2 + 1)], 0)
                last.then_inc(ada_used, 1)
            pe.wait_ge(ada_ready, 1)
            for j in range(4):
                last = pe.transpose(ps[1][:, j * P:(j + 1) * P], ada[:, 0, j * P:(j + 1) * P], ident[:])
            last.then_inc(mod1_T, 1)

            def rope_T(u):
                pe.wait_ge(rope_ready, u + 1)
                if u >= 2:
                    pe.wait_ge(ropeT_out, u - 1)
                else:
                    pe.wait_ge(xT_even, KD // 2)
                    pe.wait_ge(xT_odd, KD // 2)
                for j in range(4):
                    last = pe.transpose(ps[2 + u % 2][:, j * P:(j + 1) * P], roped[:, u % 2, j * P:(j + 1) * P], ident[:])
                last.then_inc(ropeT_done, 1)

            def ki_T(t):
                pe.wait_ge(ki_ready, t + 1)
                pe.transpose(ps[5][:, t * P:(t + 1) * P], ki_rows[:, t % 2, :], ident[:]).then_inc(kiT_done, 1)

            def index_dots(t):
                for h in range(IH):
                    n = (t - 1) * IH + h
                    if n >= 2:
                        pe.wait_ge(relu_done, n - 1)
                    hp = 64 * (h % 2)
                    pe.matmul(ps[6 + h % 2][:, 0:P * (t + 1)], qiT[hp:hp + 64, h // 2, t * P:(t + 1) * P],
                              kiT[hp:hp + 64, 0:P * (t + 1)], start=True, stop=True).then_inc(dots_done, 1)

            for u, (w, t) in enumerate(UNITS):
                if u < 2:
                    pe.wait_ge(mod1_T, 1)
                elif u - 2 < NROPE:
                    pe.wait_ge(rope_ready, u - 1)
                else:
                    pe.wait_ge(v_out, u - 1 - NROPE)
                w_hi, w_lo = halves(w)
                rows = slice(t * P, (t + 1) * P)
                if u < 2:
                    pe.wait_ge(h_hi_ready, u + 1)
                for k in range(KD):
                    if t == 0 and (w == QI or k == 0):
                        pe.wait_ge(hi_ready, piece(w, k)[1] if w == QI else piece(w, PIECES[w] - 1)[1])
                    pe.matmul(ps[u % 2][:], h_hi[:, k, rows], w_hi[:, k, :], start=(k == 0), stop=False)
                if u < 2:
                    pe.wait_ge(h_lo_ready, u + 1)
                for k in range(KD):
                    pe.matmul(ps[u % 2][:], h_lo[:, k, rows], w_hi[:, k, :], start=False, stop=False)
                if t == 0:
                    wait_lo(pe, w)
                for k in range(KD):
                    last = pe.matmul(ps[u % 2][:], h_hi[:, k, rows], w_lo[:, k, :], start=False, stop=(k == KD - 1))
                last.then_inc(proj_done, 1)
                if u == 0:
                    pe.wait_ge(params_loaded, 16 * 5)
                    pe.transpose(ps[7][:, 0:32], par_rows, ident[0:32, 0:32]).then_inc(par_T, 1)
                if w == QI:
                    pe.wait_ge(kiwi_hi_ready, 1)
                    pe.wait_ge(kiwi_lo_ready, 1)
                    if t >= 2:
                        pe.wait_ge(ki_ready, t - 1)
                    for m, (left, right) in enumerate(((h_hi, kiwi_hi), (h_lo, kiwi_hi), (h_hi, kiwi_lo))):
                        for k in range(KD):
                            last = pe.matmul(ps[4 + 2 * (t % 2)][:, 0:ID + IH], left[:, k, rows], right[:, k, :],
                                             start=(m == 0 and k == 0), stop=(m == 2 and k == KD - 1))
                    last.then_inc(ki_done, 1)
                if 1 <= u <= NROPE:
                    rope_T(u - 1)
                if 1 <= u <= NT:
                    ki_T(u - 1)
                if u in (5, 6, 7):
                    if u == 5:
                        pe.wait_ge(ropeT_out, NT)
                        pe.wait_ge(kiT_out, 1)
                    index_dots(u - 4)
                if w in (K, V):
                    ada_later(u - 8)

            def proj_T(w, c, bank, done):
                w_hi, w_lo = halves(w)
                if c == 0:
                    pe.wait_ge(hi_ready, piece(w, PIECES[w] - 1)[1])
                for m, (left, right) in enumerate(((w_hi, h_hi), (w_hi, h_lo), (w_lo, h_hi))):
                    if c == 0 and m == 2:
                        wait_lo(pe, w)
                    for k in range(KD):
                        last = pe.matmul(ps[bank][:], left[:, k, c * P:(c + 1) * P], right[:, k, :],
                                         start=(m == 0 and k == 0), stop=(m == 2 and k == KD - 1))
                last.then_inc(done, 1)

            def gates(c):
                pe.wait_ge(conv_ready, c + 1)
                if c >= 1:
                    pe.wait_ge(gate_act, c)
                for g in range(2):
                    for half in range(2):
                        r = slice(64 * half, 64 * half + 64)
                        last = pe.matmul(ps[4 + g][r, :], w_gates[r, g, c, :], conv[r, c % 2, :], start=True, stop=True)
                last.then_inc(gate_mm, 1)

            pe.wait_ge(v_out, NT)
            pe.wait_ge(gates_loaded, 64)
            for c in range(RC):
                if c >= 2:
                    pe.wait_ge(xr_out, c - 1)
                proj_T(XR, c, c % 2, xr_done)
                ada_later(8 + c)
                if c >= 1:
                    gates(c - 1)
            pe.wait_ge(ropeT_out, NROPE)
            for c in range(RC):
                if c == 2:
                    pe.wait_ge(xr_out, RC)
                proj_T(XG, c, XG_BANK[c], xg_done)
                ada_later(12 + c)
                if c == 0:
                    gates(RC - 1)

            def scores_mm(i):
                t, hp = PAIRS[i]
                if i == 0:
                    pe.wait_ge(xg_mult, RC)
                if i >= 2:
                    pe.wait_ge(nmax_ready, i - 1)
                for hh in range(2):
                    r = slice(64 * hh, 64 * hh + 64)
                    last = pe.matmul(ps[2 * (i % 2) + hh][:, 0:P * (t + 1)], qT[r, hp, t * P:(t + 1) * P],
                                     kT[r, hp, 0:P * (t + 1)], start=True, stop=True)
                last.then_inc(qk_done, 1)

            def prob_T(i):
                t, hp = PAIRS[i]
                pe.wait_ge(prob_ready, i + 1)
                if i >= 1:
                    pe.wait_ge(probT_even, i)
                    pe.wait_ge(probT_odd, i)
                for hh in range(2):
                    for kc in range(t + 1):
                        last = pe.transpose(ps[4 + hh][:, kc * P:(kc + 1) * P], prob[:, i % 3, hh, kc * P:(kc + 1) * P], ident[:])
                last.then_inc(probT_done, 1)

            def values_mm(i):
                t, hp = PAIRS[i]
                pe.wait_ge(probT_even, i + 1)
                pe.wait_ge(probT_odd, i + 1)
                if i == 0:
                    pe.wait_ge(ada_ready, 3)
                if hp == 0 and t >= 2:
                    pe.wait_ge(attn_out, t - 1)
                for kc in range(t + 1):
                    for hh in range(2):
                        h = 2 * hp + hh
                        last = pe.matmul(ps[6 + t % 2][64 * hh:64 * hh + 64, hp * P:(hp + 1) * P], v_sb[:, kc, h * HD:(h + 1) * HD],
                                         probT[:, hh, kc * P:(kc + 1) * P], start=(kc == 0), stop=(kc == t))
                last.then_inc(pv_done, 1)

            for i in range(len(PAIRS) + 3):
                if i < len(PAIRS):
                    scores_mm(i)
                if 2 <= i < len(PAIRS) + 2:
                    prob_T(i - 2)
                if i >= 3:
                    values_mm(i - 3)

            pe.wait_ge(nmax_ready, len(PAIRS))
            for s in range(2):
                for r in range(4):
                    if s == 1:
                        pe.wait_ge(rows_out, r + 1)
                    pe.matmul(ps[r][:], ones_f[32 * r:32 * r + 1, :], ada[32 * r:32 * r + 1, 1 + s, :],
                              start=True, stop=True).then_inc(rows_mm, 1)

            def tokens_T(t):
                pe.wait_ge(h2_ready, t + 1)
                if t >= 1:
                    pe.wait_ge(h2T_out, t)
                for k in range(KD):
                    last = pe.transpose(ps[4 + k // 4][:, (k % 4) * P:(k % 4 + 1) * P], h2[:, t, k * P:(k + 1) * P], ident[:])
                last.then_inc(h2T_done, 1)

            def router(t):
                pe.wait_ge(h2T_out, t + 1)
                if t == 0:
                    pe.wait_ge(router_loaded, 64)
                    pe.wait_ge(attn_out, NT)
                else:
                    pe.wait_ge(slots_ready, t)
                for k in range(KD):
                    last = pe.matmul(ps[6][:, 0:NL], h2T[:, t % 2, k, :], w_router[:, k, :],
                                     start=(k == 0), stop=(k == KD - 1))
                last.then_inc(logit_mm, 1)

            def positions(t):
                pe.wait_ge(chosen_ready, t + 1)
                for s in range(t + 1):
                    last = pe.matmul(ps[6][:, 0:NE], before[:] if s == t else ones_b[:], chosen[:, s, :],
                                     start=(s == 0), stop=(s == t))
                last.then_inc(pos_mm, 1)

            def to_table(t):
                pe.wait_ge(slots_ready, t + 1)
                for k in range(2):
                    last = pe.matmul(ps[7][:, 0:NE], at_slot[:, k, :], token_of[:, k, :],
                                     start=(t == 0 and k == 0), stop=(t == NT - 1 and k == 1))
                last.then_inc(table_mm, 1)

            pe.wait_ge(wo_loaded, 16)
            pe.wait_ge(attn_out, NT)
            pe.wait_ge(rows_out, 8)
            for t in range(NT):
                if t >= 2:
                    pe.wait_ge(x2_ready, t - 1)
                for n in range(2):
                    for k in range(KD):
                        if t >= 1 and n == 1 and k == 4:
                            if t >= 2:
                                to_table(t - 2)
                            tokens_T(t - 1)
                        if t >= 1 and n == 1 and k == 6:
                            router(t - 1)
                        last = pe.matmul(ps[2 * (t % 2) + n][:], mixT[:, k, t * P:(t + 1) * P], wo_sb[:, k, 512 * n:512 * (n + 1)],
                                         start=(k == 0), stop=(k == KD - 1))
                last.then_inc(mix_done, 1)
                if t >= 1:
                    positions(t - 1)
            to_table(NT - 2)
            tokens_T(NT - 1)
            router(NT - 1)
            positions(NT - 1)
            to_table(NT - 1)
            for t in range(NT):
                last = pe.matmul(ps[6][:, 0:NE], ones_b[:], chosen[:, t, :], start=(t == 0), stop=(t == NT - 1))
            last.then_inc(count_mm, 1)

            def rows_T(e, j, turn):
                pe.wait_ge(gathered[j], turn * 16 + 16)
                if not (isinstance(e, int) and e < 2):
                    pe.wait_ge(xgT_out, e - 1)
                apart(pe)
                for k in range(KD):
                    last = pe.transpose(ps[j % 2][:, k * CAP:(k + 1) * CAP], x_gath[:, j, k:D:KD], ident[0:CAP, 0:CAP])
                last.then_inc(xgT_done, 1)

            def gate_up(e, j, turn):
                pe.wait_ge(expert_loaded[j], turn * 48 + 48)
                pe.wait_ge(xgT_out, e + 1)
                if not (isinstance(e, int) and e < 2):
                    pe.wait_ge(hid_ready, e - 1)
                for k in range(KD):
                    for m in range(2):
                        last = pe.matmul(ps[2 + j % 2][CAP * m:CAP * m + CAP, 0:FE], xgT[:, j % 2, k, :],
                                         expert_w[:, j, m, k * FE:(k + 1) * FE], start=(k == 0), stop=(k == KD - 1))
                last.then_inc(gu_done, 1)

            def hidden_T(e, j):
                pe.wait_ge(hid_ready, e + 1)
                apart(pe)
                for k in range(FC):
                    last = pe.transpose(ps[4 + j % 2][:, k * CAP:(k + 1) * CAP], hid[:, j % 2, k:FE:FC], ident[0:CAP, 0:CAP])
                last.then_inc(hidT_done, 1)

            def down(e, j):
                pe.wait_ge(hidT_out, e + 1)
                if not (isinstance(e, int) and e < 2):
                    pe.wait_ge(y_ready, e - 1)
                for k in range(FC):
                    for n in range(2):
                        last = pe.matmul(ps[6 + j % 2][CAP * n:CAP * n + CAP, :], hidT[:, j % 2, k, :],
                                         expert_w[:, j, 2, k * D + 512 * n:k * D + 512 * (n + 1)],
                                         start=(k == 0), stop=(k == FC - 1))
                last.then_inc(down_done, 1)

            def turn_of(i, n):
                return i + n // RING

            def step(i, n):
                e, j = i * RING + n, n % RING
                gate_up(e, j, turn_of(i, n))
                hidden_T(i * RING + (n - 1), (n - 1) % RING)
                rows_T(i * RING + (n + 1), (n + 1) % RING, turn_of(i, n + 1))
                down(i * RING + (n - 1), (n - 1) % RING)

            rows_T(0, 0, 0)
            gate_up(0, 0, 0)
            rows_T(1, 1, 0)
            step(0, 1)
            step(0, 2)
            with pe.Fori(0, NE // RING - 1) as i:
                for n in range(3, 3 + RING):
                    step(i, n)
            gate_up(NE - 1, RING - 1, NE // RING - 1)
            hidden_T(NE - 2, RING - 2)
            down(NE - 2, RING - 2)
            hidden_T(NE - 1, RING - 1)
            down(NE - 1, RING - 1)

            def more(r, e, m):
                pe.wait_ge(more_loaded, m * 80)
                pe.wait_ge(more_gathered, m * 16)
                apart(pe)
                for k in range(KD):
                    last = pe.transpose(ps[0][:, k * CAP:(k + 1) * CAP], x_gath[:, 0, k:D:KD], ident[0:CAP, 0:CAP])
                last.then_inc(more_xT, 1)
                pe.wait_ge(more_xT_out, m)
                for k in range(KD):
                    for g in range(2):
                        last = pe.matmul(ps[2][CAP * g:CAP * g + CAP, 0:FE], xgT[:, 0, k, :],
                                         expert_w[:, 0, g, k * FE:(k + 1) * FE], start=(k == 0), stop=(k == KD - 1))
                last.then_inc(more_gu, 1)
                pe.wait_ge(more_hid, m)
                apart(pe)
                for k in range(FC):
                    last = pe.transpose(ps[4][:, k * CAP:(k + 1) * CAP], hid[:, 0, k:FE:FC], ident[0:CAP, 0:CAP])
                last.then_inc(more_hidT, 1)
                pe.wait_ge(more_hidT_out, m)
                for k in range(FC):
                    for n in range(2):
                        last = pe.matmul(ps[6][CAP * n:CAP * n + CAP, :], hidT[:, 0, k, :],
                                         expert_w[:, 0, 2, k * D + 512 * n:k * D + 512 * (n + 1)],
                                         start=(k == 0), stop=(k == FC - 1))
                last.then_inc(more_down, 1)

            more_rounds(pe, more)

        @block.scalar
        def _(act):
            n = [0]

            def link(ins):
                n[0] += 1
                ins.then_inc(achain, 1)
                act.wait_ge(achain, n[0])

            act.dma_start(c_col, a["c"][0].rearrange("(p k) -> p k", k=KD)).then_inc(c_loaded, 16)
            act.wait_ge(c_loaded, 16)
            act.activation(c_col, c_col, ACT.Silu).then_inc(silu_c, 1)
            for t in range(NT):
                act.wait_ge(tile_loaded[t], 16)
                if t >= 1:
                    act.wait_ge(sq_done, t)
                act.activation(junk, x_in_sb[:, t, :], ACT.Square, accum_out=ssq[:, t:t + 1]).then_inc(sq_done, 1)
            act.wait_ge(var_ready, 1)
            act.activation(rstd, rstd, ACT.Sqrt).then_inc(root_ready, 1)
            for k in range(0, KD, 2):
                act.wait_ge(xT_done, k + 1)
                act.activation(hT[:, k, :], ps[k][:], ACT.Copy).then_inc(xT_even, 1)
            for i in range(3):
                split_hi(act, QI, i)
            act.wait_ge(h_ready, KD)
            act.activation(h_hi[:, :, 0:P], hT[:, :, 0:P], ACT.Copy).then_inc(h_hi_ready, 1)
            for i in range(3, KD):
                split_hi(act, QI, i)
            act.wait_ge(h_ready, 2 * KD)
            act.activation(h_hi[:, :, P:S], hT[:, :, P:S], ACT.Copy).then_inc(h_hi_ready, 1)
            act.wait_ge(kiwi_loaded, 16)
            act.activation(kiwi_hi, w_kiwi, ACT.Copy).then_inc(kiwi_hi_ready, 1)
            act.wait_ge(par_sb, 2)
            act.activation(spt[:, 0:RC], spt[:, 0:RC], ACT.Exp, scale=-1.0).then_inc(sp_exp, 1)

            def unit_out(u):
                dst = {QI: qiT, Q: qT, K: kT}[UNITS[u][0]]
                t = UNITS[u][1]
                act.wait_ge(ropeT_done, u + 1)
                act.activation(dst[:, :, t * P:(t + 1) * P], ps[2 + u % 2][:].rearrange("p (k s) -> p k s", k=4),
                               ACT.Copy).then_inc(ropeT_out, 1)

            def relus(t):
                for h in range(IH):
                    m = (t - 1) * IH + h
                    act.wait_ge(dots_done, m + 1)
                    if m >= 2:
                        act.wait_ge(score_acc, m - 1)
                    act.activation(relu_b[:, m % 2, 0:P * (t + 1)], ps[6 + h % 2][:, 0:P * (t + 1)], ACT.Relu).then_inc(relu_done, 1)

            for u, (w, t) in enumerate(UNITS):
                if w == V:
                    act.wait_ge(proj_done, u + 1)
                    act.wait_ge(table_clear, 16)
                    act.activation(v_sb[:, t, :], ps[u % 2][:], ACT.Copy).then_inc(v_out, 1)
                    if u == NROPE:
                        unit_out(u - 1)
                if 1 <= u < NROPE:
                    unit_out(u - 1)
                if u == NT:
                    act.wait_ge(kiT_done, NT)
                    act.activation(kiT, ps[5][:], ACT.Copy).then_inc(kiT_out, 1)
                if t in (1, 2):
                    split_hi(act, w + 1, t - 1)
                if u in (5, 6, 7):
                    relus(u - 4)

            def gate_acts(c):
                act.wait_ge(gate_mm, c + 1)
                if c >= 1:
                    act.wait_ge(rec_done, c)
                act.activation(tanh_r, ps[4][:], ACT.Tanh, bias=par[:, 20 + c:21 + c], scale=0.5).then_inc(achain, 1)
                act.activation(tanh_i, ps[5][:], ACT.Tanh, bias=par[:, 24 + c:25 + c], scale=0.5).then_inc(achain, 1)
                n[0] += 2
                act.wait_ge(achain, n[0])
                link(act.activation(a_rec[:, c, :], tanh_r, ACT.Exp, bias=sp4n[:, c:c + 1], scale=sp4n[:, c:c + 1]))
                act.activation(tanh_r, tanh_r, ACT.Tanh, bias=sp4[:, c:c + 1], scale=sp4[:, c:c + 1]).then_inc(gate_act, 1)

            act.wait_ge(par_sb, 3)
            for c in range(RC):
                act.wait_ge(xr_done, c + 1)
                act.activation(xr[:, c, :], ps[c % 2][:], ACT.Copy).then_inc(xr_out, 1)
                if c in (1, 2):
                    split_hi(act, XG, c - 1)
                if c >= 1:
                    gate_acts(c - 1)
            gate_acts(RC - 1)
            act.wait_ge(rec_done, RC)
            m_all = xr.rearrange("p c s -> p (c s)")
            act.activation(m_all, m_all, ACT.Sqrt, scale=0.25).then_inc(rec_root, 1)

            def gelu_sq(c):
                act.wait_ge(xg_done, c + 1)
                if c >= 2:
                    act.wait_ge(xg_mult, c - 1)
                act.activation(gel[:, c % 2, :], ps[XG_BANK[c]][:], ACT.Square).then_inc(xg_sq, 1)

            gelu_sq(0)
            for c in range(RC):
                if c + 1 < RC:
                    gelu_sq(c + 1)
                act.wait_ge(xg_cubic, c + 1)
                act.activation(gel[:, c % 2, :], gel[:, c % 2, :], ACT.Tanh, scale=GELU_SCALE).then_inc(xg_tanh, 1)

            def exps(i):
                t, hp = PAIRS[i]
                act.wait_ge(nmax_ready, i + 1)
                if i >= 2:
                    act.wait_ge(prob_ready, i - 1)
                for hh in range(2):
                    p = prob[:, i % 3, hh, 0:P * (t + 1)]
                    q = 2 * (i % 2) + hh
                    act.activation(p, p, ACT.Exp, bias=nmax[:, q:q + 1], scale=HD ** -0.5, accum_out=rsum[:, q:q + 1]).then_inc(exp_done, 1)

            def probT_copy(i):
                t, hp = PAIRS[i]
                act.wait_ge(probT_done, i + 1)
                if i >= 1:
                    act.wait_ge(pv_done, i)
                act.activation(probT[:, 0, 0:P * (t + 1)], ps[4][:, 0:P * (t + 1)], ACT.Copy).then_inc(probT_even, 1)

            for i in range(len(PAIRS) + 2):
                if i < len(PAIRS):
                    exps(i)
                if i >= 2:
                    probT_copy(i - 2)
                if i >= 3 and (i - 3) % 4 == 3:
                    attn_copy(act, (i - 3) // 4)
            attn_copy(act, NT - 1)
            for m in range(8):
                act.wait_ge(rows_mm, m + 1)
                act.activation(mod_rows[:, m // 2, 512 * (m % 2):512 * (m % 2 + 1)], ps[m % 4][:], ACT.Copy).then_inc(rows_out, 1)

            def mix_norm(t):
                act.wait_ge(mix_done, t + 1)
                for m in range(2):
                    if t >= 1 and m == 0:
                        act.wait_ge(mix_var, t)
                    act.activation(h2[:, t, 512 * m:512 * (m + 1)], ps[2 * (t % 2) + m][:], ACT.Square,
                                   accum_out=pssq[:, m:m + 1]).then_inc(mix_sq, 1)
                act.wait_ge(mix_var, t + 1)
                act.activation(rstd[:, t:t + 1], ssq[:, t:t + 1], ACT.Sqrt).then_inc(mix_root, 1)

            def x2_norm(t):
                act.wait_ge(x2_ready, t + 1)
                act.activation(h2[:, t, :], x2[:, t, :], ACT.Square, accum_out=ssq[:, t:t + 1]).then_inc(x2_sq, 1)
                act.wait_ge(x2_var, t + 1)
                act.activation(rstd[:, t:t + 1], ssq[:, t:t + 1], ACT.Sqrt).then_inc(x2_root, 1)

            def h2T_copy(t):
                act.wait_ge(h2T_done, t + 1)
                for m in range(2):
                    last = act.activation(h2T[:, t % 2, 4 * m:4 * m + 4, :].rearrange("p k s -> p (k s)"), ps[4 + m][:], ACT.Copy)
                last.then_inc(h2T_out, 1)

            for t in range(NT):
                mix_norm(t)
                x2_norm(t)
                h2T_copy(t)
            for t in range(NT):
                act.wait_ge(logit_ready, t + 1)
                act.activation(logit[:, t, 0:NG], logit[:, t, 0:NG], ACT.Exp, accum_out=ssq[:, t:t + 1]).then_inc(route_exp, 1)
                act.activation(cw[:, 1, t:t + 1], cw[:, 1, t:t + 1], ACT.Exp).then_inc(route_exp, 1)

            def xgT_copy(e, j):
                act.wait_ge(xgT_done, e + 1)
                if not (isinstance(e, int) and e < 2):
                    act.wait_ge(gu_done, e - 1)
                act.activation(xgT[:, j % 2].rearrange("p k s -> p (k s)"), ps[j % 2][:], ACT.Copy).then_inc(xgT_out, 1)

            def silu(e, j):
                act.wait_ge(gu_done, e + 1)
                if not (isinstance(e, int) and e < 2):
                    act.wait_ge(hid_ready, e - 1)
                act.activation(silu_g[:, j % 2, :], ps[2 + j % 2][0:CAP, 0:FE], ACT.Silu).then_inc(silu_done, 1)

            xgT_copy(0, 0)
            xgT_copy(1, 1)
            silu(0, 0)
            silu(1, 1)
            with act.Fori(0, NE // RING - 1) as i:
                for m in range(2, 2 + RING):
                    xgT_copy(i * RING + m, m % RING)
                    silu(i * RING + m, m % RING)
            for m in range(NE - 2, NE):
                xgT_copy(m, m % RING)
                silu(m, m % RING)

            def more(r, e, m):
                act.wait_ge(more_xT, m)
                act.activation(xgT[:, 0].rearrange("p k s -> p (k s)"), ps[0][:], ACT.Copy).then_inc(more_xT_out, 1)
                act.wait_ge(more_gu, m)
                act.activation(silu_g[:, 0, :], ps[2][0:CAP, 0:FE], ACT.Silu).then_inc(more_silu, 1)

            more_rounds(act, more)

            def scale_first(t):
                act.wait_ge(tile_loaded[t], 48)
                act.activation(y_back[:, 0, t, :], y_back[:, 0, t, :], ACT.Copy, scale=cw[:, 0, t:t + 1]).then_inc(fin_scaled, 1)

            scale_first(0)
            for t in range(NT):
                if t + 1 < NT:
                    scale_first(t + 1)
                act.wait_ge(fin_sum, t + 1)
                act.activation(h2[:, t, :], y_back[:, 0, t, :], ACT.Square, accum_out=ssq[:, t:t + 1]).then_inc(fin_sq, 1)
                act.wait_ge(fin_var, t + 1)
                act.activation(rstd[:, t:t + 1], ssq[:, t:t + 1], ACT.Sqrt).then_inc(fin_root, 1)

        @block.vector
        def _(dve):
            n = [0]

            def link(ins):
                n[0] += 1
                ins.then_inc(chain, 1)
                dve.wait_ge(chain, n[0])

            def tick(ins):
                n[0] += 1
                ins.then_inc(chain, 1)

            def settle():
                dve.wait_ge(chain, n[0])

            tick(dve.memset(gain[0:64, 0, :], 1.0))
            tick(dve.memset(gain[64:P, 1, :], 1.0))
            tick(dve.memset(ones_f, 1.0))
            tick(dve.memset(half[0:CAP, :], 0.0))
            tick(dve.memset(half[CAP:P, :], 1.0))
            tick(dve.memset(score[0], 0.0))
            settle()
            tick(dve.memset(score[0][0:CHUNK, CHUNK:P], MASKED))
            dve.wait_ge(sq_done, NT)
            dve.tensor_scalar(rstd, ssq, 1.0 / D, EPS, ALU.mult, ALU.add).then_inc(var_ready, 1)
            dve.wait_ge(root_ready, 1)
            link(dve.reciprocal(rstd, rstd))
            for t in range(NT):
                dve.tensor_scalar(x_in_sb[:, t, :], x_in_sb[:, t, :], rstd[:, t:t + 1], None, ALU.mult).then_inc(xn_ready, 1)
            dve.wait_ge(silu_c, 1)
            dve.tensor_copy(c_rep, c_col.unsqueeze(2).broadcast_to([P, KD, 32])).then_inc(c_ready, 1)
            for k in range(1, KD, 2):
                dve.wait_ge(xT_done, k + 1)
                dve.tensor_copy(hT[:, k, :], ps[k][:]).then_inc(xT_odd, 1)
            dve.wait_ge(first_loaded, 16 * 6)
            link(dve.tensor_scalar(ada[64:P, 0, :], ada[64:P, 0, :], 1.0, None, ALU.add))

            def ada_rows(s, used, bank):
                dve.wait_ge(ada_used, used)
                link(dve.tensor_tensor(ada[:, s, :], ps[bank][:], ada[:, s, :], ALU.add))
                dve.tensor_tensor(ada[:, s, :], ada[:, s, :], gain[:, s, :], ALU.mult).then_inc(ada_ready, 1)

            ada_rows(0, 4, 0)
            dve.wait_ge(mod1_T, 1)
            link(dve.tensor_copy(mod1.rearrange("p (r j) -> p r j", j=4),
                                 ps[1][:].rearrange("p (j r q) -> p r j q", j=4, q=32)[:, :, :, 0]))
            dve.wait_ge(xT_even, KD // 2)
            dve.wait_ge(xT_odd, KD // 2)
            parts = (slice(0, P), slice(P, S))
            for part in parts:
                for k in range(KD):
                    dve.tensor_scalar(hT[:, k, part], hT[:, k, part], mod1[:, KD + k:KD + k + 1], mod1[:, k:k + 1],
                                      ALU.mult, ALU.add).then_inc(h_ready, 1)
            for m, part in enumerate(parts):
                dve.wait_ge(h_hi_ready, m + 1)
                dve.wait_ge(h_ready, KD * (m + 1))
                dve.tensor_tensor(h_lo[:, :, part], hT[:, :, part], h_hi[:, :, part], ALU.subtract).then_inc(h_lo_ready, 1)
                if m == 0:
                    for i in range(1, KD, 2):
                        split_lo(dve, QI, i, lo_odd)

            def rope(u):
                t = UNITS[u][1]
                dve.wait_ge(proj_done, u + 1)
                if u >= 1:
                    dve.wait_ge(rope_ready, u)
                if u >= 2:
                    dve.wait_ge(ropeT_done, u - 1)
                x = ps[u % 2][:].rearrange("p (h s f) -> p h s f", s=2, f=32)
                o = roped[:, u % 2, :].rearrange("p (h s f) -> p h s f", s=2, f=32)
                o3 = roped[:, u % 2, :].rearrange("p (h f) -> p h f", f=32)
                x3 = ps[u % 2][:].rearrange("p (h f) -> p h f", f=32)
                tmp = rope_tmp.rearrange("p (h s f) -> p h s f", s=2, f=32)
                tick(dve.tensor_tensor(o3, x3, rope_cos[:, t, :].unsqueeze(1).broadcast_to([P, 16, 32]), ALU.mult))
                link(dve.tensor_tensor(tmp, x[:, :, ::-1, :], rope_sin[:, t].unsqueeze(1).broadcast_to([P, 8, 2, 32]), ALU.mult))
                dve.tensor_tensor(roped[:, u % 2, :], roped[:, u % 2, :], rope_tmp, ALU.add).then_inc(rope_ready, 1)

            def rope_ki(t):
                dve.wait_ge(ki_done, t + 1)
                if t >= 1:
                    dve.wait_ge(ki_ready, t)
                if t >= 2:
                    dve.wait_ge(kiT_done, t - 1)
                src = ps[4 + 2 * (t % 2)][:, 0:ID]
                row = ki_rows[:, t % 2, :].rearrange("p (a n) -> p a n", a=2)
                tick(dve.tensor_tensor(row[:, 0, :].rearrange("p (s f) -> p s f", s=2), src.rearrange("p (s f) -> p s f", s=2),
                                       rope_cos[:, t, :].unsqueeze(1).broadcast_to([P, 2, 32]), ALU.mult))
                tick(dve.tensor_tensor(ki_tmp.rearrange("p (s f) -> p s f", s=2), src.rearrange("p (s f) -> p s f", s=2)[:, ::-1, :],
                                       rope_sin[:, t], ALU.mult))
                tick(dve.tensor_scalar(w_idx[:, t, :], ps[4 + 2 * (t % 2)][:, ID:ID + IH], IH ** -0.5 * ID ** -0.5, None, ALU.mult))
                settle()
                link(dve.tensor_tensor(row[:, 0, :], row[:, 0, :], ki_tmp, ALU.add))
                dve.tensor_copy(row[:, 1, :], row[:, 0, :]).then_inc(ki_ready, 1)

            def index_sum(t):
                for h in range(IH):
                    m = (t - 1) * IH + h
                    dve.wait_ge(relu_done, m + 1)
                    r = relu_b[:, m % 2, 0:P * (t + 1)]
                    if h == 0:
                        dve.tensor_scalar(score[t], r, w_idx[:, t, 0:1], None, ALU.mult).then_inc(score_acc, 1)
                    else:
                        dve.wait_ge(score_acc, m)
                        dve.scalar_tensor_tensor(score[t], r, w_idx[:, t, h:h + 1], score[t], ALU.mult, ALU.add).then_inc(score_acc, 1)
                dve.wait_ge(score_acc, t * IH)
                tick(dve.memset(score[t][0:CHUNK, P * t + CHUNK:P * (t + 1)], NOT_ADMISSIBLE))

            def topk_round():
                settle()
                for t in range(1, NT):
                    tick(dve.max(top8[:, t - 1, :], score[t]))
                for t in range(1, NT):
                    dve.wait_ge(chain, n[0] - (NT - 1 - t) - (t - 1))
                    tick(dve.match_replace(score[t], top8[:, t - 1, :], score[t], TAKEN))

            def channel_params():
                dve.wait_ge(par_T, 1)
                dve.tensor_copy(par, ps[7][:, 0:32]).then_inc(par_sb, 1)
                dve.wait_ge(par_sb, 1)
                lam = par[:, 28:32]
                z, q = spt[:, 0:RC], spt[:, RC:2 * RC]
                tick(dve.tensor_scalar(par[:, 20:28], par[:, 20:28], 0.5, None, ALU.mult))
                link(dve.tensor_scalar(q, lam, -1.0, None, ALU.mult))
                dve.tensor_tensor(z, lam, q, ALU.max).then_inc(par_sb, 1)
                dve.wait_ge(sp_exp, 1)
                link(dve.tensor_scalar(q, z, 2.0, None, ALU.add))
                link(dve.reciprocal(q, q))
                link(dve.tensor_tensor(z, z, q, ALU.mult))
                link(dve.tensor_tensor(q, z, z, ALU.mult))
                TERMS = 8
                link(dve.tensor_scalar(sp4, q, 1.0 / (2 * TERMS + 1), 1.0 / (2 * TERMS - 1), ALU.mult, ALU.add))
                for m in range(TERMS - 1, 0, -1):
                    link(dve.tensor_tensor(sp4, sp4, q, ALU.mult))
                    link(dve.tensor_scalar(sp4, sp4, 1.0 / (2 * m - 1), None, ALU.add))
                link(dve.tensor_tensor(sp4, sp4, z, ALU.mult))
                link(dve.tensor_scalar(q, lam, -1.0, 0.0, ALU.mult, ALU.max))
                link(dve.scalar_tensor_tensor(sp4, sp4, 2.0, q, ALU.mult, ALU.add))
                link(dve.tensor_scalar(sp4, sp4, 4.0, None, ALU.mult))
                dve.tensor_scalar(sp4n, sp4, -1.0, None, ALU.mult).then_inc(par_sb, 1)

            dve.wait_ge(rope_loaded, 32)
            for u in range(NROPE):
                rope(u)
                if u < NT:
                    rope_ki(u)
                if u == 0:
                    channel_params()
                if u in (5, 6, 7):
                    index_sum(u - 4)
                if u >= 8:
                    topk_round()
            for _ in range(ROUNDS - 7):
                topk_round()

            def convolve(c):
                dve.wait_ge(xr_out, c + 1)
                if c >= 2:
                    dve.wait_ge(gate_mm, c - 1)
                o = conv[:, c % 2, :]
                tap = lambda j: par[:, RC * j + c:RC * j + c + 1]
                link(dve.tensor_scalar(o, xr[:, c, :], tap(NTAPS - 1), par[:, 16 + c:17 + c], ALU.mult, ALU.add))
                for back in range(1, NTAPS):
                    ins = dve.scalar_tensor_tensor(o[:, back:], xr[:, c, 0:S - back], tap(NTAPS - 1 - back), o[:, back:], ALU.mult, ALU.add)
                    if back < NTAPS - 1:
                        link(ins)
                    else:
                        ins.then_inc(conv_ready, 1)

            def recur_in(c):
                dve.wait_ge(conv_ready, c + 1)
                dve.wait_ge(gate_act, c + 1)
                tick(dve.scalar_tensor_tensor(mixT[:, 4 + c, :], tanh_i, 1.0, conv[:, c % 2, :], ALU.add, ALU.mult))
                link(dve.tensor_tensor(xr[:, c, :], a_rec[:, c, :], a_rec[:, c, :], ALU.mult))
                dve.scalar_tensor_tensor(xr[:, c, :], xr[:, c, :], 1.0, tanh_r, ALU.add, ALU.mult).then_inc(rec_done, 1)

            for c in range(RC):
                convolve(c)
                if c < 3:
                    topk_round()
                if c >= 1:
                    recur_in(c - 1)
            settle()
            for t in range(1, NT):
                dve.tensor_scalar(score[t], score[t], BETWEEN, MASKED, ALU.is_gt, ALU.mult).then_inc(mask_ready, 1)
            recur_in(RC - 1)
            dve.wait_ge(rec_root, 1)
            settle()
            rnn = mixT[:, 4:8, :]
            dve.tensor_tensor(rnn, rnn, xr, ALU.mult).then_inc(rec_b, 1)
            dve.wait_ge(rec_b, 1)
            for c in range(RC):
                tick(dve.tensor_tensor_scan(rnn[:, c, :], a_rec[:, c, :], rnn[:, c, :], 0.0, ALU.mult, ALU.add))

            def gelu_cubic(c):
                g = gel[:, c % 2, :]
                dve.wait_ge(xg_sq, c + 1)
                link(dve.tensor_scalar(g, g, GELU_CUBIC, 1.0, ALU.mult, ALU.add))
                dve.tensor_tensor(g, g, ps[XG_BANK[c]][:], ALU.mult).then_inc(xg_cubic, 1)

            gelu_cubic(0)
            for c in range(RC):
                if c + 1 < RC:
                    gelu_cubic(c + 1)
                g = gel[:, c % 2, :]
                dve.wait_ge(xg_tanh, c + 1)
                link(dve.scalar_tensor_tensor(g, g, 1.0, ps[XG_BANK[c]][:], ALU.add, ALU.mult))
                dve.scalar_tensor_tensor(rnn[:, c, :], g, 0.5, rnn[:, c, :], ALU.mult, ALU.mult).then_inc(xg_mult, 1)

            dve.wait_ge(ada_params_loaded, 16 * 14)
            link(dve.tensor_scalar(ada[0:64, 2, :], ada[0:64, 2, :], 1.0, None, ALU.add))
            ada_rows(1, 4 + KD, 7)
            ada_rows(2, 4 + 2 * KD, 6)

            def masked_max(i):
                t, hp = PAIRS[i]
                dve.wait_ge(qk_done, i + 1)
                if i >= 3:
                    dve.wait_ge(probT_done, i - 2)
                if i >= 2:
                    dve.wait_ge(exp_done, 2 * (i - 1))
                if i == 0:
                    dve.wait_ge(xg_mult, RC)
                for hh in range(2):
                    q = 2 * (i % 2) + hh
                    tick(dve.tensor_tensor_reduce(prob[:, i % 3, hh, 0:P * (t + 1)], ps[2 * (i % 2) + hh][:, 0:P * (t + 1)], score[t],
                                                  1.0, TAKEN, ALU.add, ALU.max, rmax[:, q:q + 1]))
                settle()
                q = 2 * (i % 2)
                dve.tensor_scalar(nmax[:, q:q + 2], rmax[:, q:q + 2], -HD ** -0.5, None, ALU.mult).then_inc(nmax_ready, 1)

            def normalise(i):
                t, hp = PAIRS[i]
                q = 2 * (i % 2)
                dve.wait_ge(exp_done, 2 * i + 2)
                link(dve.reciprocal(rsum[:, q:q + 2], rsum[:, q:q + 2]))
                for hh in range(2):
                    p = prob[:, i % 3, hh, 0:P * (t + 1)]
                    last = dve.tensor_scalar(p, p, rsum[:, q + hh:q + hh + 1], None, ALU.mult)
                last.then_inc(prob_ready, 1)

            def probT_copy(i):
                t, hp = PAIRS[i]
                dve.wait_ge(probT_done, i + 1)
                if i >= 1:
                    dve.wait_ge(pv_done, i)
                dve.tensor_copy(probT[:, 1, 0:P * (t + 1)], ps[5][:, 0:P * (t + 1)]).then_inc(probT_odd, 1)

            dve.wait_ge(mask_ready, NT - 1)
            for i in range(len(PAIRS) + 2):
                if i < len(PAIRS):
                    masked_max(i)
                if 1 <= i <= len(PAIRS):
                    normalise(i - 1)
                if i >= 2:
                    probT_copy(i - 2)

            def post_mix(t):
                one = slice(t, t + 1)
                dve.wait_ge(mix_sq, 2 * t + 2)
                link(dve.tensor_tensor(ssq[:, one], pssq[:, 0:1], pssq[:, 1:2], ALU.add))
                dve.tensor_scalar(ssq[:, one], ssq[:, one], 1.0 / D, EPS, ALU.mult, ALU.add).then_inc(mix_var, 1)
                dve.wait_ge(mix_root, t + 1)
                link(dve.reciprocal(rstd[:, one], rstd[:, one]))
                for m in range(2):
                    w = slice(512 * m, 512 * (m + 1))
                    tick(dve.scalar_tensor_tensor(h2[:, t, w], ps[2 * (t % 2) + m][:], rstd[:, one], mod_rows[:, GATE1, w], ALU.mult, ALU.mult))
                settle()
                dve.wait_ge(x_again, 16 * NT)
                dve.tensor_tensor(x2[:, t, :], x2[:, t, :], h2[:, t, :], ALU.add).then_inc(x2_ready, 1)
                dve.wait_ge(x2_sq, t + 1)
                dve.tensor_scalar(ssq[:, one], ssq[:, one], 1.0 / D, EPS, ALU.mult, ALU.add).then_inc(x2_var, 1)
                dve.wait_ge(x2_root, t + 1)
                link(dve.reciprocal(rstd[:, one], rstd[:, one]))
                link(dve.scalar_tensor_tensor(h2[:, t, :], x2[:, t, :], rstd[:, one], mod_rows[:, SCALE2, :], ALU.mult, ALU.mult))
                dve.tensor_tensor(h2[:, t, :], h2[:, t, :], mod_rows[:, SHIFT2, :], ALU.add).then_inc(h2_ready, 1)

            def route(t):
                dve.wait_ge(logit_mm, t + 1)
                lg = logit[:, t, :]
                link(dve.tensor_tensor(lg, ps[6][:, 0:NL], b_router, ALU.add))
                link(dve.tensor_copy(group8[:, 0:NG], lg[:, 0:NG]))
                link(dve.max(top_e[:, t, :], group8))
                tick(dve.max_index(gtop_i, top_e[:, t, :], group8))
                tick(dve.tensor_scalar(lg[:, 0:NG], lg[:, 0:NG], top_e[:, t, 0:1], None, ALU.subtract))
                settle()
                link(dve.tensor_copy(gi_f, gtop_i[:, 0:1]))
                link(dve.tensor_scalar(in_group[:, t, :], iota_e[:, 0:NG], gi_f, None, ALU.is_equal))
                link(dve.tensor_scalar(in_group[:, t, :], in_group[:, t, :], -1.0, -MASKED, ALU.add, ALU.mult))
                link(dve.tensor_tensor(lg[:, NG:NL].rearrange("p (g e) -> p g e", g=NG), lg[:, NG:NL].rearrange("p (g e) -> p g e", g=NG),
                                       in_group[:, t, :].unsqueeze(2).broadcast_to([P, NG, NE_G]), ALU.add))
                link(dve.max(top_e[:, t, :], lg[:, NG:NL]))
                tick(dve.max_index(top_i[:, t, :], top_e[:, t, :], lg[:, NG:NL]))
                dve.tensor_tensor(cw[:, 1, t:t + 1], top_e[:, t, 1:2], top_e[:, t, 0:1], ALU.subtract).then_inc(logit_ready, 1)
                settle()
                link(dve.tensor_copy(ei_f, top_i[:, t, 0:2]))
                for k in range(2):
                    tick(dve.tensor_scalar(choice[k][:, t, :], iota_e, ei_f[:, k:k + 1], None, ALU.is_equal))
                settle()
                dve.tensor_tensor(chosen[:, t, :], choice[0][:, t, :], choice[1][:, t, :], ALU.add).then_inc(chosen_ready, 1)
                if t >= 1:
                    dve.wait_ge(table_mm, t)
                for k in range(2):
                    tick(dve.tensor_scalar(token_of[:, k, :], choice[k][:, t, :], token_f[:, k * NT + t:k * NT + t + 1], None, ALU.mult))
                dve.wait_ge(pos_mm, t + 1)
                for k in range(2):
                    link(dve.tensor_tensor_reduce(route_tmp, ps[6][:, 0:NE], choice[k][:, t, :], 1.0, 0.0, ALU.mult, ALU.add, pos_f[:, k:k + 1]))
                for k in range(2):
                    tick(dve.tensor_scalar(at_slot[:, k, :], iota_slot, pos_f[:, k:k + 1], None, ALU.is_equal))
                settle()
                dve.scalar_tensor_tensor(slot_i[:, 2 * t:2 * t + 2], pos_f, float(NE), ei_f, ALU.mult, ALU.add).then_inc(slots_ready, 1)

            tick(dve.memset(group8, TAKEN))
            settle()
            dve.wait_ge(setup, 7)
            for t in range(NT):
                if t >= 1:
                    if t == 1:
                        dve.wait_ge(router_loaded, 64)
                    route(t - 1)
                post_mix(t)
            route(NT - 1)
            dve.wait_ge(table_mm, NT)
            link(dve.tensor_scalar(table_sb, ps[7][:, 0:NE], 2.0 * S, None, ALU.add))
            dve.tensor_single_scalar(gather_at, table_sb, S - 1, ALU.bitwise_and).then_inc(gath_idx, 1)
            dve.tensor_scalar(scatter_at, table_sb, 2.0, half, ALU.mult, ALU.add).then_inc(scat_idx, 1)
            dve.wait_ge(count_mm, 1)
            link(dve.tensor_reduce(count_f, ps[6][:, 0:NE], AX.X, ALU.max))
            dve.tensor_copy(most_tokens[:, 0:1], count_f).then_inc(count_ready, 1)
            dve.wait_ge(route_exp, 2 * NT)
            link(dve.tensor_scalar(cw[:, 0, :], cw[:, 1, :], 1.0, None, ALU.add))
            link(dve.tensor_tensor(cw[:, 0, :], cw[:, 0, :], ssq, ALU.mult))
            link(dve.reciprocal(cw[:, 0, :], cw[:, 0, :]))
            link(dve.tensor_tensor(cw[:, 1, :], cw[:, 1, :], cw[:, 0, :], ALU.mult))
            def hidden(e, j):
                dve.wait_ge(silu_done, e + 1)
                if not (isinstance(e, int) and e < 2):
                    dve.wait_ge(hidT_done, e - 1)
                dve.tensor_tensor(hid[:, j % 2, :], silu_g[:, j % 2, :], ps[2 + j % 2][CAP:P, 0:FE], ALU.mult).then_inc(hid_ready, 1)

            def hiddenT_copy(e, j):
                dve.wait_ge(hidT_done, e + 1)
                if not (isinstance(e, int) and e < 2):
                    dve.wait_ge(down_done, e - 1)
                dve.tensor_copy(hidT[:, j % 2].rearrange("p k s -> p (k s)"), ps[4 + j % 2][:, 0:FC * CAP]).then_inc(hidT_out, 1)

            def y_copy(e, j, turn):
                dve.wait_ge(down_done, e + 1)
                if not (isinstance(turn, int) and turn == 0):
                    dve.wait_ge(scattered[j], turn * 16)
                dve.tensor_copy(y_out[:, j, :], ps[6 + j % 2][:]).then_inc(y_ready, 1)

            def dve_step(i, m):
                hiddenT_copy(i * RING + (m - 1), (m - 1) % RING)
                hidden(i * RING + m, m % RING)
                y_copy(i * RING + (m - 1), (m - 1) % RING, i + (m - 1) // RING)

            hidden(0, 0)
            for m in range(1, RING + 1):
                dve_step(0, m)
            with dve.Fori(1, NE // RING - 1) as i:
                for m in range(1, RING + 1):
                    dve_step(i, m)
            for m in range(1, RING):
                dve_step(NE // RING - 1, m)
            hiddenT_copy(NE - 1, RING - 1)
            y_copy(NE - 1, RING - 1, NE // RING - 1)

            def more(r, e, m):
                dve.wait_ge(more_loaded, m * 80)
                dve.tensor_single_scalar(gather_at, table_sb, S - 1, ALU.bitwise_and).then_inc(more_table, 1)
                dve.tensor_scalar(scatter_at, table_sb, 2.0, half, ALU.mult, ALU.add).then_inc(more_table, 1)
                dve.wait_ge(more_silu, m)
                dve.tensor_tensor(hid[:, 0, :], silu_g[:, 0, :], ps[2][CAP:P, 0:FE], ALU.mult).then_inc(more_hid, 1)
                dve.wait_ge(more_hidT, m)
                dve.tensor_copy(hidT[:, 0].rearrange("p k s -> p (k s)"), ps[4][:, 0:FC * CAP]).then_inc(more_hidT_out, 1)
                dve.wait_ge(more_down, m)
                dve.tensor_copy(y_out[:, 0, :], ps[6][:]).then_inc(more_y, 1)

            more_rounds(dve, more)

            def fin_add(t):
                y0, y1 = y_back[:, 0, t, :], y_back[:, 1, t, :]
                dve.wait_ge(fin_scaled, t + 1)
                dve.wait_ge(tile_loaded[t], 48)
                dve.scalar_tensor_tensor(y0, y1, cw[:, 1, t:t + 1], y0, ALU.mult, ALU.add).then_inc(fin_sum, 1)

            def fin_norm(t):
                one = slice(t, t + 1)
                y0 = y_back[:, 0, t, :]
                dve.wait_ge(fin_sq, t + 1)
                dve.tensor_scalar(ssq[:, one], ssq[:, one], 1.0 / D, EPS, ALU.mult, ALU.add).then_inc(fin_var, 1)
                dve.wait_ge(fin_root, t + 1)
                link(dve.reciprocal(rstd[:, one], rstd[:, one]))
                link(dve.scalar_tensor_tensor(y0, y0, rstd[:, one], mod_rows[:, GATE2, :], ALU.mult, ALU.mult))
                dve.tensor_tensor(y0, y0, x2[:, t, :], ALU.add).then_inc(fin_out, 1)

            fin_add(0)
            for t in range(NT):
                if t + 1 < NT:
                    fin_add(t + 1)
                fin_norm(t)


_INS = ["x", "c", "w_ada", "b_ada", "g_pre_mix", "g_post_mix", "g_pre_ffn", "g_post_ffn", "w_in", "conv_w", "conv_b",
        "w_rg_a", "b_rg_a", "w_rg_x", "b_rg_x", "lru_lambda", "w_out", "w_router_group", "b_router_group",
        "w_router_expert", "b_router_expert", "w_gate", "w_up", "w_down"]


def kernel(**inputs):
    import numpy as _np
    import concourse.bacc as _bacc
    from concourse import mybir as _mybir
    from concourse.bass_utils import run_bass_kernel_spmd as _run

    nc = _bacc.Bacc("TRN2", target_bir_lowering=False, num_devices=1)
    arrays = {name: _np.ascontiguousarray(inputs[name]) for name in _INS}
    _, seq, d = arrays["x"].shape
    hd = d // 16
    inv = _np.float32(ROPE_THETA) ** (-_np.arange(0, hd, 2, dtype=_np.float32) / _np.float32(hd))
    ang = _np.arange(seq, dtype=_np.float32)[:, None] * inv.astype(_np.float32)[None, :]
    cos, sin = _np.cos(ang).astype(_np.float32), _np.sin(ang).astype(_np.float32)
    arrays["rope_cos"] = cos
    arrays["rope_sin"] = _np.ascontiguousarray(_np.stack([-sin, sin], axis=1))
    dram = {name: nc.dram_tensor(f"in_{name}_dram", v.shape, _mybir.dt.from_np(v.dtype), kind="ExternalInput").ap()
            for name, v in arrays.items()}
    dram["out"] = nc.dram_tensor("out_0_dram", (1, seq, d), _mybir.dt.float32, kind="ExternalOutput").ap()
    hybrid_block(nc, dram)
    r = _run(nc, [{f"in_{name}_dram": v for name, v in arrays.items()}], core_ids=[0])
    return r.results[0]["out_0_dram"]
```

```python
from contextlib import ExitStack

import concourse.bass as bass
from concourse import mybir

P = 128
F32 = mybir.dt.float32
F32R = mybir.dt.float32r
BF16 = mybir.dt.bfloat16
I32 = mybir.dt.int32
U32 = mybir.dt.uint32
ALU = mybir.AluOpType
ACT = mybir.ActivationFunctionType
AX = mybir.AxisListType

EPS = 1e-6
CHUNK = 64
TOPK_MAX = 256
ROPE_THETA = 10000.0
NOT_ADMISSIBLE = -3.0e38
TAKEN = -3.4e38
BETWEEN = -3.2e38
MASKED = -1.0e30
GELU_CUBIC = 0.044715
GELU_SCALE = 0.7978845608028654
SLOTS = 6
H_SLOT = 5
RING = 4
CAP = 64


def hybrid_block(nc, a):
    _, S, D = a["x"].shape
    NT = S // P
    KD = D // P
    H, HD = 8, D // 16
    DA = H * HD
    IH, ID = 8, 64
    R = D // 2
    RC = R // P
    NTAPS = a["conv_w"].shape[1]
    NG, NE_G = a["w_gate"].shape[1:3]
    NE = NG * NE_G
    FE = a["w_gate"].shape[4]
    FC = FE // P
    NSEL = min(TOPK_MAX, S // 4)
    ROUNDS = NSEL // 8
    NL = NG + NE
    KI = IH * ID + 3 * DA
    assert NT == 4 and KD == 8 and NSEL == P and RC == 4 and HD == ID == 64 and FC == 2

    w_in = a["w_in"][0].rearrange("(k p) n -> p k n", p=P)
    w_ada = a["w_ada"][0].rearrange("(p k) n -> p k n", k=KD)
    w_out = a["w_out"][0].rearrange("(k p) n -> p k n", p=P)
    w_gate = a["w_gate"][0].rearrange("g e (p k) f -> (g e) p k f", k=KD)
    w_up = a["w_up"][0].rearrange("g e (p k) f -> (g e) p k f", k=KD)
    w_down = a["w_down"][0].rearrange("g e (p k) n -> (g e) p k n", k=FC)
    x_rows = a["x"][0].rearrange("(t p) d -> t p d", p=P)
    out_rows = a["out"][0].rearrange("(t p) d -> t p d", p=P)

    h2_dram = nc.dram_tensor("h2_dram", [S, D], F32).ap()
    table_dram = nc.dram_tensor("table_dram", [S * NE, 1], I32).ap()
    y_dram = nc.dram_tensor("y_dram", [4 * S, D // 2], F32).ap()
    mod_dram = nc.dram_tensor("mod_dram", [8, 512], F32).ap()
    table_rows = table_dram.rearrange("(s e) one -> s (e one)", e=NE)

    with ExitStack() as ctx:
        def sb(name, shape, dt=F32):
            return ctx.enter_context(nc.sbuf_tensor(name, shape, dt))

        def sem(name):
            return ctx.enter_context(nc.semaphore(name))

        region_x = sb("region_x", [P, 4096])
        with nc.sbuf_tensor("split_y", [P, 4096], F32R) as split_y:
            pass
        region_y = sb("region_y", [P, 4096])
        with nc.sbuf_tensor("split_w", [P, 4096 * SLOTS], F32R) as split_w:
            pass
        region_w = sb("region_w", [P, 4096 * SLOTS])
        with nc.sbuf_tensor("split_h", [P, 8192], F32R) as split_h:
            pass
        region_h = sb("region_h", [P, 8192])
        region_qk = sb("region_qk", [P, 4096])
        region_v = sb("region_v", [P, 2048])
        region_m = sb("region_m", [P, 1280])
        with nc.sbuf_tensor("split_t", [P, 4096], F32R) as split_t:
            pass
        region_t = sb("region_t", [P, 4096])
        ident = sb("ident", [P, P])
        region_c = sb("region_c", [P, KD * 32])
        before = sb("before", [P, P], BF16)
        ones_b = sb("ones_b", [P, P], BF16)
        small = sb("small", [P, 208])

        c_rep = region_c[:, :].rearrange("p (k n) -> p k n", k=KD)
        at_slot = region_c[:, :].rearrange("p (k n) -> p k n", k=2)
        ada = region_x[:, 0:1536].rearrange("p (s n) -> p s n", s=3)
        gain = region_x[:, 1536:3072].rearrange("p (s n) -> p s n", s=3)
        kiT = region_x[:, 3072:3584]
        rope_cos = region_x[:, 3584:3712].rearrange("p (t f) -> p t f", t=NT)
        rope_sin = region_x[:, 3712:3968].rearrange("p (t s f) -> p t s f", t=NT, s=2)
        x2 = region_x[:, :].rearrange("p (t d) -> p t d", t=NT)
        x_in_sb = region_y[:, :].rearrange("p (t d) -> p t d", t=NT)
        roped = region_y[:, 0:1024].rearrange("p (b n) -> p b n", b=2)
        rope_tmp = region_y[:, 1024:1536]
        w_gates = region_y[:, 1536:2048].rearrange("p (g c n) -> p g c n", g=2, c=RC)
        mixT = region_y[:, :].rearrange("p (k s) -> p k s", k=KD)
        mix_lo = split_y[:, :].rearrange("p (k s) -> p k s", k=KD)
        y_out = region_y[:, 0:2048].rearrange("p (b n) -> p b n", b=RING)
        xgT = region_y[:, 2048:3072].rearrange("p (b k s) -> p b k s", b=2, k=KD)
        hid = region_y[0:CAP, 3072:3584].rearrange("p (b n) -> p b n", b=2)
        silu_g = region_y[0:CAP, 3584:4096].rearrange("p (b n) -> p b n", b=2)
        slot = region_w[:, :].rearrange("p (s n) -> p s n", s=SLOTS)
        split_slot = split_w[:, :].rearrange("p (s k n) -> p s k n", s=SLOTS, k=KD)
        expert_w = region_w[:, :].rearrange("p (b m n) -> p b m n", b=RING, m=3)
        wo_hi_at = (RING - 2) * 3 * 2048
        mix_hi_at = wo_hi_at + KD * D
        wo_hi = split_w[:, wo_hi_at:mix_hi_at].rearrange("p (k n) -> p k n", k=KD)
        mix_hi = split_w[:, mix_hi_at:mix_hi_at + KD * S].rearrange("p (k s) -> p k s", k=KD)
        hT = region_h[:, 0:4096].rearrange("p (k s) -> p k s", k=KD)
        h_lo = split_h[:, 0:4096].rearrange("p (k s) -> p k s", k=KD)
        h_hi = split_slot[:, H_SLOT, :, :]
        qiT = region_h[:, 4096:6144].rearrange("p (k s) -> p k s", k=4)
        xr = region_h[:, 6144:8192].rearrange("p (c s) -> p c s", c=RC)
        wo_sb = region_h[:, :].rearrange("p (k n) -> p k n", k=KD)
        wo_lo = split_h[:, :].rearrange("p (k n) -> p k n", k=KD)
        y_back = region_h[:, :].rearrange("p (k t n) -> p k t n", k=2, t=NT)
        qT = region_qk[:, 0:2048].rearrange("p (k s) -> p k s", k=4)
        kT = region_qk[:, 2048:4096].rearrange("p (k s) -> p k s", k=4)
        mod_rows = region_qk[:, :].rearrange("p (m n) -> p m n", m=4)
        GATE1, SHIFT2, SCALE2, GATE2 = range(4)
        v_sb = region_v[:, :].rearrange("p (t n) -> p t n", t=NT)
        h2T = region_v[:, :].rearrange("p (b k s) -> p b k s", b=2, k=KD)
        hidT = region_qk[:, 2048:2304].rearrange("p (b k s) -> p b k s", b=2, k=FC)
        spare_w = [[region_h[:, 2048 * m:2048 * (m + 1)] for m in range(3)], [region_h[:, 6144:8192], region_qk[:, 0:2048], region_v[:, :]]]
        score_at = [0, 128, 384, 768]
        score = [region_m[:, score_at[t]:score_at[t] + P * (t + 1)] for t in range(NT)]
        m_at = [0]

        def in_m(n, dt=F32):
            m_at[0] += n
            v = region_m[:, m_at[0] - n:m_at[0]]
            return v if dt == F32 else v.bitcast(dt)

        w_router = in_m(KD * NL).rearrange("p (k n) -> p k n", k=KD)
        b_router = in_m(NL)
        logit = in_m(NT * NL).rearrange("p (t n) -> p t n", t=NT)
        group8 = in_m(8)
        in_group = in_m(NT * NG).rearrange("p (t n) -> p t n", t=NT)
        choice = [in_m(NT * NE).rearrange("p (t n) -> p t n", t=NT) for _ in range(2)]
        chosen = in_m(NT * NE // 2, BF16).rearrange("p (t n) -> p t n", t=NT)
        iota_e = in_m(NE)
        route_tmp = in_m(NE)
        token_of = in_m(2 * NE).rearrange("p (k n) -> p k n", k=2)
        iota_slot = in_m(2 * CAP)
        table_sb = in_m(NE, I32)
        gather_at = in_m(NE, I32)
        scatter_at = in_m(NE, I32)
        top_e = in_m(NT * 8).rearrange("p (t n) -> p t n", t=NT)
        top_i = in_m(NT * 8, U32).rearrange("p (t n) -> p t n", t=NT)
        gtop_i = in_m(8, U32)
        junk = region_t[:, 1024:2048]
        w_kiwi = region_t[:, 0:576].rearrange("p (k n) -> p k n", k=KD)
        kiwi_both = split_t[:, 1024:2176].rearrange("p (k a n) -> p k a n", k=KD, a=2)
        ki_sum = region_t[:, 896:896 + ID + IH]
        ki_rows = region_t[:, 576:832].rearrange("p (b n) -> p b n", b=2)
        ki_tmp = region_t[:, 832:896]
        a_rec = region_t[:, 0:2048].rearrange("p (c s) -> p c s", c=RC)
        conv = region_t[:, 2048:3072].rearrange("p (b s) -> p b s", b=2)
        tanh_r = region_t[:, 3072:3584]
        tanh_i = region_t[:, 3584:4096]
        relu_b = region_t[:, 3072:4096].rearrange("p (b s) -> p b s", b=2)
        gel = region_t[:, 3072:4096].rearrange("p (b s) -> p b s", b=2)
        prob = region_t[:, 0:3072].rearrange("p (b h s) -> p b h s", b=3, h=2)
        probT = region_t[:, 3072:4096].rearrange("p (h s) -> p h s", h=2)
        h2 = region_t[:, :].rearrange("p (t d) -> p t d", t=NT)
        x_gath = region_t[0:CAP, :].rearrange("p (b n) -> p b n", b=RING)

        n_small = [0]

        def col(n, dt=F32):
            n_small[0] += n
            v = small[:, n_small[0] - n:n_small[0]]
            return v if dt == F32 else v.bitcast(dt)

        c_col = col(KD)
        ssq = col(NT)
        rstd = col(NT)
        mod1 = col(2 * KD)
        par = col(32)
        sp4 = col(RC)
        sp4n = col(RC)
        spt = col(2 * RC)
        w_idx = col(NT * IH).rearrange("p (t n) -> p t n", t=NT)
        top8 = col(3 * 8).rearrange("p (t n) -> p t n", t=3)
        rmax = col(4)
        nmax = col(4)
        rsum = col(4)
        pssq = col(2)
        cw = col(2 * NT).rearrange("p (k t) -> p k t", k=2)
        token_v = col(2 * NT, I32)
        slot_i = col(2 * NT, I32)
        token_f = col(2 * NT)
        pos_f = col(2)
        count_f = col(1)
        gidx = col(RING, I32)
        sidx = col(RING, I32)
        gi_f = col(1)
        ei_f = col(2)
        half = col(1)
        most_tokens = col(2, I32)
        assert n_small[0] <= 208 and m_at[0] <= 1280, (n_small, m_at)
        par_rows = region_t[0:32, 3968:4096]

        ps = [ctx.enter_context(nc.psum_tensor(f"ps{i}", [P, 512], F32)) for i in range(8)]

        tile_loaded = [sem(f"tile_loaded{t}") for t in range(NT)]
        c_loaded = sem("c_loaded")
        first_loaded = sem("first_loaded")
        params_loaded = sem("params_loaded")
        ada_params_loaded = sem("ada_params_loaded")
        rope_loaded = sem("rope_loaded")
        kiwi_loaded = sem("kiwi_loaded")
        gates_loaded = sem("gates_loaded")
        slot_loaded = [sem(f"slot_loaded{s}") for s in range(H_SLOT)]
        ada_used = sem("ada_used")
        ada_loaded = [sem(f"ada_loaded{b}") for b in range(2)]
        hi_ready = sem("hi_ready")
        lo_ready = sem("lo_ready")
        lo_odd = sem("lo_odd")
        kiwi_hi_ready = sem("kiwi_hi_ready")
        h_hi_ready = sem("h_hi_ready")
        h_lo_ready = sem("h_lo_ready")
        wo_loaded = sem("wo_loaded")
        router_loaded = sem("router_loaded")
        x_again = sem("x_again")
        setup = sem("setup")
        chain = sem("chain")
        achain = sem("achain")
        pchain = sem("pchain")
        silu_c = sem("silu_c")
        c_ready = sem("c_ready")
        sq_done = sem("sq_done")
        var_ready = sem("var_ready")
        root_ready = sem("root_ready")
        xn_ready = sem("xn_ready")
        par_T = sem("par_T")
        par_sb = sem("par_sb")
        sp_exp = sem("sp_exp")
        xT_done = sem("xT_done")
        xT_even = sem("xT_even")
        xT_odd = sem("xT_odd")
        ada_ready = sem("ada_ready")
        mod1_T = sem("mod1_T")
        h_ready = sem("h_ready")
        proj_done = sem("proj_done")
        rope_ready = sem("rope_ready")
        ropeT_done = sem("ropeT_done")
        ropeT_out = sem("ropeT_out")
        ki_done = sem("ki_done")
        ki_ready = sem("ki_ready")
        kiT_done = sem("kiT_done")
        kiT_out = sem("kiT_out")
        v_out = sem("v_out")
        dots_done = sem("dots_done")
        relu_done = sem("relu_done")
        score_acc = sem("score_acc")
        xr_done = sem("xr_done")
        xr_out = sem("xr_out")
        conv_ready = sem("conv_ready")
        gate_mm = sem("gate_mm")
        gate_act = sem("gate_act")
        rec_done = sem("rec_done")
        rec_root = sem("rec_root")
        rec_b = sem("rec_b")
        xg_done = sem("xg_done")
        xg_sq = sem("xg_sq")
        xg_cubic = sem("xg_cubic")
        xg_tanh = sem("xg_tanh")
        xg_mult = sem("xg_mult")
        mask_ready = sem("mask_ready")
        qk_done = sem("qk_done")
        nmax_ready = sem("nmax_ready")
        exp_done = sem("exp_done")
        prob_ready = sem("prob_ready")
        probT_done = sem("probT_done")
        probT_even = sem("probT_even")
        probT_odd = sem("probT_odd")
        pv_done = sem("pv_done")
        attn_hi = sem("attn_hi")
        attn_out = sem("attn_out")
        spare_loaded = sem("spare_loaded")
        mod_stored = sem("mod_stored")
        rows_loaded = sem("rows_loaded")
        mix_done = sem("mix_done")
        mix_sq = sem("mix_sq")
        mix_var = sem("mix_var")
        mix_root = sem("mix_root")
        x2_ready = sem("x2_ready")
        x2_sq = sem("x2_sq")
        x2_var = sem("x2_var")
        x2_root = sem("x2_root")
        h2_ready = sem("h2_ready")
        h2_stored = sem("h2_stored")
        h2T_done = sem("h2T_done")
        h2T_out = sem("h2T_out")
        logit_mm = sem("logit_mm")
        logit_ready = sem("logit_ready")
        route_exp = sem("route_exp")
        chosen_ready = sem("chosen_ready")
        pos_mm = sem("pos_mm")
        slots_ready = sem("slots_ready")
        table_clear = sem("table_clear")
        table_set = sem("table_set")
        table_mm = sem("table_mm")
        gath_idx = sem("gath_idx")
        gidx_ready = sem("gidx_ready")
        sidx_ready = sem("sidx_ready")
        gathered = [sem(f"gathered{j}") for j in range(RING)]
        expert_loaded = [sem(f"expert_loaded{j}") for j in range(RING)]
        xgT_done = sem("xgT_done")
        xgT_out = sem("xgT_out")
        gu_done = sem("gu_done")
        silu_done = sem("silu_done")
        hid_ready = sem("hid_ready")
        hidT_done = sem("hidT_done")
        hidT_out = sem("hidT_out")
        down_done = sem("down_done")
        y_ready = sem("y_ready")
        scattered = [sem(f"scattered{j}") for j in range(RING)]
        all_scattered = sem("all_scattered")
        fin_scaled = sem("fin_scaled")
        fin_gated = sem("fin_gated")
        fin_sum = sem("fin_sum")
        fin_sq = sem("fin_sq")
        fin_var = sem("fin_var")
        fin_root = sem("fin_root")
        fin_out = sem("fin_out")
        stored = sem("stored")
        count_ready = sem("count_ready")
        passed = sem("passed")
        more_turn = sem("more_turn")
        more_loaded = sem("more_loaded")
        more_table = sem("more_table")
        more_idx = sem("more_idx")
        more_gathered = sem("more_gathered")
        more_xT = sem("more_xT")
        more_xT_out = sem("more_xT_out")
        more_gu = sem("more_gu")
        more_silu = sem("more_silu")
        more_hid = sem("more_hid")
        more_hidT = sem("more_hidT")
        more_hidT_out = sem("more_hidT_out")
        more_down = sem("more_down")
        more_y = sem("more_y")
        more_scattered = sem("more_scattered")

        QI, Q, K, V, XR, XG = range(6)
        W_COL = (3 * DA, 0, DA, 2 * DA, KI + ID + IH, KI + ID + IH + R)
        LO_SLOT = (4, 0, 1, 4, 1, 4)
        HI_SLOT = (2, 3, 2, 3, 2, 3)
        LO_USE = (1, 2, 2, 2, 3, 3)
        SLOT_USES = (2, 3, 1, 1)
        PIECES = (8, 2, 2, 2, 2, 2)
        ADA_SLOT = slot[:, 0, :].rearrange("p (b n) -> p b n", b=2)
        NADA = 2 * KD

        W_HI, W_LO, WO_PIECES = sum(PIECES), sum(PIECES) - PIECES[0] // 2 + 1, 4

        WO_STEP = 7

        def wo_piece(i):
            return slice(i * KD // WO_PIECES, (i + 1) * KD // WO_PIECES)

        def piece(w, i):
            n = KD // PIECES[w]
            return slice(i * n, (i + 1) * n), sum(PIECES[:w]) + i + 1

        def halves(w):
            return split_slot[:, HI_SLOT[w]], split_slot[:, LO_SLOT[w]]

        def raw(w):
            return slot[:, LO_SLOT[w], :].rearrange("p (k n) -> p k n", k=KD)

        def split_hi(act, w, i):
            if i == 0:
                act.wait_ge(slot_loaded[LO_SLOT[w]], 16 * LO_USE[w])
                if w >= 2:
                    wait_used(act, w - 2)
                elif w == QI:
                    act.wait_ge(ada_used, 4)
                else:
                    act.wait_ge(ada_used, 4)
            k, _ = piece(w, i)
            act.activation(halves(w)[0][:, k, :], raw(w)[:, k, :], ACT.Copy).then_inc(hi_ready, 1)

        def split_lo(eng, w, i, done):
            k, n = piece(w, i)
            hi, lo = halves(w)
            eng.wait_ge(hi_ready, n)
            eng.tensor_tensor(lo[:, k, :], raw(w)[:, k, :], hi[:, k, :], ALU.subtract).then_inc(done, 1)

        def wait_lo(pe, w):
            if w == QI:
                pe.wait_ge(lo_odd, KD // 2)
            pe.wait_ge(lo_ready, KD // 2 + (1 + 2 * w if w > QI else 0))

        def wait_used(eng, w):
            if w < XR:
                eng.wait_ge(proj_done, NT * (w + 1))
            else:
                eng.wait_ge(xr_done if w == XR else xg_done, RC)

        UNITS = [(w, t) for w in (QI, Q, K, V) for t in range(NT)]
        NROPE = 3 * NT
        DOT_UNITS = (6, 7, 8)
        XG_BANK = (2, 3, 4, 5)
        LOGIT_BANK = (6, 6, 6, 0)
        PAIRS = [(t, hp) for t in range(NT) for hp in range(H // 2)]

        def load_expert(eng, e, places, done, down_done=None):
            for m, (w, k) in enumerate(((w_gate, KD), (w_up, KD), (w_down, FC))):
                src = w[bass.ds(e, 1)].rearrange("e p k n -> p (e k) n")
                eng.dma_start(places[m].rearrange("p (k n) -> p k n", k=k), src).then_inc(down_done if down_done and m == 2 else done, 16)

        SPARE = 4 * RING
        assert NE % RING == 0 and SPARE < NE

        def ring_w(j):
            return [expert_w[:, j, m, :] for m in range(3)]

        def load_ring(eng, e, j):
            load_expert(eng, e, ring_w(j), expert_loaded[j], slot_loaded[j])

        def weights_of(i, n, late=False):
            if isinstance(i, int) and i * RING + n in (SPARE, SPARE + 1):
                m = i * RING + n - SPARE
                return spare_w[m], spare_loaded, 96, spare_loaded, 96
            if late or (isinstance(i, int) and i * RING + n > SPARE):
                n -= 2
            j, turn = n % RING, i + n // RING
            return ring_w(j), expert_loaded[j], turn * 32 + 32, slot_loaded[j], turn * 16 + (16 * SLOT_USES[j] + 16)

        def attn_tile(t):
            w = slice(t * P, (t + 1) * P)
            return ps[7 - t % 2][:].rearrange("p (k s) -> p k s", k=4), mix_hi[:, 0:4, w], mix_lo[:, 0:4, w]

        def apart(eng):
            eng.sem_inc(passed, 1)

        def more_rounds(eng, body):
            eng.wait_ge(count_ready, 1)
            most = eng.value_load(most_tokens[0:1, 0:1], min_val=0, max_val=S)
            with eng.If(most > CAP):
                with eng.Fori(1, S // CAP) as r:
                    with eng.Fori(0, NE) as e:
                        body(r, e, r * NE + e - (NE - 1))

        block = ctx.enter_context(nc.Block())

        @block.sync
        def _(sp):
            for t in range(NT):
                sp.dma_start(x_in_sb[:, t, :], x_rows[t]).then_inc(tile_loaded[t], 16)

            b_quad = a["b_ada"][0].rearrange("(q n) -> q n", n=512)

            def load_bias(s, done):
                for r in range(4):
                    sp.dma_start(ada[32 * r:32 * r + 32, s, :], b_quad[4 * s + r].partition_broadcast(32)).then_inc(done, 16)

            def load_gain(name, s, half, done):
                g = a[name][0].rearrange("(q n) -> q n", n=512)
                for q in range(2):
                    r = 2 * half + q
                    sp.dma_start(gain[32 * r:32 * r + 32, s, :], g[q].partition_broadcast(32)).then_inc(done, 16)

            def load_weight(w):
                sp.dma_start(raw(w), w_in[:, :, W_COL[w]:W_COL[w] + 512]).then_inc(slot_loaded[LO_SLOT[w]], 16)

            def load_ada(q):
                if q >= 2:
                    sp.wait_ge(ada_used, 4 + q - 1)
                third = 1 + q // KD
                sp.dma_start(ADA_SLOT[:, q % 2, :], w_ada[:, q % KD, 2048 * third:2048 * (third + 1)]).then_inc(ada_loaded[q % 2], 16)

            for j in range(4):
                sp.dma_start(slot[:, j, :].rearrange("p (k n) -> p k n", k=2), w_ada[:, 2 * j:2 * j + 2, 0:2048]).then_inc(slot_loaded[j], 16)
            load_bias(0, first_loaded)
            load_gain("g_pre_mix", 0, 1, first_loaded)
            load_weight(QI)
            sp.dma_start(rope_cos, a["rope_cos"].rearrange("(t p) f -> p t f", p=P)).then_inc(rope_loaded, 16)
            sp.dma_start(rope_sin, a["rope_sin"].rearrange("(t p) s f -> p t s f", p=P)).then_inc(rope_loaded, 16)
            for name, r0, nr in (("conv_w", 0, 16), ("conv_b", 16, 4), ("b_rg_a", 20, 4), ("b_rg_x", 24, 4), ("lru_lambda", 28, 4)):
                src = a[name][0]
                src = src.rearrange("w (c p) -> (w c) p", p=P) if name == "conv_w" else src.rearrange("(c p) -> c p", p=P)
                sp.dma_start(par_rows[r0:r0 + nr, :], src).then_inc(params_loaded, 16)
            sp.dma_start(w_kiwi, w_in[:, :, KI:KI + ID + IH]).then_inc(kiwi_loaded, 16)
            sp.wait_ge(ada_used, 2)
            load_weight(Q)
            load_weight(K)
            sp.wait_ge(xT_done, KD)
            for g, name in enumerate(("w_rg_a", "w_rg_x")):
                for half in range(2):
                    w = a[name][0].rearrange("(c b) i j -> b i c j", b=2)[half]
                    sp.dma_start(w_gates[64 * half:64 * half + 64, g], w).then_inc(gates_loaded, 16)
            for s in (1, 2):
                load_bias(s, ada_params_loaded)
            for name, s, half in (("g_post_mix", 1, 0), ("g_pre_ffn", 2, 0), ("g_post_ffn", 2, 1)):
                load_gain(name, s, half, ada_params_loaded)
            wait_used(sp, QI)
            load_weight(V)
            wait_used(sp, Q)
            for q in range(NADA - 2):
                if q == 5:
                    wait_used(sp, K)
                    load_weight(XR)
                if q == 9:
                    wait_used(sp, V)
                    load_weight(XG)
                load_ada(q)
            for q in range(NADA - 2, NADA):
                load_ada(q)
            wait_used(sp, XG)
            sp.wait_ge(dots_done, 8 * (NT - 1))
            sp.wait_ge(rec_b, 1)
            sp.dma_start(wo_sb, w_out).then_inc(wo_loaded, 16)
            sp.wait_ge(ada_used, 4 + NADA)
            for j in range(2):
                load_ring(sp, j, j)
            sp.wait_ge(ada_ready, 3)
            for r in range(4):
                sp.dma_start(mod_dram.rearrange("(s r) n -> r s n", r=4)[r:r + 1], ada[32 * r:32 * r + 1, 1:3, :]).then_inc(mod_stored, 16)
            sp.wait_ge(mod_stored, 64)
            for t in range(NT):
                sp.dma_start(x2[:, t, :], x_rows[t]).then_inc(x_again, 16)
            sp.wait_ge(qk_done, len(PAIRS))
            for m in range(4):
                src = mod_dram[2 * m:2 * m + 2, :].rearrange("r n -> (r n)").partition_broadcast(P)
                sp.dma_start(mod_rows[:, m, :], src).then_inc(rows_loaded, 16)
            sp.wait_ge(nmax_ready, len(PAIRS))
            sp.dma_start(w_router[:, :, 0:NG], a["w_router_group"][0].rearrange("(k p) n -> p k n", p=P)).then_inc(router_loaded, 16)
            sp.dma_start(w_router[:, :, NG:NL], a["w_router_expert"][0].rearrange("(k p) n -> p k n", p=P)).then_inc(router_loaded, 16)
            sp.dma_start(b_router[:, 0:NG], a["b_router_group"][0].partition_broadcast(P)).then_inc(router_loaded, 16)
            sp.dma_start(b_router[:, NG:NL], a["b_router_expert"][0].partition_broadcast(P)).then_inc(router_loaded, 16)
            for t in range(NT):
                if t == NT - 1:
                    sp.wait_ge(mix_done, 2 * NT)
                    load_ring(sp, 2, 2)
                sp.wait_ge(h2_ready, 2 * t + 2)
                sp.dma_start(h2_dram[t * P:(t + 1) * P, :], h2[:, t, :]).then_inc(h2_stored, 16)
            load_ring(sp, 3, 3)
            sp.wait_ge(logit_mm, NT)
            sp.wait_ge(gathered[RING - 1], 16)
            for m in range(2):
                load_expert(sp, SPARE + m, spare_w[m], spare_loaded)
            with sp.Fori(0, SPARE // RING - 1) as i:
                for j in range(RING):
                    sp.wait_ge(down_done, i * RING + (j + 1))
                    load_ring(sp, i * RING + (j + RING), j)
            for j in range(RING):
                sp.wait_ge(down_done, SPARE - RING + j + 1)
                load_ring(sp, SPARE + 2 + j, j)
            with sp.Fori(SPARE // RING, NE // RING - 2) as i:
                for j in range(RING):
                    sp.wait_ge(down_done, i * RING + (j + 3))
                    load_ring(sp, i * RING + (j + RING + 2), j)
            for j in range(2):
                sp.wait_ge(down_done, NE - 2 - RING + j + 1)
                load_ring(sp, NE - 2 + j, j)

            def more(r, e, m):
                sp.wait_ge(more_turn, m)
                for k, (w, kc) in enumerate(((w_gate, KD), (w_up, KD), (w_down, FC))):
                    src = w[bass.ds(e, 1)].rearrange("e p k n -> p (e k) n")
                    sp.dma_start(expert_w[:, 0, k, :].rearrange("p (k n) -> p k n", k=kc), src).then_inc(more_loaded, 16)
                for n in range(2):
                    sp.dma_start(table_sb[CAP * n:CAP * n + CAP, :], table_rows[bass.ds(r * CAP, CAP), :]).then_inc(more_loaded, 16)

            sp.wait_ge(table_set, 16 * 2 * NT)
            more_rounds(sp, more)
            sp.wait_ge(all_scattered, 1)
            for t in range(NT):
                for k in range(2):
                    src = y_dram[2 * (k * S + t * P):2 * (k * S + t * P + P), :].rearrange("(p two) n -> p (two n)", two=2)
                    sp.dma_start(y_back[:, k, t, :], src).then_inc(tile_loaded[t], 16)
            for t in range(NT):
                if t < NT - 1:
                    sp.wait_ge(fin_out, t + 1)
                else:
                    sp.wait_ge(fin_gated, NT)
                sp.dma_start(out_rows[t], y_back[:, 0, t, :]).then_inc(stored, 16)
            sp.wait_ge(stored, 16 * NT)

        @block.gpsimd
        def _(pool):
            pool.memset(ident[:], 0.0).then_inc(pchain, 1)
            pool.memset(before[:], 0.0).then_inc(pchain, 1)
            pool.wait_ge(pchain, 2)
            pool.affine_select(out=ident[:], in_=ident[:], compare_op=ALU.not_equal, fill=1.0, base=0,
                               pattern=[[-1, P]], channel_multiplier=1).then_inc(setup, 1)
            pool.affine_select(out=before[:], in_=before[:], compare_op=ALU.is_ge, fill=1.0, base=0,
                               pattern=[[-1, P]], channel_multiplier=1).then_inc(setup, 1)
            pool.memset(ones_b[:], 1.0).then_inc(setup, 1)
            pool.iota(token_v[:, :], pattern=[[P, NT], [S, 2]], base=0, channel_multiplier=1).then_inc(setup, 1)
            pool.iota(token_f, pattern=[[S, 2], [P, NT]], base=-2 * S, channel_multiplier=1,
                      allow_small_or_imprecise_dtypes=True).then_inc(setup, 1)
            clear = region_v[:, 0:P].bitcast(I32)
            pool.iota(clear, pattern=[[0, P]], base=2 * S, channel_multiplier=0).then_inc(pchain, 1)
            pool.wait_ge(pchain, 3)
            pool.dma_start(table_dram.rearrange("(p n) one -> p (n one)", p=P), clear).then_inc(table_clear, 16)
            for w in range(6):
                for i in range(PIECES[w]):
                    if w == QI and i % 2 == 1:
                        continue
                    split_lo(pool, w, i, lo_ready)
                if w == QI:
                    pool.wait_ge(kiwi_hi_ready, 1)
                    pool.tensor_tensor(kiwi_both[:, :, 1, :], w_kiwi, kiwi_both[:, :, 0, :], ALU.subtract).then_inc(lo_ready, 1)
            pool.wait_ge(hi_ready, W_HI + 1)
            pool.tensor_tensor(mix_lo[:, 4:8, :], mixT[:, 4:8, :], mix_hi[:, 4:8, :], ALU.subtract).then_inc(lo_ready, 1)
            for i in range(WO_PIECES):
                k = wo_piece(i)
                pool.wait_ge(hi_ready, W_HI + 2 + i)
                pool.tensor_tensor(wo_lo[:, k, :], wo_sb[:, k, :], wo_hi[:, k, :], ALU.subtract).then_inc(lo_ready, 1)
            pool.wait_ge(nmax_ready, len(PAIRS))
            pool.iota(iota_e, pattern=[[1, NE]], base=0, channel_multiplier=0,
                      allow_small_or_imprecise_dtypes=True).then_inc(setup, 1)
            pool.iota(iota_slot, pattern=[[0, 2], [1, CAP]], base=0, channel_multiplier=0,
                      allow_small_or_imprecise_dtypes=True).then_inc(setup, 1)
            pool.wait_ge(h2_stored, 16 * NT)
            pool.wait_ge(gath_idx, 1)

            def gather(e, j):
                pool.tensor_copy(gidx[0:CAP, j:j + 1], gather_at[0:CAP, bass.ds(e, 1)]).then_inc(gidx_ready, 1)
                pool.wait_ge(gidx_ready, e + 1)
                apart(pool)
                pool.indirect_dma_start(out=x_gath[:, j, :], out_offset=None, in_=h2_dram,
                                        in_offset=bass.IndirectOffsetOnAxis(ap=gidx[0:CAP, j:j + 1], axis=0),
                                        bounds_check=S - 1, oob_is_err=False).then_inc(gathered[j], 16)

            def scatter(e, j, turn):
                if not (isinstance(turn, int) and turn == 0):
                    pool.wait_ge(scattered[j], turn * 16)
                pool.tensor_copy(sidx[:, j:j + 1], scatter_at[:, bass.ds(e, 1)]).then_inc(sidx_ready, 1)
                pool.wait_ge(sidx_ready, e + 1)
                pool.wait_ge(y_ready, e + 1)
                apart(pool)
                pool.indirect_dma_start(out=y_dram, out_offset=bass.IndirectOffsetOnAxis(ap=sidx[:, j:j + 1], axis=0),
                                        in_=y_out[:, j, :], in_offset=None, bounds_check=4 * S - 1,
                                        oob_is_err=False).then_inc(scattered[j], 16)

            def pool_turn(i):
                for j in range(RING):
                    pool.wait_ge(xgT_done, i * RING + (j + 1))
                    apart(pool)
                    gather(i * RING + (j + RING), j)
                    scatter(i * RING + j, j, i)

            for j in range(RING):
                gather(j, j)
            pool.wait_ge(table_clear, 16)
            pool.wait_ge(slots_ready, NT)
            for n in range(2 * NT):
                pool.indirect_dma_start(out=table_dram, out_offset=bass.IndirectOffsetOnAxis(ap=slot_i[:, n:n + 1], axis=0),
                                        in_=token_v[:, n:n + 1], in_offset=None).then_inc(table_set, 16)
            pool.wait_ge(gath_idx, 2)
            pool_turn(0)
            with pool.Fori(1, NE // RING - 1) as i:
                pool_turn(i)
            for j in range(RING):
                scatter(NE - RING + j, j, NE // RING - 1)
            for j in range(RING):
                pool.wait_ge(scattered[j], NE // RING * 16)

            def more(r, e, m):
                pool.wait_ge(more_table, m * 2)
                pool.tensor_copy(gidx[0:CAP, 0:1], gather_at[0:CAP, bass.ds(e, 1)]).then_inc(more_idx, 1)
                pool.tensor_copy(sidx[:, 0:1], scatter_at[:, bass.ds(e, 1)]).then_inc(more_idx, 1)
                pool.wait_ge(more_idx, m * 2)
                apart(pool)
                pool.indirect_dma_start(out=x_gath[:, 0, :], out_offset=None, in_=h2_dram,
                                        in_offset=bass.IndirectOffsetOnAxis(ap=gidx[0:CAP, 0:1], axis=0),
                                        bounds_check=S - 1, oob_is_err=False).then_inc(more_gathered, 16)
                pool.wait_ge(more_y, m)
                apart(pool)
                pool.indirect_dma_start(out=y_dram, out_offset=bass.IndirectOffsetOnAxis(ap=sidx[:, 0:1], axis=0),
                                        in_=y_out[:, 0, :], in_offset=None, bounds_check=4 * S - 1,
                                        oob_is_err=False).then_inc(more_scattered, 16)
                pool.wait_ge(more_scattered, m * 16)
                pool.sem_inc(more_turn, 1)

            pool.sem_inc(more_turn, 1)
            more_rounds(pool, more)
            pool.engine_nop().then_inc(all_scattered, 1)
            for t in range(NT - 1):
                pool.wait_ge(fin_gated, t + 1)
                pool.tensor_tensor(y_back[:, 0, t, :], y_back[:, 0, t, :], x2[:, t, :], ALU.add).then_inc(fin_out, 1)

        @block.tensor
        def _(pe):
            pe.wait_ge(setup, 1)
            for t in range(NT):
                pe.wait_ge(xn_ready, t + 1)
            for k in range(KD):
                for t in range(NT):
                    last = pe.transpose(ps[k][:, t * P:(t + 1) * P], x_in_sb[:, t, k * P:(k + 1) * P], ident[:])
                last.then_inc(xT_done, 1)

            def ada_chunk(k, w, bank):
                for r in range(4):
                    last = pe.matmul(ps[bank][32 * r:32 * r + 32, :], c_rep[:, k, :], w[:, 512 * r:512 * (r + 1)],
                                     start=(k == 0), stop=(k == KD - 1))
                return last

            def ada_later(q):
                pe.wait_ge(ada_loaded[q % 2], 16 * (q // 2 + 1))
                if q == 0:
                    pe.wait_ge(relu_done, IH * (NT - 1))
                ada_chunk(q % KD, ADA_SLOT[:, q % 2, :], 7 - q // KD).then_inc(ada_used, 1)

            pe.wait_ge(c_ready, 1)
            pe.wait_ge(xT_even, 1)
            pe.wait_ge(xT_odd, 1)
            for j in range(4):
                pe.wait_ge(slot_loaded[j], 16)
                for k in (2 * j, 2 * j + 1):
                    last = ada_chunk(k, slot[:, j, 2048 * (k % 2):2048 * (k % 2 + 1)], 0)
                last.then_inc(ada_used, 1)
            pe.wait_ge(ada_ready, 1)
            for j in range(4):
                last = pe.transpose(ps[1][:, j * P:(j + 1) * P], ada[:, 0, j * P:(j + 1) * P], ident[:])
            last.then_inc(mod1_T, 1)

            def rope_T(u):
                pe.wait_ge(rope_ready, u + 1)
                if u >= 2:
                    pe.wait_ge(ropeT_out, u - 1)
                else:
                    pe.wait_ge(xT_even, KD // 2)
                    pe.wait_ge(xT_odd, KD // 2)
                for j in range(4):
                    last = pe.transpose(ps[2 + u % 2][:, j * P:(j + 1) * P], roped[:, u % 2, j * P:(j + 1) * P], ident[:])
                last.then_inc(ropeT_done, 1)

            def ki_T(t):
                pe.wait_ge(ki_ready, t + 1)
                pe.transpose(ps[5][:, t * P:(t + 1) * P], ki_rows[:, t % 2, :], ident[:]).then_inc(kiT_done, 1)

            def index_dot(t, h):
                n = (t - 1) * IH + h
                if n == 0:
                    pe.wait_ge(ropeT_out, NT)
                    pe.wait_ge(kiT_out, 1)
                if n >= 2:
                    pe.wait_ge(relu_done, n - 1)
                hp = 64 * (h % 2)
                pe.matmul(ps[6 + h % 2][:, 0:P * (t + 1)], qiT[hp:hp + 64, h // 2, t * P:(t + 1) * P],
                          kiT[hp:hp + 64, 0:P * (t + 1)], start=True, stop=True).then_inc(dots_done, 1)

            for u, (w, t) in enumerate(UNITS):
                if u < 2:
                    pe.wait_ge(mod1_T, 1)
                elif u - 2 < NROPE:
                    pe.wait_ge(rope_ready, u - 1)
                else:
                    pe.wait_ge(v_out, u - 1 - NROPE)
                w_hi, w_lo = halves(w)
                rows = slice(t * P, (t + 1) * P)
                if u < 2:
                    pe.wait_ge(h_hi_ready, u + 1)
                for k in range(KD):
                    if t == 0 and (w == QI or k == 0):
                        pe.wait_ge(hi_ready, piece(w, k)[1] if w == QI else piece(w, PIECES[w] - 1)[1])
                    pe.matmul(ps[u % 2][:], h_hi[:, k, rows], w_hi[:, k, :], start=(k == 0), stop=False)
                if u < 2:
                    pe.wait_ge(h_lo_ready, u + 1)
                for k in range(KD):
                    pe.matmul(ps[u % 2][:], h_lo[:, k, rows], w_hi[:, k, :], start=False, stop=False)
                    if u in DOT_UNITS and k % 2 == 1:
                        index_dot(u - DOT_UNITS[0] + 1, k // 2)
                if t == 0:
                    wait_lo(pe, w)
                for k in range(KD):
                    last = pe.matmul(ps[u % 2][:], h_hi[:, k, rows], w_lo[:, k, :], start=False, stop=(k == KD - 1))
                    if u in DOT_UNITS and k % 2 == 0:
                        index_dot(u - DOT_UNITS[0] + 1, 4 + k // 2)
                last.then_inc(proj_done, 1)
                if u == 0:
                    pe.wait_ge(params_loaded, 16 * 5)
                    pe.transpose(ps[7][:, 0:32], par_rows, ident[0:32, 0:32]).then_inc(par_T, 1)
                if w == QI:
                    pe.wait_ge(kiwi_hi_ready, 1)
                    pe.wait_ge(lo_ready, KD // 2 + 1)
                    if t >= 2:
                        pe.wait_ge(ki_ready, t - 1)
                    out = ps[4 + 2 * (t % 2)]
                    for k in range(KD):
                        pe.matmul(out[:, 0:2 * (ID + IH)], h_hi[:, k, rows], kiwi_both[:, k, :, :].rearrange("p a n -> p (a n)"),
                                  start=(k == 0), stop=False)
                    for k in range(KD):
                        last = pe.matmul(out[:, 0:ID + IH], h_lo[:, k, rows], kiwi_both[:, k, 0, :], start=False, stop=(k == KD - 1))
                    last.then_inc(ki_done, 1)
                if 1 <= u <= NROPE:
                    rope_T(u - 1)
                if 1 <= u <= NT:
                    ki_T(u - 1)
                if w in (K, V):
                    ada_later(u - 8)

            def proj_T(w, c, bank, done):
                w_hi, w_lo = halves(w)
                if c == 0:
                    pe.wait_ge(hi_ready, piece(w, PIECES[w] - 1)[1])
                for m, (left, right) in enumerate(((w_hi, h_hi), (w_hi, h_lo), (w_lo, h_hi))):
                    if c == 0 and m == 2:
                        wait_lo(pe, w)
                    for k in range(KD):
                        last = pe.matmul(ps[bank][:], left[:, k, c * P:(c + 1) * P], right[:, k, :],
                                         start=(m == 0 and k == 0), stop=(m == 2 and k == KD - 1))
                last.then_inc(done, 1)

            def gates(c):
                pe.wait_ge(conv_ready, c + 1)
                if c >= 1:
                    pe.wait_ge(gate_act, 2 * c)
                for g in range(2):
                    for half in range(2):
                        r = slice(64 * half, 64 * half + 64)
                        last = pe.matmul(ps[4 + g][r, :], w_gates[r, g, c, :], conv[r, c % 2, :], start=True, stop=True)
                last.then_inc(gate_mm, 1)

            pe.wait_ge(v_out, NT)
            pe.wait_ge(gates_loaded, 64)
            for c in range(RC):
                if c >= 2:
                    pe.wait_ge(xr_out, c - 1)
                proj_T(XR, c, c % 2, xr_done)
                ada_later(8 + c)
                if c >= 1:
                    gates(c - 1)
            pe.wait_ge(ropeT_out, NROPE)
            for c in range(RC):
                if c == 2:
                    pe.wait_ge(gate_act, 2 * RC)
                proj_T(XG, c, XG_BANK[c], xg_done)
                if c == 0:
                    gates(RC - 1)

            def scores_mm(i):
                t, hp = PAIRS[i]
                if i == 0:
                    pe.wait_ge(xr_out, RC)
                if i == 1:
                    pe.wait_ge(xg_mult, 2)
                if i >= 2:
                    pe.wait_ge(nmax_ready, i - 1)
                for hh in range(2):
                    r = slice(64 * hh, 64 * hh + 64)
                    last = pe.matmul(ps[2 * (i % 2) + hh][:, 0:P * (t + 1)], qT[r, hp, t * P:(t + 1) * P],
                                     kT[r, hp, 0:P * (t + 1)], start=True, stop=True)
                last.then_inc(qk_done, 1)

            def prob_T(i):
                t, hp = PAIRS[i]
                pe.wait_ge(prob_ready, i + 1)
                if i == 0:
                    pe.wait_ge(xg_mult, RC)
                if i >= 1:
                    pe.wait_ge(probT_even, i)
                    pe.wait_ge(probT_odd, i)
                for hh in range(2):
                    for kc in range(t + 1):
                        last = pe.transpose(ps[4 + hh][:, kc * P:(kc + 1) * P], prob[:, i % 3, hh, kc * P:(kc + 1) * P], ident[:])
                last.then_inc(probT_done, 1)

            def values_mm(i):
                t, hp = PAIRS[i]
                pe.wait_ge(probT_even, i + 1)
                pe.wait_ge(probT_odd, i + 1)
                if hp == 0 and t <= 1:
                    pe.wait_ge(ada_ready, 2 + t)
                if hp == 0 and t >= 2:
                    pe.wait_ge(attn_out, t - 1)
                for kc in range(t + 1):
                    for hh in range(2):
                        h = 2 * hp + hh
                        last = pe.matmul(ps[7 - t % 2][64 * hh:64 * hh + 64, hp * P:(hp + 1) * P], v_sb[:, kc, h * HD:(h + 1) * HD],
                                         probT[:, hh, kc * P:(kc + 1) * P], start=(kc == 0), stop=(kc == t))
                last.then_inc(pv_done, 1)

            def tokens_T(t):
                if t >= 1:
                    pe.wait_ge(h2T_out, t)
                if t >= 2:
                    pe.wait_ge(slots_ready, t - 1)
                for m in range(2):
                    pe.wait_ge(h2_ready, 2 * t + m + 1)
                    for k in range(4 * m, 4 * m + 4):
                        last = pe.transpose(ps[4 + m][:, (k % 4) * P:(k % 4 + 1) * P], h2[:, t, k * P:(k + 1) * P], ident[:])
                    last.then_inc(h2T_done, 1)

            def router(t):
                pe.wait_ge(h2T_out, t + 1)
                if t == 0:
                    pe.wait_ge(router_loaded, 64)
                    pe.wait_ge(attn_out, NT)
                elif LOGIT_BANK[t] == LOGIT_BANK[t - 1]:
                    pe.wait_ge(chosen_ready, t)
                else:
                    pe.wait_ge(x2_ready, NT - 1)
                for k in range(KD):
                    if t == NT - 1 and k == 4:
                        positions(NT - 2)
                    last = pe.matmul(ps[LOGIT_BANK[t]][:, 0:NL], h2T[:, t % 2, k, :], w_router[:, k, :],
                                     start=(k == 0), stop=(k == KD - 1))
                last.then_inc(logit_mm, 1)

            def positions(t):
                pe.wait_ge(chosen_ready, t + 1)
                pe.wait_ge(h2T_out, t + 2 if t < NT - 1 else NT)
                if t >= 1:
                    pe.wait_ge(slots_ready, t)
                for s in range(t + 1):
                    last = pe.matmul(ps[4][:, 0:NE], before[:] if s == t else ones_b[:], chosen[:, s, :],
                                     start=(s == 0), stop=(s == t))
                last.then_inc(pos_mm, 1)

            def to_table(t):
                pe.wait_ge(slots_ready, t + 1)
                for k in range(2):
                    last = pe.matmul(ps[7][:, 0:NE], at_slot[:, k, :], token_of[:, k, :],
                                     start=(t == 0 and k == 0), stop=(t == NT - 1 and k == 1))
                last.then_inc(table_mm, 1)

            def mix_pass(t, n, m):
                left, right = ((mix_hi, wo_hi), (mix_lo, wo_hi), (mix_hi, wo_lo))[m]
                for k in range(KD):
                    last = pe.matmul(ps[2 * (t % 2) + n][:], left[:, k, t * P:(t + 1) * P], right[:, k, 512 * n:512 * (n + 1)],
                                     start=(m == 0 and k == 0), stop=(m == 2 and k == KD - 1))
                if m == 2:
                    last.then_inc(mix_done, 1)

            for i in range(len(PAIRS) + 3):
                if i < len(PAIRS):
                    scores_mm(i)
                    if i in (0, 1, 3, 4):
                        ada_later(NADA - 4 + (0, 1, 3, 4).index(i))
                else:
                    if i == len(PAIRS):
                        pe.wait_ge(hi_ready, W_HI + 1 + WO_PIECES)
                        pe.wait_ge(lo_ready, W_LO + 1 + WO_PIECES)
                        pe.wait_ge(attn_out, 1)
                        pe.wait_ge(nmax_ready, len(PAIRS) - 1)
                    for part in (2 * (i - len(PAIRS)), 2 * (i - len(PAIRS)) + 1):
                        mix_pass(0, part // 3, part % 3)
                if 2 <= i < len(PAIRS) + 2:
                    prob_T(i - 2)
                if i >= 3:
                    values_mm(i - 3)

            pe.wait_ge(nmax_ready, len(PAIRS))
            for t in range(1, NT):
                pe.wait_ge(attn_out, t + 1)
                if t >= 2:
                    pe.wait_ge(x2_ready, t - 1)
                for part in range(6):
                    if part == (5 if t == 1 else 4):
                        tokens_T(t - 1)
                    if part == 5 and t >= 2:
                        positions(t - 2)
                    mix_pass(t, part // 3, part % 3)
                if t >= 2:
                    to_table(t - 2)
                router(t - 1)
            tokens_T(NT - 1)
            router(NT - 1)
            to_table(NT - 2)
            positions(NT - 1)
            to_table(NT - 1)
            for t in range(NT):
                last = pe.matmul(ps[6][:, 0:NE], ones_b[:], chosen[:, t, :], start=(t == 0), stop=(t == NT - 1))
            last.then_inc(pos_mm, 1)

            def rows_T(e, j, turn):
                pe.wait_ge(gathered[j], turn * 16 + 16)
                if not (isinstance(e, int) and e < 2):
                    pe.wait_ge(xgT_out, e - 1)
                apart(pe)
                for k in range(KD):
                    last = pe.transpose(ps[j % 2][:, k * CAP:(k + 1) * CAP], x_gath[:, j, k:D:KD], ident[0:CAP, 0:CAP])
                last.then_inc(xgT_done, 1)

            def gate_up(e, j, weights):
                (w_g, w_u, _), loaded, count = weights[:3]
                pe.wait_ge(loaded, count)
                pe.wait_ge(xgT_out, e + 1)
                if not (isinstance(e, int) and e < 2):
                    pe.wait_ge(hid_ready, e - 1)
                for k in range(KD):
                    for m in range(2):
                        last = pe.matmul(ps[2 + j % 2][CAP * m:CAP * m + CAP, 0:FE], xgT[:, j % 2, k, :],
                                         (w_g, w_u)[m][:, k * FE:(k + 1) * FE], start=(k == 0), stop=(k == KD - 1))
                last.then_inc(gu_done, 1)

            def hidden_T(e, j):
                pe.wait_ge(hid_ready, e + 1)
                apart(pe)
                for k in range(FC):
                    last = pe.transpose(ps[4 + j % 2][:, k * CAP:(k + 1) * CAP], hid[:, j % 2, k:FE:FC], ident[0:CAP, 0:CAP])
                last.then_inc(hidT_done, 1)

            def down(e, j, weights):
                w_d = weights[0][2]
                pe.wait_ge(weights[3], weights[4])
                pe.wait_ge(hidT_out, e + 1)
                if not (isinstance(e, int) and e < 2):
                    pe.wait_ge(y_ready, e - 1)
                for k in range(FC):
                    for n in range(2):
                        last = pe.matmul(ps[6 + j % 2][CAP * n:CAP * n + CAP, :], hidT[:, j % 2, k, :],
                                         w_d[:, k * D + 512 * n:k * D + 512 * (n + 1)],
                                         start=(k == 0), stop=(k == FC - 1))
                last.then_inc(down_done, 1)

            def turn_of(i, n):
                return i + n // RING

            def step(i, n, late=False):
                e, j = i * RING + n, n % RING
                gate_up(e, j, weights_of(i, n, late))
                hidden_T(i * RING + (n - 1), (n - 1) % RING)
                rows_T(i * RING + (n + 1), (n + 1) % RING, turn_of(i, n + 1))
                down(i * RING + (n - 1), (n - 1) % RING, weights_of(i, n - 1, late))

            rows_T(0, 0, 0)
            gate_up(0, 0, weights_of(0, 0))
            rows_T(1, 1, 0)
            step(0, 1)
            step(0, 2)
            with pe.Fori(0, SPARE // RING - 1) as i:
                for n in range(3, 3 + RING):
                    step(i, n)
            for n in range(3, 3 + RING):
                step(SPARE // RING - 1, n)
            with pe.Fori(SPARE // RING, NE // RING - 1) as i:
                for n in range(3, 3 + RING):
                    step(i, n, late=True)
            last_turn = NE // RING - 1
            gate_up(NE - 1, RING - 1, weights_of(last_turn, RING - 1))
            hidden_T(NE - 2, RING - 2)
            down(NE - 2, RING - 2, weights_of(last_turn, RING - 2))
            hidden_T(NE - 1, RING - 1)
            down(NE - 1, RING - 1, weights_of(last_turn, RING - 1))

            def more(r, e, m):
                pe.wait_ge(more_loaded, m * 80)
                pe.wait_ge(more_gathered, m * 16)
                apart(pe)
                for k in range(KD):
                    last = pe.transpose(ps[0][:, k * CAP:(k + 1) * CAP], x_gath[:, 0, k:D:KD], ident[0:CAP, 0:CAP])
                last.then_inc(more_xT, 1)
                pe.wait_ge(more_xT_out, m)
                for k in range(KD):
                    for g in range(2):
                        last = pe.matmul(ps[2][CAP * g:CAP * g + CAP, 0:FE], xgT[:, 0, k, :],
                                         expert_w[:, 0, g, k * FE:(k + 1) * FE], start=(k == 0), stop=(k == KD - 1))
                last.then_inc(more_gu, 1)
                pe.wait_ge(more_hid, m)
                apart(pe)
                for k in range(FC):
                    last = pe.transpose(ps[4][:, k * CAP:(k + 1) * CAP], hid[:, 0, k:FE:FC], ident[0:CAP, 0:CAP])
                last.then_inc(more_hidT, 1)
                pe.wait_ge(more_hidT_out, m)
                for k in range(FC):
                    for n in range(2):
                        last = pe.matmul(ps[6][CAP * n:CAP * n + CAP, :], hidT[:, 0, k, :],
                                         expert_w[:, 0, 2, k * D + 512 * n:k * D + 512 * (n + 1)],
                                         start=(k == 0), stop=(k == FC - 1))
                last.then_inc(more_down, 1)

            more_rounds(pe, more)

        @block.scalar
        def _(act):
            n = [0]

            def link(ins):
                n[0] += 1
                ins.then_inc(achain, 1)
                act.wait_ge(achain, n[0])

            act.dma_start(c_col, a["c"][0].rearrange("(p k) -> p k", k=KD)).then_inc(c_loaded, 16)
            act.wait_ge(c_loaded, 16)
            act.activation(c_col, c_col, ACT.Silu).then_inc(silu_c, 1)
            for t in range(NT):
                act.wait_ge(tile_loaded[t], 16)
                if t >= 1:
                    act.wait_ge(sq_done, t)
                act.activation(junk, x_in_sb[:, t, :], ACT.Square, accum_out=ssq[:, t:t + 1]).then_inc(sq_done, 1)
            act.wait_ge(var_ready, 1)
            act.activation(rstd, rstd, ACT.Sqrt).then_inc(root_ready, 1)
            for k in range(0, KD, 2):
                act.wait_ge(xT_done, k + 1)
                act.activation(hT[:, k, :], ps[k][:], ACT.Copy).then_inc(xT_even, 1)
            for i in range(3):
                split_hi(act, QI, i)
            act.wait_ge(h_ready, KD)
            act.activation(h_hi[:, :, 0:P], hT[:, :, 0:P], ACT.Copy).then_inc(h_hi_ready, 1)
            for i in range(3, KD):
                split_hi(act, QI, i)
            act.wait_ge(h_ready, 2 * KD)
            act.activation(h_hi[:, :, P:S], hT[:, :, P:S], ACT.Copy).then_inc(h_hi_ready, 1)
            act.wait_ge(kiwi_loaded, 16)
            act.activation(kiwi_both[:, :, 0, :], w_kiwi, ACT.Copy).then_inc(kiwi_hi_ready, 1)
            act.wait_ge(par_sb, 2)
            act.activation(spt[:, 0:RC], spt[:, 0:RC], ACT.Exp, scale=-1.0).then_inc(sp_exp, 1)

            def unit_out(u):
                dst = {QI: qiT, Q: qT, K: kT}[UNITS[u][0]]
                t = UNITS[u][1]
                act.wait_ge(ropeT_done, u + 1)
                act.activation(dst[:, :, t * P:(t + 1) * P], ps[2 + u % 2][:].rearrange("p (k s) -> p k s", k=4),
                               ACT.Copy).then_inc(ropeT_out, 1)

            def relus(t):
                for h in range(IH):
                    m = (t - 1) * IH + h
                    act.wait_ge(dots_done, m + 1)
                    if m >= 2:
                        act.wait_ge(score_acc, m - 1)
                    act.activation(relu_b[:, m % 2, 0:P * (t + 1)], ps[6 + h % 2][:, 0:P * (t + 1)], ACT.Relu).then_inc(relu_done, 1)

            for u, (w, t) in enumerate(UNITS):
                if u in DOT_UNITS:
                    relus(u - DOT_UNITS[0] + 1)
                if w == V:
                    act.wait_ge(proj_done, u + 1)
                    act.wait_ge(table_clear, 16)
                    act.activation(v_sb[:, t, :], ps[u % 2][:], ACT.Copy).then_inc(v_out, 1)
                    if u == NROPE:
                        unit_out(u - 1)
                if 1 <= u < NROPE:
                    unit_out(u - 1)
                if u == NT:
                    act.wait_ge(kiT_done, NT)
                    act.activation(kiT, ps[5][:], ACT.Copy).then_inc(kiT_out, 1)
                if t in (1, 2):
                    split_hi(act, w + 1, t - 1)
            def gate_acts(c):
                act.wait_ge(gate_mm, c + 1)
                if c >= 1:
                    act.wait_ge(rec_done, c)
                act.activation(tanh_r, ps[4][:], ACT.Tanh, bias=par[:, 20 + c:21 + c], scale=0.5).then_inc(achain, 1)
                act.activation(tanh_i, ps[5][:], ACT.Tanh, bias=par[:, 24 + c:25 + c], scale=0.5).then_inc(achain, 1)
                n[0] += 2
                act.wait_ge(achain, n[0])
                link(act.activation(a_rec[:, c, :], tanh_r, ACT.Exp, bias=sp4n[:, c:c + 1], scale=sp4n[:, c:c + 1]))
                act.activation(xr[:, c, :], a_rec[:, c, :], ACT.Square).then_inc(gate_act, 1)
                act.activation(tanh_r, tanh_r, ACT.Tanh, bias=sp4[:, c:c + 1], scale=sp4[:, c:c + 1]).then_inc(gate_act, 1)

            act.wait_ge(par_sb, 3)
            for c in range(RC):
                act.wait_ge(xr_done, c + 1)
                act.activation(xr[:, c, :], ps[c % 2][:], ACT.Copy).then_inc(xr_out, 1)
                if c in (1, 2):
                    split_hi(act, XG, c - 1)
                if c >= 1:
                    gate_acts(c - 1)
            gate_acts(RC - 1)
            act.wait_ge(rec_done, RC)
            m_all = xr.rearrange("p c s -> p (c s)")
            act.activation(m_all, m_all, ACT.Sqrt, scale=0.25).then_inc(rec_root, 1)

            def gelu_sq(c):
                act.wait_ge(xg_done, c + 1)
                if c >= 2:
                    act.wait_ge(xg_mult, c - 1)
                act.activation(gel[:, c % 2, :], ps[XG_BANK[c]][:], ACT.Square).then_inc(xg_sq, 1)

            gelu_sq(0)
            for c in range(RC):
                if c + 1 < RC:
                    gelu_sq(c + 1)
                act.wait_ge(xg_cubic, c + 1)
                act.activation(gel[:, c % 2, :], gel[:, c % 2, :], ACT.Tanh, scale=GELU_SCALE * GELU_CUBIC).then_inc(xg_tanh, 1)

            def exps(i):
                t, hp = PAIRS[i]
                act.wait_ge(nmax_ready, i + 1)
                if i >= 2:
                    act.wait_ge(prob_ready, i - 1)
                for hh in range(2):
                    p = prob[:, i % 3, hh, 0:P * (t + 1)]
                    q = 2 * (i % 2) + hh
                    act.activation(p, p, ACT.Exp, bias=nmax[:, q:q + 1], scale=HD ** -0.5, accum_out=rsum[:, q:q + 1]).then_inc(exp_done, 1)

            def probT_copy(i):
                t, hp = PAIRS[i]
                act.wait_ge(probT_done, i + 1)
                if i >= 1:
                    act.wait_ge(pv_done, i)
                act.activation(probT[:, 0, 0:P * (t + 1)], ps[4][:, 0:P * (t + 1)], ACT.Copy).then_inc(probT_even, 1)

            def attn_halves(t):
                out, hi, _ = attn_tile(t)
                act.wait_ge(pv_done, 4 * (t + 1))
                act.activation(hi, out, ACT.Copy).then_inc(attn_hi, 1)

            for i in range(len(PAIRS) + 2):
                if i < len(PAIRS):
                    exps(i)
                if i >= 2:
                    probT_copy(i - 2)
                if i >= 3 and (i - 3) % 4 == 3:
                    attn_halves((i - 3) // 4)
                if i == 2:
                    act.wait_ge(xg_mult, RC)
                    act.activation(mix_hi[:, 4:8, :], mixT[:, 4:8, :], ACT.Copy).then_inc(hi_ready, 1)
                if WO_STEP <= i < WO_STEP + WO_PIECES:
                    if i == WO_STEP:
                        act.wait_ge(wo_loaded, 16)
                    k = wo_piece(i - WO_STEP)
                    act.activation(wo_hi[:, k, :], wo_sb[:, k, :], ACT.Copy).then_inc(hi_ready, 1)
            attn_halves(NT - 1)

            def mix_norm(t):
                for m in range(2):
                    act.wait_ge(mix_done, 2 * t + m + 1)
                    if t >= 1 and m == 0:
                        act.wait_ge(mix_var, t)
                    act.activation(h2[:, t, 512 * m:512 * (m + 1)], ps[2 * (t % 2) + m][:], ACT.Square,
                                   accum_out=pssq[:, m:m + 1]).then_inc(mix_sq, 1)
                act.wait_ge(mix_var, t + 1)
                act.activation(rstd[:, t:t + 1], ssq[:, t:t + 1], ACT.Sqrt).then_inc(mix_root, 1)

            def x2_norm(t):
                act.wait_ge(x2_ready, t + 1)
                act.activation(h2[:, t, :], x2[:, t, :], ACT.Square, accum_out=ssq[:, t:t + 1]).then_inc(x2_sq, 1)
                act.wait_ge(x2_var, t + 1)
                act.activation(rstd[:, t:t + 1], ssq[:, t:t + 1], ACT.Sqrt).then_inc(x2_root, 1)

            def h2T_copy(t):
                for m in range(2):
                    act.wait_ge(h2T_done, 2 * t + m + 1)
                    last = act.activation(h2T[:, t % 2, 4 * m:4 * m + 4, :].rearrange("p k s -> p (k s)"), ps[4 + m][:], ACT.Copy)
                last.then_inc(h2T_out, 1)

            for t in range(NT):
                mix_norm(t)
                x2_norm(t)
                h2T_copy(t)
            for t in range(NT):
                act.wait_ge(logit_ready, t + 1)
                act.activation(logit[:, t, 0:NG], logit[:, t, 0:NG], ACT.Exp, accum_out=ssq[:, t:t + 1]).then_inc(route_exp, 1)
                act.activation(cw[:, 1, t:t + 1], cw[:, 1, t:t + 1], ACT.Exp).then_inc(route_exp, 1)

            def xgT_copy(e, j):
                act.wait_ge(xgT_done, e + 1)
                if not (isinstance(e, int) and e < 2):
                    act.wait_ge(gu_done, e - 1)
                act.activation(xgT[:, j % 2].rearrange("p k s -> p (k s)"), ps[j % 2][:], ACT.Copy).then_inc(xgT_out, 1)

            def silu(e, j):
                act.wait_ge(gu_done, e + 1)
                if not (isinstance(e, int) and e < 2):
                    act.wait_ge(hid_ready, e - 1)
                act.activation(silu_g[:, j % 2, :], ps[2 + j % 2][0:CAP, 0:FE], ACT.Silu).then_inc(silu_done, 1)

            xgT_copy(0, 0)
            xgT_copy(1, 1)
            silu(0, 0)
            silu(1, 1)
            with act.Fori(0, NE // RING - 1) as i:
                for m in range(2, 2 + RING):
                    xgT_copy(i * RING + m, m % RING)
                    silu(i * RING + m, m % RING)
            for m in range(NE - 2, NE):
                xgT_copy(m, m % RING)
                silu(m, m % RING)

            def more(r, e, m):
                act.wait_ge(more_xT, m)
                act.activation(xgT[:, 0].rearrange("p k s -> p (k s)"), ps[0][:], ACT.Copy).then_inc(more_xT_out, 1)
                act.wait_ge(more_gu, m)
                act.activation(silu_g[:, 0, :], ps[2][0:CAP, 0:FE], ACT.Silu).then_inc(more_silu, 1)

            more_rounds(act, more)

            def scale_first(t):
                act.wait_ge(tile_loaded[t], 48)
                act.activation(y_back[:, 0, t, :], y_back[:, 0, t, :], ACT.Copy, scale=cw[:, 0, t:t + 1]).then_inc(fin_scaled, 1)

            act.activation(rstd, ssq, ACT.Sqrt).then_inc(achain, 1)
            n[0] += 1
            scale_first(0)
            for t in range(NT):
                if t + 1 < NT:
                    scale_first(t + 1)
                act.wait_ge(fin_sum, t + 1)
                act.activation(h2[:, t, :], y_back[:, 0, t, :], ACT.Square, accum_out=ssq[:, t:t + 1]).then_inc(fin_sq, 1)
                act.wait_ge(fin_var, t + 1)
                if t == 0:
                    act.wait_ge(achain, n[0])
                act.activation(rstd[:, t:t + 1], ssq[:, t:t + 1], ACT.Sqrt).then_inc(fin_root, 1)

        @block.vector
        def _(dve):
            n = [0]

            def link(ins):
                n[0] += 1
                ins.then_inc(chain, 1)
                dve.wait_ge(chain, n[0])

            def tick(ins):
                n[0] += 1
                ins.then_inc(chain, 1)

            def settle():
                dve.wait_ge(chain, n[0])

            tick(dve.memset(gain[0:64, 0, :], 1.0))
            tick(dve.memset(gain[64:P, 1, :], 1.0))
            tick(dve.memset(half[0:CAP, :], 0.0))
            tick(dve.memset(half[CAP:P, :], 1.0))
            tick(dve.memset(score[0], 0.0))
            settle()
            tick(dve.memset(score[0][0:CHUNK, CHUNK:P], MASKED))
            dve.wait_ge(sq_done, NT)
            dve.tensor_scalar(rstd, ssq, 1.0 / D, EPS, ALU.mult, ALU.add).then_inc(var_ready, 1)
            dve.wait_ge(root_ready, 1)
            link(dve.reciprocal(rstd, rstd))
            for t in range(NT):
                dve.tensor_scalar(x_in_sb[:, t, :], x_in_sb[:, t, :], rstd[:, t:t + 1], None, ALU.mult).then_inc(xn_ready, 1)
            dve.wait_ge(silu_c, 1)
            dve.tensor_copy(c_rep, c_col.unsqueeze(2).broadcast_to([P, KD, 32])).then_inc(c_ready, 1)
            for k in range(1, KD, 2):
                dve.wait_ge(xT_done, k + 1)
                dve.tensor_copy(hT[:, k, :], ps[k][:]).then_inc(xT_odd, 1)
            dve.wait_ge(first_loaded, 16 * 6)
            link(dve.tensor_scalar(ada[64:P, 0, :], ada[64:P, 0, :], 1.0, None, ALU.add))

            def ada_rows(s, used, bank):
                dve.wait_ge(ada_used, used)
                link(dve.tensor_tensor(ada[:, s, :], ps[bank][:], ada[:, s, :], ALU.add))
                dve.tensor_tensor(ada[:, s, :], ada[:, s, :], gain[:, s, :], ALU.mult).then_inc(ada_ready, 1)

            ada_rows(0, 4, 0)
            dve.wait_ge(mod1_T, 1)
            link(dve.tensor_copy(mod1.rearrange("p (r j) -> p r j", j=4),
                                 ps[1][:].rearrange("p (j r q) -> p r j q", j=4, q=32)[:, :, :, 0]))
            dve.wait_ge(xT_even, KD // 2)
            dve.wait_ge(xT_odd, KD // 2)
            parts = (slice(0, P), slice(P, S))
            for part in parts:
                for k in range(KD):
                    dve.tensor_scalar(hT[:, k, part], hT[:, k, part], mod1[:, KD + k:KD + k + 1], mod1[:, k:k + 1],
                                      ALU.mult, ALU.add).then_inc(h_ready, 1)
            for m, part in enumerate(parts):
                dve.wait_ge(h_hi_ready, m + 1)
                dve.wait_ge(h_ready, KD * (m + 1))
                dve.tensor_tensor(h_lo[:, :, part], hT[:, :, part], h_hi[:, :, part], ALU.subtract).then_inc(h_lo_ready, 1)
                if m == 0:
                    for i in range(1, KD, 2):
                        split_lo(dve, QI, i, lo_odd)

            def rope(u):
                t = UNITS[u][1]
                dve.wait_ge(proj_done, u + 1)
                if u >= 1:
                    dve.wait_ge(rope_ready, u)
                if u >= 2:
                    dve.wait_ge(ropeT_done, u - 1)
                x = ps[u % 2][:].rearrange("p (h s f) -> p h s f", s=2, f=32)
                o = roped[:, u % 2, :].rearrange("p (h s f) -> p h s f", s=2, f=32)
                o3 = roped[:, u % 2, :].rearrange("p (h f) -> p h f", f=32)
                x3 = ps[u % 2][:].rearrange("p (h f) -> p h f", f=32)
                tmp = rope_tmp.rearrange("p (h s f) -> p h s f", s=2, f=32)
                tick(dve.tensor_tensor(o3, x3, rope_cos[:, t, :].unsqueeze(1).broadcast_to([P, 16, 32]), ALU.mult))
                link(dve.tensor_tensor(tmp, x[:, :, ::-1, :], rope_sin[:, t].unsqueeze(1).broadcast_to([P, 8, 2, 32]), ALU.mult))
                dve.tensor_tensor(roped[:, u % 2, :], roped[:, u % 2, :], rope_tmp, ALU.add).then_inc(rope_ready, 1)

            def rope_ki(t):
                dve.wait_ge(ki_done, t + 1)
                if t >= 1:
                    dve.wait_ge(ki_ready, t)
                if t >= 2:
                    dve.wait_ge(kiT_done, t - 1)
                both = ps[4 + 2 * (t % 2)][:, 0:2 * (ID + IH)].rearrange("p (a n) -> p n a", a=2)
                link(dve.tensor_reduce(ki_sum, both, AX.X, ALU.add))
                src = ki_sum[:, 0:ID]
                row = ki_rows[:, t % 2, :].rearrange("p (a n) -> p a n", a=2)
                tick(dve.tensor_tensor(row[:, 0, :].rearrange("p (s f) -> p s f", s=2), src.rearrange("p (s f) -> p s f", s=2),
                                       rope_cos[:, t, :].unsqueeze(1).broadcast_to([P, 2, 32]), ALU.mult))
                tick(dve.tensor_tensor(ki_tmp.rearrange("p (s f) -> p s f", s=2), src.rearrange("p (s f) -> p s f", s=2)[:, ::-1, :],
                                       rope_sin[:, t], ALU.mult))
                tick(dve.tensor_scalar(w_idx[:, t, :], ki_sum[:, ID:ID + IH], IH ** -0.5 * ID ** -0.5, None, ALU.mult))
                settle()
                link(dve.tensor_tensor(row[:, 0, :], row[:, 0, :], ki_tmp, ALU.add))
                dve.tensor_copy(row[:, 1, :], row[:, 0, :]).then_inc(ki_ready, 1)

            def index_sum(t):
                for h in range(IH):
                    m = (t - 1) * IH + h
                    dve.wait_ge(relu_done, m + 1)
                    r = relu_b[:, m % 2, 0:P * (t + 1)]
                    if h == 0:
                        dve.tensor_scalar(score[t], r, w_idx[:, t, 0:1], None, ALU.mult).then_inc(score_acc, 1)
                    else:
                        dve.wait_ge(score_acc, m)
                        dve.scalar_tensor_tensor(score[t], r, w_idx[:, t, h:h + 1], score[t], ALU.mult, ALU.add).then_inc(score_acc, 1)
                dve.wait_ge(score_acc, t * IH)
                tick(dve.memset(score[t][0:CHUNK, P * t + CHUNK:P * (t + 1)], NOT_ADMISSIBLE))

            def topk_round():
                settle()
                for t in range(1, NT):
                    tick(dve.max(top8[:, t - 1, :], score[t]))
                for t in range(1, NT):
                    dve.wait_ge(chain, n[0] - (NT - 1 - t) - (t - 1))
                    tick(dve.match_replace(score[t], top8[:, t - 1, :], score[t], TAKEN))

            def channel_params():
                dve.wait_ge(par_T, 1)
                dve.tensor_copy(par, ps[7][:, 0:32]).then_inc(par_sb, 1)
                dve.wait_ge(par_sb, 1)
                lam = par[:, 28:32]
                z, q = spt[:, 0:RC], spt[:, RC:2 * RC]
                tick(dve.tensor_scalar(par[:, 20:28], par[:, 20:28], 0.5, None, ALU.mult))
                link(dve.tensor_scalar(q, lam, -1.0, None, ALU.mult))
                dve.tensor_tensor(z, lam, q, ALU.max).then_inc(par_sb, 1)
                dve.wait_ge(sp_exp, 1)
                link(dve.tensor_scalar(q, z, 2.0, None, ALU.add))
                link(dve.reciprocal(q, q))
                link(dve.tensor_tensor(z, z, q, ALU.mult))
                link(dve.tensor_tensor(q, z, z, ALU.mult))
                TERMS = 8
                link(dve.tensor_scalar(sp4, q, 1.0 / (2 * TERMS + 1), 1.0 / (2 * TERMS - 1), ALU.mult, ALU.add))
                for m in range(TERMS - 1, 0, -1):
                    link(dve.tensor_tensor(sp4, sp4, q, ALU.mult))
                    link(dve.tensor_scalar(sp4, sp4, 1.0 / (2 * m - 1), None, ALU.add))
                link(dve.tensor_tensor(sp4, sp4, z, ALU.mult))
                link(dve.tensor_scalar(q, lam, -1.0, 0.0, ALU.mult, ALU.max))
                link(dve.scalar_tensor_tensor(sp4, sp4, 2.0, q, ALU.mult, ALU.add))
                link(dve.tensor_scalar(sp4, sp4, 4.0, None, ALU.mult))
                dve.tensor_scalar(sp4n, sp4, -1.0, None, ALU.mult).then_inc(par_sb, 1)

            dve.wait_ge(rope_loaded, 32)
            for u in range(NROPE):
                if u in DOT_UNITS:
                    index_sum(u - DOT_UNITS[0] + 1)
                rope(u)
                if u < NT:
                    rope_ki(u)
                if u == 0:
                    channel_params()
                if u > DOT_UNITS[-1]:
                    topk_round()
            for _ in range(ROUNDS - 6):
                topk_round()

            dve.wait_ge(ada_params_loaded, 16 * 14)
            link(dve.tensor_scalar(ada[0:64, 2, :], ada[0:64, 2, :], 1.0, None, ALU.add))
            ada_rows(1, 4 + KD, 7)

            def convolve(c):
                dve.wait_ge(xr_out, c + 1)
                if c >= 2:
                    dve.wait_ge(gate_mm, c - 1)
                    settle()
                o = conv[:, c % 2, :]
                tap = lambda j: par[:, RC * j + c:RC * j + c + 1]
                link(dve.tensor_scalar(o, xr[:, c, :], tap(NTAPS - 1), par[:, 16 + c:17 + c], ALU.mult, ALU.add))
                for back in range(1, NTAPS):
                    ins = dve.scalar_tensor_tensor(o[:, back:], xr[:, c, 0:S - back], tap(NTAPS - 1 - back), o[:, back:], ALU.mult, ALU.add)
                    if back < NTAPS - 1:
                        link(ins)
                    else:
                        ins.then_inc(conv_ready, 1)

            def recur_in(c):
                dve.wait_ge(conv_ready, c + 1)
                dve.wait_ge(gate_act, 2 * c + 2)
                tick(dve.scalar_tensor_tensor(mixT[:, 4 + c, :], tanh_i, 1.0, conv[:, c % 2, :], ALU.add, ALU.mult))
                dve.scalar_tensor_tensor(xr[:, c, :], xr[:, c, :], 1.0, tanh_r, ALU.add, ALU.mult).then_inc(rec_done, 1)

            for c in range(RC):
                convolve(c)
                if c < 3:
                    topk_round()
                if c >= 1:
                    recur_in(c - 1)
            settle()
            for t in range(1, NT):
                dve.tensor_scalar(score[t], score[t], BETWEEN, MASKED, ALU.is_gt, ALU.mult).then_inc(mask_ready, 1)
            recur_in(RC - 1)
            dve.wait_ge(rec_root, 1)
            settle()
            rnn = mixT[:, 4:8, :]
            dve.tensor_tensor(rnn, rnn, xr, ALU.mult).then_inc(rec_b, 1)
            dve.wait_ge(rec_b, 1)
            for c in range(RC):
                tick(dve.tensor_tensor_scan(rnn[:, c, :], a_rec[:, c, :], rnn[:, c, :], 0.0, ALU.mult, ALU.add))

            def gelu_cubic(c):
                g = gel[:, c % 2, :]
                dve.wait_ge(xg_sq, c + 1)
                dve.scalar_tensor_tensor(g, g, 1.0 / GELU_CUBIC, ps[XG_BANK[c]][:], ALU.add, ALU.mult).then_inc(xg_cubic, 1)

            def masked_max(i):
                t, hp = PAIRS[i]
                dve.wait_ge(qk_done, i + 1)
                if i >= 3:
                    dve.wait_ge(probT_done, i - 2)
                if i >= 2:
                    dve.wait_ge(exp_done, 2 * (i - 1))
                if i == 0:
                    settle()
                for hh in range(2):
                    q = 2 * (i % 2) + hh
                    tick(dve.tensor_tensor_reduce(prob[:, i % 3, hh, 0:P * (t + 1)], ps[2 * (i % 2) + hh][:, 0:P * (t + 1)], score[t],
                                                  1.0, TAKEN, ALU.add, ALU.max, rmax[:, q:q + 1]))
                settle()
                q = 2 * (i % 2)
                dve.tensor_scalar(nmax[:, q:q + 2], rmax[:, q:q + 2], -HD ** -0.5, None, ALU.mult).then_inc(nmax_ready, 1)

            gelu_cubic(0)
            for c in range(RC):
                if c + 1 < RC:
                    gelu_cubic(c + 1)
                g = gel[:, c % 2, :]
                if c == RC - 1:
                    dve.wait_ge(mask_ready, NT - 1)
                    masked_max(0)
                dve.wait_ge(xg_tanh, c + 1)
                link(dve.scalar_tensor_tensor(g, g, 1.0, ps[XG_BANK[c]][:], ALU.add, ALU.mult))
                dve.scalar_tensor_tensor(rnn[:, c, :], g, 0.5, rnn[:, c, :], ALU.mult, ALU.mult).then_inc(xg_mult, 1)

            def normalise(i):
                t, hp = PAIRS[i]
                q = 2 * (i % 2)
                dve.wait_ge(exp_done, 2 * i + 2)
                link(dve.reciprocal(rsum[:, q:q + 2], rsum[:, q:q + 2]))
                for hh in range(2):
                    p = prob[:, i % 3, hh, 0:P * (t + 1)]
                    last = dve.tensor_scalar(p, p, rsum[:, q + hh:q + hh + 1], None, ALU.mult)
                last.then_inc(prob_ready, 1)

            def probT_copy(i):
                t, hp = PAIRS[i]
                dve.wait_ge(probT_done, i + 1)
                if i >= 1:
                    dve.wait_ge(pv_done, i)
                dve.tensor_copy(probT[:, 1, 0:P * (t + 1)], ps[5][:, 0:P * (t + 1)]).then_inc(probT_odd, 1)

            def attn_low(t):
                out, hi, lo = attn_tile(t)
                dve.wait_ge(attn_hi, t + 1)
                dve.tensor_tensor(lo, out, hi, ALU.subtract).then_inc(attn_out, 1)

            for i in range(len(PAIRS) + 2):
                if 1 <= i < len(PAIRS):
                    masked_max(i)
                if 1 <= i <= len(PAIRS):
                    normalise(i - 1)
                if i >= 2:
                    probT_copy(i - 2)
                if i == 6:
                    ada_rows(2, 4 + NADA, 6)
                if i >= 7 and i % 4 == 3:
                    attn_low(i // 4 - 1)
            attn_low(NT - 1)

            def post_mix(t):
                one = slice(t, t + 1)
                dve.wait_ge(mix_sq, 2 * t + 2)
                link(dve.tensor_tensor(ssq[:, one], pssq[:, 0:1], pssq[:, 1:2], ALU.add))
                dve.tensor_scalar(ssq[:, one], ssq[:, one], 1.0 / D, EPS, ALU.mult, ALU.add).then_inc(mix_var, 1)
                dve.wait_ge(mix_root, t + 1)
                link(dve.reciprocal(rstd[:, one], rstd[:, one]))
                if t == 0:
                    dve.wait_ge(rows_loaded, 64)
                for m in range(2):
                    w = slice(512 * m, 512 * (m + 1))
                    tick(dve.scalar_tensor_tensor(h2[:, t, w], ps[2 * (t % 2) + m][:], rstd[:, one], mod_rows[:, GATE1, w], ALU.mult, ALU.mult))
                settle()
                dve.wait_ge(x_again, 16 * NT)
                dve.tensor_tensor(x2[:, t, :], x2[:, t, :], h2[:, t, :], ALU.add).then_inc(x2_ready, 1)
                dve.wait_ge(x2_sq, t + 1)
                dve.tensor_scalar(ssq[:, one], ssq[:, one], 1.0 / D, EPS, ALU.mult, ALU.add).then_inc(x2_var, 1)
                dve.wait_ge(x2_root, t + 1)
                link(dve.reciprocal(rstd[:, one], rstd[:, one]))
                for m in range(2):
                    w = slice(512 * m, 512 * (m + 1))
                    link(dve.scalar_tensor_tensor(h2[:, t, w], x2[:, t, w], rstd[:, one], mod_rows[:, SCALE2, w], ALU.mult, ALU.mult))
                    dve.tensor_tensor(h2[:, t, w], h2[:, t, w], mod_rows[:, SHIFT2, w], ALU.add).then_inc(h2_ready, 1)

            def route(t):
                dve.wait_ge(logit_mm, t + 1)
                lg = logit[:, t, :]
                link(dve.tensor_tensor(lg, ps[LOGIT_BANK[t]][:, 0:NL], b_router, ALU.add))
                link(dve.tensor_copy(group8[:, 0:NG], lg[:, 0:NG]))
                link(dve.max(top_e[:, t, :], group8))
                tick(dve.max_index(gtop_i, top_e[:, t, :], group8))
                tick(dve.tensor_scalar(lg[:, 0:NG], lg[:, 0:NG], top_e[:, t, 0:1], None, ALU.subtract))
                settle()
                link(dve.tensor_copy(gi_f, gtop_i[:, 0:1]))
                link(dve.tensor_scalar(in_group[:, t, :], iota_e[:, 0:NG], gi_f, None, ALU.is_equal))
                link(dve.tensor_scalar(in_group[:, t, :], in_group[:, t, :], -1.0, -MASKED, ALU.add, ALU.mult))
                link(dve.tensor_tensor(lg[:, NG:NL].rearrange("p (g e) -> p g e", g=NG), lg[:, NG:NL].rearrange("p (g e) -> p g e", g=NG),
                                       in_group[:, t, :].unsqueeze(2).broadcast_to([P, NG, NE_G]), ALU.add))
                link(dve.max(top_e[:, t, :], lg[:, NG:NL]))
                tick(dve.max_index(top_i[:, t, :], top_e[:, t, :], lg[:, NG:NL]))
                dve.tensor_tensor(cw[:, 1, t:t + 1], top_e[:, t, 1:2], top_e[:, t, 0:1], ALU.subtract).then_inc(logit_ready, 1)
                settle()
                link(dve.tensor_copy(ei_f, top_i[:, t, 0:2]))
                for k in range(2):
                    tick(dve.tensor_scalar(choice[k][:, t, :], iota_e, ei_f[:, k:k + 1], None, ALU.is_equal))
                settle()
                dve.tensor_tensor(chosen[:, t, :], choice[0][:, t, :], choice[1][:, t, :], ALU.add).then_inc(chosen_ready, 1)
                if t >= 1:
                    dve.wait_ge(table_mm, t)
                for k in range(2):
                    tick(dve.tensor_scalar(token_of[:, k, :], choice[k][:, t, :], token_f[:, k * NT + t:k * NT + t + 1], None, ALU.mult))
                dve.wait_ge(pos_mm, t + 1)
                for k in range(2):
                    link(dve.tensor_tensor_reduce(route_tmp, ps[4][:, 0:NE], choice[k][:, t, :], 1.0, 0.0, ALU.mult, ALU.add, pos_f[:, k:k + 1]))
                for k in range(2):
                    tick(dve.tensor_scalar(at_slot[:, k, :], iota_slot, pos_f[:, k:k + 1], None, ALU.is_equal))
                settle()
                dve.scalar_tensor_tensor(slot_i[:, 2 * t:2 * t + 2], pos_f, float(NE), ei_f, ALU.mult, ALU.add).then_inc(slots_ready, 1)

            tick(dve.memset(group8, TAKEN))
            settle()
            dve.wait_ge(setup, 7)
            for t in range(NT):
                post_mix(t)
                if t >= 1:
                    if t == 1:
                        dve.wait_ge(router_loaded, 64)
                    route(t - 1)
            route(NT - 1)
            dve.wait_ge(table_mm, NT)
            link(dve.tensor_scalar(table_sb, ps[7][:, 0:NE], 2.0 * S, None, ALU.add))
            dve.tensor_single_scalar(gather_at, table_sb, 3 * S - 1, ALU.bitwise_and).then_inc(gath_idx, 1)
            dve.tensor_scalar(scatter_at, table_sb, 2.0, half, ALU.mult, ALU.add).then_inc(gath_idx, 1)
            dve.wait_ge(pos_mm, NT + 1)
            link(dve.tensor_reduce(count_f, ps[6][:, 0:NE], AX.X, ALU.max))
            dve.tensor_copy(most_tokens[:, 0:1], count_f).then_inc(count_ready, 1)
            dve.wait_ge(route_exp, 2 * NT)
            link(dve.tensor_scalar(cw[:, 0, :], cw[:, 1, :], 1.0, None, ALU.add))
            link(dve.tensor_tensor(cw[:, 0, :], cw[:, 0, :], ssq, ALU.mult))
            link(dve.reciprocal(cw[:, 0, :], cw[:, 0, :]))
            link(dve.tensor_tensor(cw[:, 1, :], cw[:, 1, :], cw[:, 0, :], ALU.mult))
            def hidden(e, j):
                dve.wait_ge(silu_done, e + 1)
                if not (isinstance(e, int) and e < 2):
                    dve.wait_ge(hidT_done, e - 1)
                dve.tensor_tensor(hid[:, j % 2, :], silu_g[:, j % 2, :], ps[2 + j % 2][CAP:P, 0:FE], ALU.mult).then_inc(hid_ready, 1)

            def hiddenT_copy(e, j):
                dve.wait_ge(hidT_done, e + 1)
                if not (isinstance(e, int) and e < 2):
                    dve.wait_ge(down_done, e - 1)
                dve.tensor_copy(hidT[:, j % 2].rearrange("p k s -> p (k s)"), ps[4 + j % 2][:, 0:FC * CAP]).then_inc(hidT_out, 1)

            def y_copy(e, j, turn):
                dve.wait_ge(down_done, e + 1)
                if not (isinstance(turn, int) and turn == 0):
                    dve.wait_ge(scattered[j], turn * 16)
                dve.tensor_copy(y_out[:, j, :], ps[6 + j % 2][:]).then_inc(y_ready, 1)

            def dve_step(i, m):
                hiddenT_copy(i * RING + (m - 1), (m - 1) % RING)
                hidden(i * RING + m, m % RING)
                y_copy(i * RING + (m - 1), (m - 1) % RING, i + (m - 1) // RING)

            hidden(0, 0)
            for m in range(1, RING + 1):
                dve_step(0, m)
            with dve.Fori(1, NE // RING - 1) as i:
                for m in range(1, RING + 1):
                    dve_step(i, m)
            for m in range(1, RING):
                dve_step(NE // RING - 1, m)
            hiddenT_copy(NE - 1, RING - 1)
            y_copy(NE - 1, RING - 1, NE // RING - 1)

            def more(r, e, m):
                dve.wait_ge(more_loaded, m * 80)
                dve.tensor_single_scalar(gather_at, table_sb, 3 * S - 1, ALU.bitwise_and).then_inc(more_table, 1)
                dve.tensor_scalar(scatter_at, table_sb, 2.0, half, ALU.mult, ALU.add).then_inc(more_table, 1)
                dve.wait_ge(more_silu, m)
                dve.tensor_tensor(hid[:, 0, :], silu_g[:, 0, :], ps[2][CAP:P, 0:FE], ALU.mult).then_inc(more_hid, 1)
                dve.wait_ge(more_hidT, m)
                dve.tensor_copy(hidT[:, 0].rearrange("p k s -> p (k s)"), ps[4][:, 0:FC * CAP]).then_inc(more_hidT_out, 1)
                dve.wait_ge(more_down, m)
                dve.tensor_copy(y_out[:, 0, :], ps[6][:]).then_inc(more_y, 1)

            more_rounds(dve, more)

            def fin_add(t):
                y0, y1 = y_back[:, 0, t, :], y_back[:, 1, t, :]
                dve.wait_ge(fin_scaled, t + 1)
                dve.wait_ge(tile_loaded[t], 48)
                dve.scalar_tensor_tensor(y0, y1, cw[:, 1, t:t + 1], y0, ALU.mult, ALU.add).then_inc(fin_sum, 1)

            def fin_norm(t):
                one = slice(t, t + 1)
                y0 = y_back[:, 0, t, :]
                dve.wait_ge(fin_sq, t + 1)
                dve.tensor_scalar(ssq[:, one], ssq[:, one], 1.0 / D, EPS, ALU.mult, ALU.add).then_inc(fin_var, 1)
                dve.wait_ge(fin_root, t + 1)
                link(dve.reciprocal(rstd[:, one], rstd[:, one]))
                gated = dve.scalar_tensor_tensor(y0, y0, rstd[:, one], mod_rows[:, GATE2, :], ALU.mult, ALU.mult)
                if t < NT - 1:
                    gated.then_inc(fin_gated, 1)
                else:
                    link(gated)
                    dve.tensor_tensor(y0, y0, x2[:, t, :], ALU.add).then_inc(fin_gated, 1)

            fin_add(0)
            for t in range(NT):
                if t + 1 < NT:
                    fin_add(t + 1)
                fin_norm(t)


_INS = ["x", "c", "w_ada", "b_ada", "g_pre_mix", "g_post_mix", "g_pre_ffn", "g_post_ffn", "w_in", "conv_w", "conv_b",
        "w_rg_a", "b_rg_a", "w_rg_x", "b_rg_x", "lru_lambda", "w_out", "w_router_group", "b_router_group",
        "w_router_expert", "b_router_expert", "w_gate", "w_up", "w_down"]


def kernel(**inputs):
    import numpy as _np
    import concourse.bacc as _bacc
    from concourse import mybir as _mybir
    from concourse.bass_utils import run_bass_kernel_spmd as _run

    nc = _bacc.Bacc("TRN2", target_bir_lowering=False, num_devices=1)
    arrays = {name: _np.ascontiguousarray(inputs[name]) for name in _INS}
    _, seq, d = arrays["x"].shape
    hd = d // 16
    inv = _np.float32(ROPE_THETA) ** (-_np.arange(0, hd, 2, dtype=_np.float32) / _np.float32(hd))
    ang = _np.arange(seq, dtype=_np.float32)[:, None] * inv.astype(_np.float32)[None, :]
    cos, sin = _np.cos(ang).astype(_np.float32), _np.sin(ang).astype(_np.float32)
    arrays["rope_cos"] = cos
    arrays["rope_sin"] = _np.ascontiguousarray(_np.stack([-sin, sin], axis=1))
    dram = {name: nc.dram_tensor(f"in_{name}_dram", v.shape, _mybir.dt.from_np(v.dtype), kind="ExternalInput").ap()
            for name, v in arrays.items()}
    dram["out"] = nc.dram_tensor("out_0_dram", (1, seq, d), _mybir.dt.float32, kind="ExternalOutput").ap()
    hybrid_block(nc, dram)
    r = _run(nc, [{f"in_{name}_dram": v for name, v in arrays.items()}], core_ids=[0])
    return r.results[0]["out_0_dram"]
```
